# Optimizing a Trainium2 kernel written in Bass

```python
import numpy as np
import jax, jax.numpy as jnp
from jax import lax

D_MODEL = 2048
BATCH = 1
SEQ = 256
DEPTH = 2

EPS = 1e-6
M_WIDTH = D_MODEL // 4
M_HEAD_DIM = 128
M_HEADS = M_WIDTH // M_HEAD_DIM
M_CHUNK = 128
M_CONV = 4
S_WIDTH = D_MODEL // 4
S_GROUP = 16
S_GROUPS = S_WIDTH // S_GROUP
S_STATE = 64
S_DT_MIN = 0.001
S_DT_MAX = 0.1
N_WIDTH = D_MODEL - M_WIDTH - S_WIDTH
N_HEAD_DIM = 128
N_HEADS = N_WIDTH // N_HEAD_DIM
N_KV_HEADS = N_HEADS // 4
CMP_BLOCK = 32
CMP_STRIDE = 16
CMP_HIDDEN = N_HEAD_DIM
SLC_BLOCK = 64
SLC_TOPK = 16
WINDOW = 512
Q_BLOCK = 128
ROPE_THETA = 10000.0
NEG_INF = -1e30
FORCED_SCORE = 1e9
D_FF = ((8 * D_MODEL // 3 + 127) // 128) * 128
FFN_CONV = 3
PROJ_SIZES = (2 * M_WIDTH, M_WIDTH, M_WIDTH, M_HEADS, M_HEADS, S_WIDTH, N_WIDTH, 6 * N_KV_HEADS * N_HEAD_DIM, 3 * N_HEADS)
D_PROJ = 4 * M_WIDTH + 2 * M_HEADS + S_WIDTH + N_WIDTH + 6 * N_KV_HEADS * N_HEAD_DIM + 3 * N_HEADS

kernel_name = "hybrid_mlstm_s5_nsa_trunk"

def rmsnorm(x, g):
    xf = x.astype(jnp.float32)
    r = lax.rsqrt(jnp.mean(xf * xf, axis=-1, keepdims=True) + EPS)
    return (xf * r).astype(x.dtype) * g

def rope(x, pos):
    half = x.shape[-1] // 2
    inv = ROPE_THETA ** (-jnp.arange(half, dtype=jnp.float32) / half)
    ang = pos.astype(jnp.float32)[..., None] * inv
    cos = jnp.cos(ang)[:, :, None, :]
    sin = jnp.sin(ang)[:, :, None, :]
    x1, x2 = x[..., :half], x[..., half:]
    return jnp.concatenate([x1 * cos - x2 * sin, x1 * sin + x2 * cos], axis=-1)

def causal_dwconv(x, w, b):
    width, ch = w.shape
    y = lax.conv_general_dilated(x, w[:, None, :].astype(x.dtype), window_strides=(1,),
                                 padding=[(width - 1, 0)], dimension_numbers=('NWC', 'WIO', 'NWC'),
                                 feature_group_count=ch)
    return y + b

def mlstm_group(qk, v, o_pre, i_pre, f_pre, conv_w, conv_b, i_bias, f_bias, norm_g):
    f32 = jnp.float32
    B, S, _ = v.shape
    H, Dh, L = M_HEADS, M_HEAD_DIM, M_CHUNK
    NC = S // L
    qk = jax.nn.silu(causal_dwconv(qk.astype(f32), conv_w, conv_b))
    q, k = jnp.split(qk, 2, axis=-1)

    def chunk(a):
        a = a.reshape((B, NC, L, H) + a.shape[3:])
        return jnp.moveaxis(a, 3, 1)

    qc = chunk(q.reshape(B, S, H, Dh))
    kc = chunk(k.reshape(B, S, H, Dh)) * (Dh ** -0.5)
    vc = chunk(v.astype(f32).reshape(B, S, H, Dh))
    ic = chunk(i_pre.astype(f32) + i_bias)
    logf = jax.nn.log_sigmoid(chunk(f_pre.astype(f32) + f_bias))
    g = jnp.cumsum(logf, axis=-1)
    g_last = g[..., -1]
    a = g_last[..., None] - g + ic
    a_max = jnp.max(a, axis=-1)
    w = jnp.exp(a - a_max[..., None])
    C_loc = jnp.einsum('bhcl,bhcld,bhcle->bhcde', w, kc, vc)
    n_loc = jnp.einsum('bhcl,bhcld->bhcd', w, kc)

    def step(carry, xs):
        C, n, m = carry
        Cl, nl, gl, am = xs
        m_new = jnp.maximum(gl + m, am)
        s_old = jnp.exp(gl + m - m_new)
        s_new = jnp.exp(am - m_new)
        C2 = s_old[..., None, None] * C + s_new[..., None, None] * Cl
        n2 = s_old[..., None] * n + s_new[..., None] * nl
        return (C2, n2, m_new), (C, n, m)

    init = (jnp.zeros((B, H, Dh, Dh), f32), jnp.zeros((B, H, Dh), f32), jnp.zeros((B, H), f32))
    xs = (jnp.moveaxis(C_loc, 2, 0), jnp.moveaxis(n_loc, 2, 0), jnp.moveaxis(g_last, 2, 0), jnp.moveaxis(a_max, 2, 0))
    _, (C_prev, n_prev, m_prev) = lax.scan(step, init, xs)
    C_prev = jnp.moveaxis(C_prev, 0, 2)
    n_prev = jnp.moveaxis(n_prev, 0, 2)
    m_prev = jnp.moveaxis(m_prev, 0, 2)

    causal = jnp.tril(jnp.ones((L, L), dtype=bool))
    Dlog = jnp.where(causal, g[..., :, None] - g[..., None, :] + ic[..., None, :], -jnp.inf)
    m_inter = g + m_prev[..., None]
    m_t = jnp.maximum(m_inter, jnp.max(Dlog, axis=-1))
    Sw = jnp.einsum('bhctd,bhcsd->bhcts', qc, kc) * jnp.exp(Dlog - m_t[..., None])
    inter = jnp.exp(m_inter - m_t)
    num = jnp.einsum('bhcts,bhcse->bhcte', Sw, vc) + inter[..., None] * jnp.einsum('bhctd,bhcde->bhcte', qc, C_prev)
    den = jnp.sum(Sw, axis=-1) + inter * jnp.einsum('bhctd,bhcd->bhct', qc, n_prev)
    h = num / jnp.maximum(jnp.abs(den), jnp.exp(-m_t))[..., None]
    h = jnp.moveaxis(h, 1, 3).reshape(B, S, H, Dh)
    h = rmsnorm(h, norm_g)
    h = jax.nn.sigmoid(o_pre.astype(f32)).reshape(B, S, H, Dh) * h
    return h.reshape(B, S, H * Dh)

def s5_group(u, lam_re, lam_im, log_dt, b_re, b_im, c_re, c_im, d_skip, w_glu, b_glu):
    f32 = jnp.float32
    B, S, W = u.shape
    uf = u.astype(f32)
    ug = uf.reshape(B, S, S_GROUPS, S_GROUP)
    lr = lam_re.astype(f32)
    li = lam_im.astype(f32)
    dt = jnp.exp(log_dt.astype(f32))[:, None]
    mag = jnp.exp(lr * dt)
    ar = mag * jnp.cos(li * dt)
    ai = mag * jnp.sin(li * dt)
    den = lr * lr + li * li
    nr = ar - 1.0
    zr = (nr * lr + ai * li) / den
    zi = (ai * lr - nr * li) / den
    br = b_re.astype(f32)
    bi = b_im.astype(f32)
    bbr = zr[..., None] * br - zi[..., None] * bi
    bbi = zr[..., None] * bi + zi[..., None] * br
    xr = jnp.einsum('bsgc,gnc->bsgn', ug, bbr)
    xi = jnp.einsum('bsgc,gnc->bsgn', ug, bbi)
    Ar = jnp.broadcast_to(ar, xr.shape)
    Ai = jnp.broadcast_to(ai, xr.shape)

    def combine(e1, e2):
        a1r, a1i, b1r, b1i = e1
        a2r, a2i, b2r, b2i = e2
        return (a2r * a1r - a2i * a1i, a2r * a1i + a2i * a1r,
                a2r * b1r - a2i * b1i + b2r, a2r * b1i + a2i * b1r + b2i)

    _, _, hr, hi = lax.associative_scan(combine, (Ar, Ai, xr, xi), axis=1)
    y = jnp.einsum('bsgn,gcn->bsgc', hr, c_re.astype(f32)) - jnp.einsum('bsgn,gcn->bsgc', hi, c_im.astype(f32))
    y = y.reshape(B, S, W) + d_skip * uf
    y = jax.nn.gelu(y)
    return y * jax.nn.sigmoid(y @ w_glu + b_glu)

def compress(x, pos_emb, w1, w2):
    B, S, Hk, Dh = x.shape
    NP = S // CMP_STRIDE
    pieces = x.reshape(B, NP, CMP_STRIDE, Hk, Dh)
    blocks = jnp.concatenate([pieces[:, :-1], pieces[:, 1:]], axis=2)
    blocks = blocks + pos_emb[:, None, :]
    flat = jnp.moveaxis(blocks, 3, 2).reshape(B, NP - 1, Hk, CMP_BLOCK * Dh)
    return jax.nn.gelu(flat @ w1) @ w2

def nsa_group(q, k_cmp, v_cmp, k_slc, v_slc, k_win, v_win, gates, cmp_pos, cmp_w1, cmp_w2):
    B, S, H, Dh = q.shape
    Hk = k_slc.shape[2]
    G = H // Hk
    n_slc = S // SLC_BLOCK
    ratio = SLC_BLOCK // CMP_STRIDE
    top = min(SLC_TOPK, n_slc)
    scale = Dh ** -0.5
    kc = compress(k_cmp, cmp_pos[0], cmp_w1[0], cmp_w2[0])
    vc = compress(v_cmp, cmp_pos[1], cmp_w1[1], cmp_w2[1])
    n_cmp = kc.shape[1]
    pad_cmp = n_slc * ratio - n_cmp
    blk_end = jnp.arange(n_cmp) * CMP_STRIDE + (CMP_BLOCK - 1)
    ks_blocks = jnp.moveaxis(k_slc.reshape(B, n_slc, SLC_BLOCK, Hk, Dh), 3, 1)
    vs_blocks = jnp.moveaxis(v_slc.reshape(B, n_slc, SLC_BLOCK, Hk, Dh), 3, 1)
    kw_pad = jnp.pad(k_win, ((0, 0), (WINDOW, 0), (0, 0), (0, 0)))
    vw_pad = jnp.pad(v_win, ((0, 0), (WINDOW, 0), (0, 0), (0, 0)))
    bidx = jnp.arange(B)[:, None, None, None]
    hidx = jnp.arange(Hk)[None, :, None, None]
    slc_j = jnp.arange(n_slc)
    in_blk = jnp.arange(SLC_BLOCK)
    win_off = jnp.arange(WINDOW + Q_BLOCK) - WINDOW

    def block(qb_idx):
        start = qb_idx * Q_BLOCK
        t = start + jnp.arange(Q_BLOCK)
        qb = lax.dynamic_slice_in_dim(q, start, Q_BLOCK, axis=1).reshape(B, Q_BLOCK, Hk, G, Dh)
        gb = lax.dynamic_slice_in_dim(gates, start, Q_BLOCK, axis=1).reshape(B, Q_BLOCK, Hk, G, 3)
        s = jnp.einsum('btkgd,bjkd->bkgtj', qb, kc) * scale
        valid = blk_end[None, :] <= t[:, None]
        p_cmp = jax.nn.softmax(jnp.where(valid, s, NEG_INF), axis=-1) * valid
        o_cmp = jnp.einsum('bkgtj,bjkd->btkgd', p_cmp, vc)
        pk = jnp.pad(p_cmp.sum(axis=2), ((0, 0), (0, 0), (0, 0), (0, pad_cmp)))
        pk = pk.reshape(B, Hk, Q_BLOCK, n_slc, ratio)
        last = pk[..., ratio - 1]
        imp = jnp.pad(last, ((0, 0), (0, 0), (0, 0), (1, 0)))[..., :-1] + 2.0 * jnp.sum(pk[..., :ratio - 1], axis=-1) + last
        tb = t // SLC_BLOCK
        allowed = slc_j[None, :] <= tb[:, None]
        forced = (slc_j[None, :] == 0) | (slc_j[None, :] == tb[:, None]) | (slc_j[None, :] == tb[:, None] - 1)
        score = jnp.where(forced, FORCED_SCORE, jnp.where(allowed, imp, -jnp.inf))
        _, idx = lax.top_k(score, top)
        ks = ks_blocks[bidx, hidx, idx].reshape(B, Hk, Q_BLOCK, top * SLC_BLOCK, Dh)
        vs = vs_blocks[bidx, hidx, idx].reshape(B, Hk, Q_BLOCK, top * SLC_BLOCK, Dh)
        kpos = (idx[..., None] * SLC_BLOCK + in_blk).reshape(B, Hk, Q_BLOCK, top * SLC_BLOCK)
        s = jnp.einsum('btkgd,bktnd->bkgtn', qb, ks) * scale
        smask = (kpos <= t[:, None])[:, :, None]
        p = jax.nn.softmax(jnp.where(smask, s, NEG_INF), axis=-1)
        o_slc = jnp.einsum('bkgtn,bktnd->btkgd', p, vs)
        kw = lax.dynamic_slice_in_dim(kw_pad, start, WINDOW + Q_BLOCK, axis=1)
        vw = lax.dynamic_slice_in_dim(vw_pad, start, WINDOW + Q_BLOCK, axis=1)
        wpos = start + win_off
        wmask = (wpos[None, :] <= t[:, None]) & (wpos[None, :] > t[:, None] - WINDOW) & (wpos[None, :] >= 0)
        s = jnp.einsum('btkgd,bnkd->bkgtn', qb, kw) * scale
        p = jax.nn.softmax(jnp.where(wmask, s, NEG_INF), axis=-1)
        o_win = jnp.einsum('bkgtn,bnkd->btkgd', p, vw)
        o = gb[..., 0:1] * o_cmp + gb[..., 1:2] * o_slc + gb[..., 2:3] * o_win
        return o.reshape(B, Q_BLOCK, H * Dh)

    out = lax.map(block, jnp.arange(S // Q_BLOCK))
    return jnp.moveaxis(out, 0, 1).reshape(B, S, H * Dh)

def hybrid_mixer(h, positions, w_in, w_out, m_conv_w, m_conv_b, m_i_bias, m_f_bias, m_norm_g,
                 s_lam_re, s_lam_im, s_log_dt, s_b_re, s_b_im, s_c_re, s_c_im, s_d, s_w_glu, s_b_glu,
                 n_cmp_pos, n_cmp_w1, n_cmp_w2):
    f32 = jnp.float32
    B, S, _ = h.shape
    proj = (h @ w_in).astype(f32)
    offs = np.cumsum(PROJ_SIZES)[:-1].tolist()
    m_qk, m_v, m_o, m_i, m_f, s_u, n_q, n_kv, n_g = jnp.split(proj, offs, axis=-1)
    y_m = mlstm_group(m_qk, m_v, m_o, m_i, m_f, m_conv_w, m_conv_b, m_i_bias, m_f_bias, m_norm_g)
    y_s = s5_group(s_u, s_lam_re, s_lam_im, s_log_dt, s_b_re, s_b_im, s_c_re, s_c_im, s_d, s_w_glu, s_b_glu)
    q = rope(n_q.reshape(B, S, N_HEADS, N_HEAD_DIM), positions)
    kv = n_kv.reshape(B, S, 6, N_KV_HEADS, N_HEAD_DIM)
    k_cmp = rope(kv[:, :, 0], positions)
    k_slc = rope(kv[:, :, 2], positions)
    k_win = rope(kv[:, :, 4], positions)
    gates = jax.nn.sigmoid(n_g).reshape(B, S, N_HEADS, 3)
    y_n = nsa_group(q, k_cmp, kv[:, :, 1], k_slc, kv[:, :, 3], k_win, kv[:, :, 5], gates,
                    n_cmp_pos, n_cmp_w1, n_cmp_w2)
    y = jnp.concatenate([y_m, y_s, y_n], axis=-1).astype(h.dtype)
    return y @ w_out

def conv_ffn(h, w_up, conv_w, conv_b, w_down):
    a, u = jnp.split(h @ w_up, 2, axis=-1)
    a = causal_dwconv(a, conv_w, conv_b)
    return (jax.nn.gelu(a) * u) @ w_down

def setup_inputs(seed: int = 0) -> dict:
    key = jax.random.key(seed)
    keys = iter(jax.random.split(key, 40))
    f32 = jnp.float32

    def nrm(shape, s):
        return jax.random.normal(next(keys), shape, f32) * s

    L, D = DEPTH, D_MODEL
    x = nrm((BATCH, SEQ, D), 1.0)
    c = nrm((BATCH, D), 1.0)
    offset = jax.random.randint(next(keys), (BATCH, 1), 0, 1024, dtype=jnp.int32)
    positions = offset + jnp.arange(SEQ, dtype=jnp.int32)[None, :]
    w_ada = nrm((L, D, 6 * D), 0.5 * D ** -0.5)
    b_ada = nrm((L, 6 * D), 0.02)
    g_pre_mix = 1.0 + nrm((L, D), 0.02)
    g_post_mix = 1.0 + nrm((L, D), 0.02)
    g_pre_ffn = 1.0 + nrm((L, D), 0.02)
    g_post_ffn = 1.0 + nrm((L, D), 0.02)
    w_in = nrm((L, D, D_PROJ), D ** -0.5)
    w_out = nrm((L, D, D), D ** -0.5)
    m_conv_w = nrm((L, M_CONV, 2 * M_WIDTH), M_CONV ** -0.5)
    m_conv_b = nrm((L, 2 * M_WIDTH), 0.02)
    m_i_bias = nrm((L, M_HEADS), 0.1)
    m_f_bias = jnp.linspace(3.0, 6.0, M_HEADS, dtype=f32)[None, :] + nrm((L, M_HEADS), 0.1)
    m_norm_g = 1.0 + nrm((L, M_HEADS, M_HEAD_DIM), 0.02)
    s_lam_re = -0.5 + nrm((L, S_GROUPS, S_STATE), 0.01)
    s_lam_im = jnp.pi * jnp.arange(S_STATE, dtype=f32) + nrm((L, S_GROUPS, S_STATE), 0.01)
    s_log_dt = jax.random.uniform(next(keys), (L, S_GROUPS), f32, float(np.log(S_DT_MIN)), float(np.log(S_DT_MAX)))
    s_b_re = nrm((L, S_GROUPS, S_STATE, S_GROUP), (2 * S_GROUP) ** -0.5)
    s_b_im = nrm((L, S_GROUPS, S_STATE, S_GROUP), (2 * S_GROUP) ** -0.5)
    s_c_re = nrm((L, S_GROUPS, S_GROUP, S_STATE), S_STATE ** -0.5)
    s_c_im = nrm((L, S_GROUPS, S_GROUP, S_STATE), S_STATE ** -0.5)
    s_d = nrm((L, S_WIDTH), 0.5)
    s_w_glu = nrm((L, S_WIDTH, S_WIDTH), S_WIDTH ** -0.5)
    s_b_glu = nrm((L, S_WIDTH), 0.02)
    n_cmp_pos = nrm((L, 2, CMP_BLOCK, N_HEAD_DIM), 0.1)
    n_cmp_w1 = nrm((L, 2, CMP_BLOCK * N_HEAD_DIM, CMP_HIDDEN), (CMP_BLOCK * N_HEAD_DIM) ** -0.5)
    n_cmp_w2 = nrm((L, 2, CMP_HIDDEN, N_HEAD_DIM), CMP_HIDDEN ** -0.5)
    f_w_up = nrm((L, D, 2 * D_FF), D ** -0.5)
    f_conv_w = nrm((L, FFN_CONV, D_FF), FFN_CONV ** -0.5)
    f_conv_b = nrm((L, D_FF), 0.02)
    f_w_down = nrm((L, D_FF, D), D_FF ** -0.5)
    return {"x": x, "c": c, "positions": positions, "w_ada": w_ada, "b_ada": b_ada,
            "g_pre_mix": g_pre_mix, "g_post_mix": g_post_mix, "g_pre_ffn": g_pre_ffn, "g_post_ffn": g_post_ffn,
            "w_in": w_in, "w_out": w_out, "m_conv_w": m_conv_w, "m_conv_b": m_conv_b,
            "m_i_bias": m_i_bias, "m_f_bias": m_f_bias, "m_norm_g": m_norm_g,
            "s_lam_re": s_lam_re, "s_lam_im": s_lam_im, "s_log_dt": s_log_dt, "s_b_re": s_b_re, "s_b_im": s_b_im,
            "s_c_re": s_c_re, "s_c_im": s_c_im, "s_d": s_d, "s_w_glu": s_w_glu, "s_b_glu": s_b_glu,
            "n_cmp_pos": n_cmp_pos, "n_cmp_w1": n_cmp_w1, "n_cmp_w2": n_cmp_w2,
            "f_w_up": f_w_up, "f_conv_w": f_conv_w, "f_conv_b": f_conv_b, "f_w_down": f_w_down}

def reference(x, c, positions, w_ada, b_ada, g_pre_mix, g_post_mix, g_pre_ffn, g_post_ffn,
              w_in, w_out, m_conv_w, m_conv_b, m_i_bias, m_f_bias, m_norm_g,
              s_lam_re, s_lam_im, s_log_dt, s_b_re, s_b_im, s_c_re, s_c_im, s_d, s_w_glu, s_b_glu,
              n_cmp_pos, n_cmp_w1, n_cmp_w2, f_w_up, f_conv_w, f_conv_b, f_w_down):
    B, S, D = x.shape
    cs = jax.nn.silu(c)
    for l in range(DEPTH):
        mod = (cs @ w_ada[l] + b_ada[l]).reshape(B, 6, D)
        sh1, sc1, gt1, sh2, sc2, gt2 = [mod[:, i][:, None, :] for i in range(6)]
        h = rmsnorm(x, g_pre_mix[l]) * (1.0 + sc1) + sh1
        y = hybrid_mixer(h, positions, w_in[l], w_out[l], m_conv_w[l], m_conv_b[l], m_i_bias[l], m_f_bias[l],
                         m_norm_g[l], s_lam_re[l], s_lam_im[l], s_log_dt[l], s_b_re[l], s_b_im[l], s_c_re[l],
                         s_c_im[l], s_d[l], s_w_glu[l], s_b_glu[l], n_cmp_pos[l], n_cmp_w1[l], n_cmp_w2[l])
        x = x + gt1 * rmsnorm(y, g_post_mix[l])
        h = rmsnorm(x, g_pre_ffn[l]) * (1.0 + sc2) + sh2
        y = conv_ffn(h, f_w_up[l], f_conv_w[l], f_conv_b[l], f_w_down[l])
        x = x + gt2 * rmsnorm(y, g_post_ffn[l])
    return x


_drawn_inputs = setup_inputs


def setup_inputs(seed=0):
    import zlib

    import numpy as np

    out = dict(_drawn_inputs(seed))
    spreads = {}
    factors = {'g_pre_mix': 5.985,
     'g_post_mix': 6.594,
     'g_pre_ffn': 5.11,
     'g_post_ffn': 7.106,
     'm_conv_b': 58.331,
     'm_i_bias': 64.0,
     'm_norm_g': 8.0,
     's_lam_re': 64.0,
     's_lam_im': 15.459,
     's_log_dt': 17.924,
     's_b_re': 23.325,
     's_b_im': 28.59,
     's_c_re': 25.966,
     's_c_im': 28.192,
     's_w_glu': 3.835,
     's_b_glu': 32.934,
     'n_cmp_pos': 2.751,
     'f_conv_b': 7.64}
    for name, (base, spread) in spreads.items():
        noise = np.random.default_rng([zlib.crc32(name.encode()), seed]).standard_normal(out[name].shape)
        drawn = base * np.exp(spread * noise) if base else spread * noise
        out[name] = __import__('jax').numpy.asarray(drawn.astype(out[name].dtype))
    for name, factor in factors.items():
        out[name] = (out[name] * factor).astype(out[name].dtype)
    return out
```

```python
import numpy as np
import concourse.bass as bass
from concourse import mybir
from concourse.alu_op_type import AluOpType as ALU
from contextlib import ExitStack

F32 = mybir.dt.float32
I32 = mybir.dt.int32
ACT = mybir.ActivationFunctionType
AX = mybir.AxisListType

P = 128
D, SEQ, DEPTH = 2048, 256, 2
EPS = 1e-6
KT = D // P
TT = SEQ // P
HD = 128
MH = 4
S_GROUPS, S_STATE, S_GROUP = 32, 64, 16
ST = S_GROUPS * S_STATE // P
UT = S_GROUPS * S_GROUP // P
SQ = ST // UT
SC = 2 * S_GROUP
NH, NKV = 8, 2
GQ = NH // NKV
CB, CS = 32, 16
NC = SEQ // CS - 1
DFF = ((8 * D // 3 + 127) // 128) * 128
FT = DFF // P
SCALE = float(HD) ** -0.5
NEG = -1e30
TWO_PI = 6.283185307179586
TURN = 1.0 / TWO_PI
MAGIC = 12582912.0
PI_1, PI_2 = 6.28125, 0.0019350051879882812
PI_3 = TWO_PI - PI_1 - PI_2
PI_IN = 3.1415925
TWO_PI_IN = 6.283185

CH = KT * P
RING = 5
C_IN = 0
C_GLU = 40
C_CMP = 41
C_OUT = 45
C_UP = 61
C_DOWN = C_UP + 2 * FT
CHUNKS = C_DOWN + FT
assert CHUNKS % RING == 0
CYCLES = CHUNKS // RING

T_O, T_U, T_Q, T_KV, T_QK, T_V = 0, 4, 8, 16, 28, 36
NPROJ = 40
T_KC, T_VC, T_KS, T_VS, T_KW, T_VW = (T_KV + 2 * j for j in range(6))
W_S5 = NPROJ
NMIX = 56

UC = 1024
UNITS = 6 * D // UC
UG = UC // P
UCH = 8

A_OFF, _o = {}, 0
for _name, _w in (("g_pre_mix", KT), ("g_post_mix", KT), ("g_pre_ffn", KT), ("g_post_ffn", KT), ("m_conv_w", 32),
                  ("m_conv_b", 8), ("m_norm_g", 4), ("s_d", 4), ("s_b_glu", 4), ("lam_re", ST), ("lam_im", ST),
                  ("log_dt", ST), ("f_conv_w", 3 * FT), ("f_conv_b", FT), ("i_bias", 1), ("f_bias", 1),
                  ("cmp_pos", 2 * CB), ("s_b_re", UT * P), ("s_b_im", UT * P), ("s_c_re", ST * SC),
                  ("s_c_im", ST * SC), ("w_gates", KT * 32), ("cmp_w2", 2 * P)):
    A_OFF[_name] = (_o, _w)
    _o += _w
A_W = _o
K_OFF, _o = {}, 0
for _name, _w in (("ident", P), ("ones", P), ("rot", P), ("mask", 2 * P), ("mask_t", P), ("cmp_mask", TT * NC),
                  ("cmp_valid", TT * NC), ("sel", MH * P), ("steps", SEQ), ("inv_freq", 1), ("half_pi", 1), ("eps", 1)):
    K_OFF[_name] = (_o, _w)
    _o += _w
K_W = _o


def trunk(nc, x, c_cols, pos, consts, aux_d, ada_d, ada_b, stream, out):
    with ExitStack() as ctx:
        def sb(name, shape, dt=F32):
            return ctx.enter_context(nc.sbuf_tensor(name, shape, dt))

        xs = sb("xs", [P, TT, D])
        hT = sb("hT", [P, KT, SEQ])
        mix = sb("mix", [P, NMIX, SEQ])
        ring = sb("ring", [P, RING, CH])
        ada_w = sb("ada_w", [P, 2, 2, UC])
        ada_acc = sb("ada_acc", [P, UC])
        gt_row = sb("gt_row", [P, D])
        aux = sb("aux", [P, A_W])
        cst = sb("cst", [P, K_W])
        posi = sb("posi", [P, SEQ], I32)
        rope_c = sb("rope_c", [P, SEQ])
        rope_s = sb("rope_s", [P, SEQ])
        mod = sb("mod", [P, 3, KT])
        modA = sb("modA", [P, KT])
        gg = sb("gg", [P, KT])
        cs = sb("cs", [P, KT])
        craw = sb("craw", [P, KT])
        stat = sb("stat", [P, 8])
        s5p = sb("s5p", [P, 20, ST])
        gates_t = sb("gates_t", [P, TT, 3 * NH])
        rows = sb("rows", [4, 10, SEQ])
        rcol = sb("rcol", [4, 4])
        bcol = sb("bcol", [P, 2, MH])
        att_s = sb("att_s", [P, 2, 16])
        sg24 = sb("sg24", [3 * NH, SEQ])
        ps = ctx.enter_context(nc.psum_tensor("ps", [P, 8, 512], F32))

        def A(name, a=None, b=None, p=P):
            o, w = A_OFF[name]
            return aux[0:p, o + (a or 0):o + (w if b is None else b)]

        def K(name, a=None, b=None, p=P):
            o, w = K_OFF[name]
            return cst[0:p, o + (a or 0):o + (w if b is None else b)]

        ident, ones = K("ident"), K("ones")

        class Signal:
            def __init__(self, name, per_layer=None):
                self.sem = ctx.enter_context(nc.semaphore(name))
                self.per_layer = per_layer
                self.given = 0

            def by(self, ins, n=1):
                self.given += n
                ins.then_inc(self.sem, n)
                return ins

            def wait(self, eng, l, k):
                eng.wait_ge(self.sem, l * self.per_layer + k)

            def chain(self, eng, l, ins):
                self.by(ins)
                self.wait(eng, l, self.given)


        def sem(name):
            return ctx.enter_context(nc.semaphore(name))

        cst_in, x_in, c_in, pos_in = sem("cst_in"), sem("x_in"), sem("c_in"), sem("pos_in")
        aux_in = sem("aux_in")
        ring_full = [sem(f"ring_full{s}") for s in range(RING)]
        ada_full = [sem(f"ada_full{s}") for s in range(2)]
        out_done = sem("out_done")
        w_used = sem("w_used")
        acc_zero, acc_bias = sem("acc_zero"), sem("acc_bias")
        ada_step = sem("ada_step")
        ada_red = sem("ada_red")
        mod_ready = sem("mod_ready")
        cs_ready, rope_dve, rope_act = sem("cs_ready"), sem("rope_dve"), sem("rope_act")
        rms_act = Signal("rms_act", 8)
        rstd = Signal("rstd", 8)
        dve = Signal("dve", DVE_STEPS)
        act = Signal("act", ACT_STEPS)
        x_ready = Signal("x_ready", 4)
        xn_ready = Signal("xn_ready", 4)
        h_tr = Signal("h_tr", 16)
        modA_ready = Signal("modA_ready", 2)
        h_act, h_dve = Signal("h_act", 16), Signal("h_dve", 16)
        gg_ready = Signal("gg_ready", 2)
        gt_mm = Signal("gt_mm", 2)
        gt_ready = Signal("gt_ready", 2)
        in_ev = sem("in_ev")
        gate_mm = Signal("gate_mm", 1)
        gate_ev = Signal("gate_ev", 3)
        s5_pd, s5_pa = Signal("s5_pd", 5), Signal("s5_pa", 4)
        s5_nf = Signal("s5_nf", UT)
        s5_tab = Signal("s5_tab", UT)
        s5_b = Signal("s5_b", ST // 2)
        s5_h = Signal("s5_h", ST // 2)
        s5_bv = Signal("s5_bv", ST // 2)
        s5_c = Signal("s5_c", ST // 2)
        s5_y = Signal("s5_y", UT)
        s5_g = Signal("s5_g", UT)
        glu_mm, glu_z, glu_y = Signal("glu_mm", 1), Signal("glu_z", 4), Signal("glu_y", 1)
        rp_mm, rp_d = Signal("rp_mm", 7), Signal("rp_d", 7)
        vt_mm, vt_ev = Signal("vt_mm", 5), Signal("vt_ev", 5)
        blk_ready = Signal("blk_ready", 2)
        ch_g, cc_mm, cc_ev = Signal("ch_g", 2), Signal("cc_mm", 1), Signal("cc_ev", 2)
        ITEMS = [(g, qt, kind) for g in range(NKV) for qt in range(TT) for kind in range(3)]
        NI = len(ITEMS)
        ns_s, ns_m, ns_e, ns_p = (Signal(n, NI) for n in ("ns_s", "ns_m", "ns_e", "ns_p"))
        ns_t, ns_pt, ns_o = (Signal(n, NI) for n in ("ns_t", "ns_pt", "ns_o"))
        ns_y = Signal("ns_y", NKV * TT)
        mc_d, mc_a = Signal("mc_d", 8), Signal("mc_a", 8)
        mg_a, mg_d = Signal("mg_a", 1), Signal("mg_d", 2)
        mb_mm, mb_ev = Signal("mb_mm", 1), Signal("mb_ev", 1)
        m_row = Signal("m_row", 2)
        m_dlog, m_exp = Signal("m_dlog", 2), Signal("m_exp", 2)
        m_sw, m_kw, m_kt, m_qi = Signal("m_sw", 2), Signal("m_kw", 1), Signal("m_kt", 1), Signal("m_qi", 1)
        m_c, m_cev = Signal("m_c", 1), Signal("m_cev", 2)
        m_num, m_abs, m_h, m_ss, m_rs, m_out = (Signal(n, 2) for n in ("m_num", "m_abs", "m_h", "m_ss", "m_rs", "m_out"))
        m_sig, m_qib_ready = Signal("m_sig", 1), Signal("m_qib_ready", 1)
        m_hsq = Signal("m_hsq", 2)
        ff_conv, ff_gelu, ff_mul = sem("ff_conv"), sem("ff_gelu"), sem("ff_mul")

        every = [v for v in list(locals().values()) if isinstance(v, Signal)]
        S5T = mix[:, W_S5:W_S5 + 16, :]
        s5_pt = S5T[:, 0:4, :]
        s5_k = S5T[:, 4:8, :]
        s5_S = S5T[:, 8:12, :]
        s5_C = S5T[:, 12:16, :]
        SP5 = lambda i: s5p[:, i, :]
        xn = mix[:, 0:KT, :].rearrange("p a b -> p (a b)").rearrange("p (t d) -> p t d", t=TT)
        hflat = hT[:, :, :].rearrange("p a b -> p (a b)")
        junk = hflat.rearrange("p (t d) -> p t d", t=TT)
        psf = ps[:, :, :].rearrange("p a b -> p (a b)")

        pr = hflat[:, 0:2048].rearrange("p (b h s) -> p b h s", b=2, h=GQ)
        pt = hflat[:, 2048:3072].rearrange("p (s n) -> p s n", s=2)
        vtok = S5T[:, 0:4, :].rearrange("p a b -> p (a b)").rearrange("p (a h s e) -> p a h s e", a=2, h=2, s=2)
        blk = S5T[:, 4:12, :].rearrange("p a b -> p (a b)")[:, 0:2 * CB * 2 * NC].rearrange(
            "p (v s h j) -> p v s h j", v=2, s=CB, h=2)
        hid = hflat[:, 3072:3072 + 60].rearrange("p (v n) -> p v n", v=2)
        kcT = hflat[:, 3136:3136 + 30]
        vct = hflat[0:NC, 3200:3200 + 256].rearrange("p (h e) -> p h e", h=2)
        rp_t = hflat[:, 3584:4096]
        vm = S5T[:, 12:16, :].rearrange("p a b -> p (a b)").rearrange("p (c h e) -> p c h e", c=2, h=MH)
        def m_buf(i):
            return S5T[:, 2 * i:2 * i + 2, :].rearrange("p a b -> p (a b)")
        m_dt = [hflat[:, 512 * i:512 * i + 512] for i in range(2)]
        m_swb = [hflat[:, 1024 + 512 * i:1536 + 512 * i] for i in range(2)]
        m_kwb, m_C, m_n, m_qib = (hflat[:, 2048 + 512 * i:2560 + 512 * i] for i in range(4))
        def m_cv(i):
            return S5T[:, 4 + i, :]
        m_hb, m_tb = m_buf(0), m_buf(1)
        m_e1, m_e2 = m_buf(2), m_buf(3)

        block = ctx.enter_context(nc.Block())

        @block.sync
        def _(sp):
            sp.dma_start(cst[:, :], consts[:, :]).then_inc(cst_in, 16)
            sp.dma_start(xs[:, :, :], x.rearrange("b (t p) d -> p (b t) d", p=P)).then_inc(x_in, 16)
            for s in range(RING):
                sp.dma_start(ring[:, s, :], stream[s, :, :]).then_inc(ring_full[s], 16)
            with sp.Fori(1, DEPTH * CYCLES) as cyc:
                for s in range(RING):
                    at = sp.snap(cyc * RING + s)
                    sp.wait_ge(w_used, cyc * RING + s - RING + 1)
                    sp.dma_start(ring[:, s, :], stream[bass.ds(at, 1), :, :].rearrange("a p n -> p (a n)")
                                 ).then_inc(ring_full[s], 16)
            x_ready.wait(sp, DEPTH - 1, 4)
            sp.dma_start(out.rearrange("b (t p) d -> p (b t) d", p=P), xs[:, :, :]).then_inc(out_done, 16)
            sp.wait_ge(out_done, 16)

        @block.gpsimd
        def _(pool):
            def wait(sem_, value):
                value = value if isinstance(value, int) else pool.to_reg(value)
                pool.wait_ge(c_in, 16)
                pool.wait_ge(sem_, value)

            def unit(u, first=False):
                if not first:
                    u = nc.s_assert_within(u, 0, DEPTH * UNITS - 1)
                    wait(ada_red, u)
                pool.memset(ada_acc[:, :], 0.0).then_inc(acc_zero, 1)
                wait(acc_zero, u + 1)
                pool.dma_start(ada_acc[0:1, :], ada_b[bass.ds(u, 1), :]).then_inc(acc_bias, 16)
                for j in range(UCH):
                    s = j % 2
                    if not (first and j < 2):
                        wait(ada_step, 2 * UCH * u + 2 * j - 2)
                    pool.dma_start(ada_w[:, s, :, :].rearrange("p a b -> p (a b)"),
                                   ada_d[bass.ds(u * UCH + j, 1), :, :].rearrange("a p n -> p (a n)")).then_inc(ada_full[s], 16)

            pool.dma_start(craw[:, :], c_cols[:, :]).then_inc(c_in, 16)
            pool.dma_start(posi[:, :], pos[:, :]).then_inc(pos_in, 16)
            pool.dma_start(aux[:, :], aux_d[0, :, :]).then_inc(aux_in, 16)
            unit(0, first=True)
            with pool.Fori(1, 4) as i:
                unit(i)
            with pool.Fori(0, DEPTH) as l:
                with pool.Fori(0, 6) as i:
                    unit(l * UNITS + 4 + i)
                with pool.Fori(0, 2) as i:
                    unit(l * UNITS + 10 + i)
                with pool.If(l < DEPTH - 1):
                    with pool.Fori(2, 6) as i:
                        unit(l * UNITS + 10 + i)
                    nxt = nc.s_assert_within(l + 1, 1, DEPTH - 1)
                    wait(w_used, l * CHUNKS + C_DOWN + 1)
                    pool.dma_start(aux[:, :], aux_d[bass.ds(nxt, 1), :, :].rearrange("a p n -> p (a n)")
                                   ).then_inc(aux_in, 16)

        @block.tensor
        def _(pe):
            def full(c, cyc):
                pe.wait_ge(ring_full[c % RING], cyc * 16 + 16)

            def reduce_unit(u):
                pe.wait_ge(ada_step, u * (2 * UCH) + 2 * UCH)
                for k in range(UG):
                    m = pe.matmul(ps[:, 7, k:k + 1], ada_acc[:, k * P:(k + 1) * P], ones[:, 0:1], start=True, stop=True)
                m.then_inc(ada_red, 1)

            def norm_transposes(l, n):
                xn_ready.wait(pe, l, 2 * n + 2)
                for b in range(8):
                    for k in range(2):
                        for t in range(TT):
                            m = pe.transpose(ps[:, b, k * SEQ + t * P:k * SEQ + (t + 1) * P],
                                             xn[:, t, (2 * b + k) * P:(2 * b + k + 1) * P], ident)
                    h_tr.by(m)

            def proj(l, cyc, c, bank, half=0, wait_ev=None):
                full(c, cyc)
                if wait_ev is not None:
                    pe.wait_ge(*wait_ev)
                for k in range(KT):
                    m = pe.matmul(ps[:, bank, half * SEQ:(half + 1) * SEQ], ring[:, c % RING, k * P:(k + 1) * P],
                                  hT[:, k, :], start=k == 0, stop=k == KT - 1)
                m.then_inc(w_used, 1)

            def gate_rows(l, n):
                gg_ready.wait(pe, l, n + 1)
                for k in range(KT):
                    m = pe.matmul(ps[:, k // 4, (k % 4) * P:(k % 4 + 1) * P], gg[:, k:k + 1].to_broadcast([P, P]),
                                  ident, start=True, stop=True)
                gt_mm.by(m)

            def to_tokens(l, c0, n_k, lhs):
                for k in range(n_k):
                    c = c0 + k
                    full(c, l * CYCLES + c // RING)
                    for t in range(TT):
                        for b in range(4):
                            m = pe.matmul(ps[:, 4 * t + b, :], lhs(k)[:, t * P:(t + 1) * P],
                                          ring[:, c % RING, b * 512:(b + 1) * 512], start=k == 0, stop=k == n_k - 1)
                    m.then_inc(w_used, 1)

            pe.wait_ge(cst_in, 16)
            reduce_unit(0)
            with pe.Fori(1, 4) as i:
                reduce_unit(i)

            with pe.Fori(0, DEPTH) as l:
                norm_transposes(l, 0)
                h_act.wait(pe, l, 8)
                h_dve.wait(pe, l, 8)
                for s in range(RING):
                    proj(l, l * CYCLES, s, s)
                with pe.Fori(1, 7) as i:
                    for s in range(RING):
                        proj(l, l * CYCLES + i, s, s, wait_ev=(in_ev, l * NPROJ + i * RING + (s - RING + 1)))
                    reduce_unit(l * UNITS + 3 + i)
                for s in range(RING):
                    proj(l, l * CYCLES + 7, s, s, wait_ev=(in_ev, l * NPROJ + 7 * RING + s - RING + 1))
                wg = A("w_gates").rearrange("p (k n) -> p k n", k=KT)
                for o, w, dst in ((0, 4, ps[0:4, 5, 0:SEQ]), (4, 4, ps[0:4, 5, SEQ:2 * SEQ]),
                                  (8, 24, ps[0:24, 6, 0:SEQ])):
                    for k in range(KT):
                        m = pe.matmul(dst, wg[:, k, o:o + w], hT[:, k, :], start=k == 0, stop=k == KT - 1)
                gate_mm.by(m)
                pe.wait_ge(in_ev, l * NPROJ + NPROJ)
                gate_rows(l, 0)

                s5_pd.wait(pe, l, 5)
                gate_ev.wait(pe, l, 3)
                for q in range(ST // 2):
                    ut = q // 2
                    if q >= 1:
                        s5_bv.wait(pe, l, q)
                    else:
                        gt_ready.wait(pe, l, 1)
                    for part, name in ((0, "s_b_re"), (1, "s_b_im")):
                        for half in range(2):
                            r = SC * (2 * (q % 2) + half)
                            o = A_OFF[name][0] + ut * P
                            m = pe.matmul(ps[:, 2 * part + half, 0:SEQ], aux[r:r + SC, o:o + P],
                                          mix[r:r + SC, T_U + ut, :], start=True, stop=True)
                    s5_b.by(m)
                    s5_h.wait(pe, l, q + 1)
                    if q % 2 == 0 and ut >= 1:
                        s5_y.wait(pe, l, ut)
                    for half in range(2):
                        j = 2 * q + half
                        r = SC * (j % SQ)
                        for part, name in ((0, "s_c_re"), (1, "s_c_im")):
                            o = A_OFF[name][0] + j * SC
                            hh = s5_pt if part == 0 else s5_k
                            m = pe.matmul(ps[r:r + SC, 6, 0:SEQ], aux[:, o:o + SC], hh[:, half, :],
                                          start=part == 0, stop=part == 1)
                    s5_c.by(m)
                full(C_GLU, l * CYCLES + C_GLU // RING)
                s5_g.wait(pe, l, UT)
                for n in range(4):
                    for k in range(4):
                        m = pe.matmul(ps[:, n // 2, (n % 2) * SEQ:(n % 2 + 1) * SEQ],
                                      ring[:, C_GLU % RING, k * 512 + n * P:k * 512 + (n + 1) * P],
                                      mix[:, T_U + k, :], start=k == 0, stop=k == 3)
                    if n == 1:
                        glu_mm.by(m)
                m.then_inc(w_used, 1)

                for n, t in enumerate(ROPE_TILES):
                    if n >= 2:
                        rp_d.wait(pe, l, n - 1)
                    m = pe.matmul(ps[:, 4 + n % 2, :], K("rot"), mix[:, t:t + 2, :], start=True, stop=True)
                    rp_mm.by(m)
                glu_z.wait(pe, l, 4)
                for a, t0 in enumerate((T_VS, T_VW)):
                    for h in range(2):
                        for s in range(2):
                            m = pe.transpose(ps[:, a, (2 * h + s) * P:(2 * h + s + 1) * P],
                                             mix[:, t0 + h, s * P:(s + 1) * P], ident)
                    vt_mm.by(m)
                for ck in range(2):
                    for h in range(MH):
                        m = pe.transpose(ps[:, 2 + ck, h * P:(h + 1) * P], mix[:, T_V + h, ck * P:(ck + 1) * P], ident)
                    vt_mm.by(m)
                pe.wait_ge(cst_in, 16)
                s5_y.wait(pe, l, UT)
                for t in range(TT):
                    m = pe.transpose(ps[:, 6, 32 * t:32 * t + 24], sg24[:, t * P:(t + 1) * P], K("ident", 0, 24, 24))
                vt_mm.by(m)
                for v in range(2):
                    blk_ready.wait(pe, l, v + 1)
                    for hf in range(2):
                        c = C_CMP + 2 * v + hf
                        full(c, l * CYCLES + c // RING)
                        for j in range(16):
                            pos_i = 16 * hf + j
                            m = pe.matmul(ps[:, 7, 64 * v:64 * v + 30], ring[:, c % RING, j * P:(j + 1) * P],
                                          blk[:, v, pos_i, :, :], start=pos_i == 0, stop=pos_i == CB - 1)
                        m.then_inc(w_used, 1)
                ch_g.wait(pe, l, 2)
                w2o = A_OFF["cmp_w2"][0]
                pe.matmul(ps[:, 7, 128:158], aux[:, w2o:w2o + P], hid[:, 0, :], start=True, stop=True)
                for h in range(NKV):
                    m = pe.matmul(ps[0:NC, 7, 256 + h * P:384 + h * P], hid[:, 1, h * NC:(h + 1) * NC],
                                  aux[:, w2o + P:w2o + 2 * P], start=True, stop=True)
                cc_mm.by(m)

                def scores(n):
                    g, qt, kind = ITEMS[n]
                    if n >= 2:
                        ns_m.wait(pe, l, n - 1)
                    b = 2 * (n % 2)
                    for h in range(GQ):
                        q = mix[:, T_Q + GQ * g + h, qt * P:(qt + 1) * P]
                        if kind == 0:
                            m = pe.matmul(ps[:, b, h * 16:h * 16 + NC], q, kcT[:, g * NC:(g + 1) * NC],
                                          start=True, stop=True)
                        else:
                            kt = (T_KS if kind == 1 else T_KW) + g
                            nk = (qt + 1) * P
                            m = pe.matmul(ps[:, b + h // 2, (h % 2) * SEQ:(h % 2) * SEQ + nk], q, mix[:, kt, 0:nk],
                                          start=True, stop=True)
                    ns_s.by(m)

                rp_d.wait(pe, l, 7)
                cc_ev.wait(pe, l, 2)
                vt_ev.wait(pe, l, 5)
                scores(0)
                for n, (g, qt, kind) in enumerate(ITEMS):
                    if n + 1 < NI:
                        scores(n + 1)
                    ns_p.wait(pe, l, n + 1)
                    if n >= 1:
                        ns_pt.wait(pe, l, n)
                    nst = 1 if kind == 0 else qt + 1
                    for s in range(nst):
                        for h in range(GQ):
                            if kind == 0:
                                m = pe.transpose(ps[0:NC, 4, h * P:(h + 1) * P], pr[:, n % 2, h, 0:NC], ident)
                            else:
                                m = pe.transpose(ps[:, 4 + s, h * P:(h + 1) * P], pr[:, n % 2, h, s * P:(s + 1) * P], ident)
                    ns_t.by(m)
                    ns_pt.wait(pe, l, n + 1)
                    if kind == 0 and n >= 3:
                        ns_y.wait(pe, l, n // 3)
                    if kind == 0:
                        m = pe.matmul(ps[:, 6, :], vct[:, g, :], pt[0:NC, 0, :], start=True, stop=False)
                    else:
                        for s in range(nst):
                            m = pe.matmul(ps[:, 6, :], vtok[:, kind - 1, g, s, :], pt[:, s, :], start=False,
                                          stop=kind == 2 and s == nst - 1)
                    ns_o.by(m)

                pe.wait_ge(cst_in, 16)
                mg_d.wait(pe, l, 1)
                for ck in range(2):
                    m = pe.transpose(ps[:, 7, 4 * ck:4 * ck + 4], rows[:, 3, ck * P:(ck + 1) * P], K("ident", 0, 4, 4))
                mb_mm.by(m)
                mc_a.wait(pe, l, 8)
                ns_y.wait(pe, l, 4)
                for ck in range(2):
                    m_row.wait(pe, l, ck + 1)
                    if ck == 1:
                        m_out.wait(pe, l, 1)
                        mb_ev.wait(pe, l, 1)
                    for b, r in ((0, 6), (1, 8)) + (((5, 7),) if ck else ()):
                        for h in range(MH):
                            m = pe.matmul(ps[:, b, h * P:(h + 1) * P], K("sel", h * P, (h + 1) * P, 4),
                                          rows[:, r, ck * P:(ck + 1) * P], start=True, stop=True)
                    for h in range(MH):
                        m = pe.matmul(ps[:, 2, h * P:(h + 1) * P], mix[:, T_QK + 4 + h, ck * P:(ck + 1) * P],
                                      mix[:, T_QK + h, ck * P:(ck + 1) * P], start=True, stop=True)
                    if ck == 0:
                        for h in range(MH):
                            m = pe.transpose(ps[:, 5, h * P:(h + 1) * P], mix[:, T_QK + 4 + h, 0:P], ident)
                    m_kt.by(m) if ck == 0 else m_qi.by(m)
                    m_sw.wait(pe, l, ck + 1)
                    if ck == 1:
                        m_qib_ready.wait(pe, l, 1)
                        m_cev.wait(pe, l, 2)
                    for h in range(MH):
                        hs = slice(h * P, (h + 1) * P)
                        pe.matmul(ps[:, 3, hs], vm[:, ck, h, :], m_swb[ck][:, hs], start=True, stop=ck == 0)
                        if ck:
                            pe.matmul(ps[:, 3, hs], m_C[:, hs], m_qib[:, hs], start=False, stop=True)
                        m = pe.matmul(ps[:, 4, hs], ones, m_swb[ck][:, hs], start=True, stop=ck == 0)
                        if ck:
                            m = pe.matmul(ps[:, 4, hs], m_n[:, hs], m_qib[:, hs], start=False, stop=True)
                    m_num.by(m)
                    if ck == 0:
                        m_kw.wait(pe, l, 1)
                        for h in range(MH):
                            hs = slice(h * P, (h + 1) * P)
                            pe.matmul(ps[:, 6, hs], m_kwb[:, hs], vm[:, 0, h, :], start=True, stop=True)
                            m = pe.matmul(ps[:, 7, hs], m_kwb[:, hs], ones, start=True, stop=True)
                        m_c.by(m)
                    m_hsq.wait(pe, l, ck + 1)
                    m = pe.matmul(ps[:, 2, :], ones, m_tb, start=True, stop=True)
                    m_ss.by(m)

                m_out.wait(pe, l, 2)
                glu_y.wait(pe, l, 1)
                to_tokens(l, C_OUT, KT, lambda k: mix[:, k, :])
                norm_transposes(l, 1)
                h_act.wait(pe, l, 16)
                h_dve.wait(pe, l, 16)

                def up(i, k, wait_mul):
                    for half in range(2):
                        cc = C_UP + 2 * k + half
                        proj(l, l * CYCLES + 2 * i + cc // RING, cc, k, half,
                             (ff_mul, l * FT + 5 * i + (k - 4)) if half == 0 and wait_mul else None)

                for k in range(5):
                    up(0, k, False)
                reduce_unit(l * UNITS + 10)
                with pe.Fori(1, 2) as i:
                    for k in range(5):
                        up(i, k, True)
                    reduce_unit(l * UNITS + 10 + i)
                with pe.Fori(2, 6) as i:
                    for k in range(5):
                        up(i, k, True)
                    with pe.If(l < DEPTH - 1):
                        reduce_unit(l * UNITS + 10 + i)
                with pe.Fori(6, 8) as i:
                    for k in range(5):
                        up(i, k, True)
                for k in range(3):
                    up(8, k, True)
                pe.wait_ge(ff_mul, l * FT + FT)
                gate_rows(l, 1)
                gt_ready.wait(pe, l, 2)
                to_tokens(l, C_DOWN, FT, lambda k: mix[:, k, :])

        @block.scalar
        def _(s):
            s.wait_ge(c_in, 16)
            s.activation(cs[:, :], craw[:, :], ACT.Silu).then_inc(cs_ready, 1)
            for n, dst in enumerate((rope_s, rope_c)):
                s.wait_ge(rope_dve, ROPE_STEPS[n])
                s.activation(dst[:, :], mix[:, 2 + n, :], ACT.Sin).then_inc(rope_act, 1)
            s.wait_ge(x_in, 16)

            with s.Fori(0, DEPTH) as l:
                def rms(n, src):
                    for t in range(TT):
                        rms_act.by(s.activation(junk[:, t, :], src(t), ACT.Square, accum_out=stat[:, t:t + 1]))
                    rms_act.wait(s, l, 2 * n + 2)
                    for t in range(TT):
                        rstd.by(s.activation(stat[:, 2 + t:3 + t], stat[:, t:t + 1], ACT.Sqrt, bias=K("eps"),
                                             scale=1.0 / D))

                def h_evac(n):
                    modA_ready.wait(s, l, n + 1)
                    for b in range(0, 8, 2):
                        h_tr.wait(s, l, 8 * n + b + 1)
                        for k in (2 * b, 2 * b + 1):
                            h_act.by(s.activation(hT[:, k, :], ps[:, b, k % 2 * SEQ:(k % 2 + 1) * SEQ], ACT.Identity,
                                                  bias=mod[:, 1, k:k + 1], scale=modA[:, k:k + 1]))

                def gt_evac(n):
                    gt_mm.wait(s, l, n + 1)
                    gt_ready.by(s.activation(gt_row[:, :], psf[:, 0:D], ACT.Copy))

                rms(0, lambda t: xs[:, t, :])
                h_evac(0)
                def in_tile(i, k, dst):
                    s.wait_ge(w_used, l * CHUNKS + i * RING + (k + 1))
                    s.activation(dst, ps[:, k, 0:SEQ], ACT.Copy).then_inc(in_ev, 1)
                with s.Fori(0, 7) as i:
                    for k in range(RING):
                        in_tile(i, k, mix[:, bass.ds(i * RING + (k + T_U), 1), :].rearrange("p a b -> p (a b)"))
                for k in range(RING):
                    in_tile(7, k, mix[:, (35 + k + T_U) % NPROJ, :])
                gate_mm.wait(s, l, 1)
                gate_ev.by(s.activation(rows[:, 0, :], ps[0:4, 5, 0:SEQ], ACT.Identity, bias=A("i_bias", p=4)))
                gate_ev.by(s.activation(rows[:, 1, :], ps[0:4, 5, SEQ:2 * SEQ], ACT.Identity, bias=A("f_bias", p=4)))
                gate_ev.by(s.activation(sg24[:, :], ps[0:24, 6, 0:SEQ], ACT.Sigmoid))
                gt_evac(0)

                s5_pa.by(s.activation(SP5(0), A("log_dt"), ACT.Exp))
                s5_pd.wait(s, l, 1)
                s5_pa.by(s.activation(SP5(2), SP5(1), ACT.Exp))
                s5_pd.wait(s, l, 2)
                s5_pa.by(s.activation(SP5(7), SP5(5), ACT.Sin))
                s5_pd.wait(s, l, 3)
                s5_pa.by(s.activation(SP5(8), SP5(6), ACT.Sin))
                for u in range(UT):
                    s5_nf.wait(s, l, u + 1)
                    s.activation(s5_S, s5_pt, ACT.Sin, scale=-TWO_PI_IN)
                    s5_tab.by(s.activation(s5_C, s5_k, ACT.Sin, scale=-TWO_PI_IN, bias=K("half_pi")))
                    if u:
                        s5_y.wait(s, l, u)
                        s5_g.by(s.activation(mix[:, T_U + u - 1, :], mix[:, T_U + u - 1, :], ACT.Gelu_apprx_tanh))
                s5_y.wait(s, l, UT)
                s5_g.by(s.activation(mix[:, T_U + UT - 1, :], mix[:, T_U + UT - 1, :], ACT.Gelu_apprx_tanh))
                for n in range(4):
                    if n % 2 == 0:
                        if n == 0:
                            glu_mm.wait(s, l, 1)
                        else:
                            s.wait_ge(w_used, l * CHUNKS + C_GLU + 1)
                    o = A_OFF["s_b_glu"][0]
                    glu_z.by(s.activation(S5T[:, n, :], ps[:, n // 2, (n % 2) * SEQ:(n % 2 + 1) * SEQ], ACT.Sigmoid,
                                          bias=aux[:, o + n:o + n + 1]))

                glu_y.wait(s, l, 1)
                for a in range(2):
                    vt_mm.wait(s, l, a + 1)
                    vt_ev.by(s.activation(vtok[:, a, :, :, :].rearrange("p h s e -> p (h s e)"), ps[:, a, :], ACT.Copy))
                for ck in range(2):
                    vt_mm.wait(s, l, 3 + ck)
                    vt_ev.by(s.activation(vm[:, ck, :, :].rearrange("p h e -> p (h e)"), ps[:, 2 + ck, :], ACT.Copy))
                vt_mm.wait(s, l, 5)
                vt_ev.by(s.activation(gates_t[:, :, :], ps[:, 6, 0:64].rearrange("p (t n) -> p t n", t=2)[:, :, 0:24],
                                      ACT.Copy))
                s.wait_ge(w_used, l * CHUNKS + C_CMP + 4)
                for v in range(2):
                    ch_g.by(s.activation(hid[:, v, :], ps[:, 7, 64 * v:64 * v + 30], ACT.Gelu_apprx_tanh))
                cc_mm.wait(s, l, 1)
                cc_ev.by(s.activation(kcT, ps[:, 7, 128:158], ACT.Copy))
                cc_ev.by(s.activation(vct[:, :, :].rearrange("p h e -> p (h e)"), ps[0:NC, 7, 256:512], ACT.Copy))
                for n, (g, qt, kind) in enumerate(ITEMS):
                    nk = NC if kind == 0 else (qt + 1) * P
                    ns_m.wait(s, l, n + 1)
                    for h in range(GQ):
                        e = s.activation(pr[:, n % 2, h, 0:nk], pr[:, n % 2, h, 0:nk], ACT.Exp,
                                         bias=att_s[:, n % 2, h:h + 1], accum_out=att_s[:, n % 2, 4 + h:5 + h])
                    ns_e.by(e)
                    ns_t.wait(s, l, n + 1)
                    if n:
                        ns_o.wait(s, l, n)
                    if kind == 0:
                        ns_pt.by(s.activation(pt[0:NC, 0, :], ps[0:NC, 4, :], ACT.Copy))
                    else:
                        ns_pt.by(s.activation(pt[:, 0:qt + 1, :], ps[:, 4:4 + qt + 1, :], ACT.Copy))
                    if kind == 2:
                        ns_o.wait(s, l, n + 1)
                        ns_y.by(s.activation(mix[:, T_Q + GQ * g:T_Q + GQ * (g + 1), qt * P:(qt + 1) * P],
                                             ps[:, 6, :].rearrange("p (h t) -> p h t", h=GQ), ACT.Copy))

                for i in range(8):
                    mc_d.wait(s, l, i + 1)
                    mc_a.by(s.activation(mix[:, T_QK + i, :], m_cv(i), ACT.Silu))
                m_sig.by(s.activation(mix[:, T_O:T_O + 4, :], mix[:, T_O:T_O + 4, :], ACT.Sigmoid))
                gate_ev.wait(s, l, 3)
                act.chain(s, l, s.activation(rows[:, 2, :], rows[:, 1, :], ACT.Abs))
                act.chain(s, l, s.activation(rows[:, 2, :], rows[:, 2, :], ACT.Exp, scale=-1.0))
                mg_a.by(s.activation(rows[:, 2, :], rows[:, 2, :], ACT.Ln, bias=1.0))
                mb_mm.wait(s, l, 1)
                mb_ev.by(s.activation(bcol[:, :, :].rearrange("p c h -> p (c h)"), ps[:, 7, 0:8], ACT.Copy))
                mg_d.wait(s, l, 2)
                m_row.by(s.activation(rows[:, 8, :], rows[:, 5, :], ACT.Exp, scale=-1.0))
                m_row.by(s.activation(rows[:, 7, P:SEQ], rows[:, 4, P:SEQ], ACT.Exp, scale=-1.0, bias=rcol[:, 0:1]))
                for ck in range(2):
                    m_dlog.wait(s, l, ck + 1)
                    m_exp.by(s.activation(m_dt[ck], m_dt[ck], ACT.Exp))
                    m_num.wait(s, l, ck + 1)
                    m_abs.by(s.activation(m_e1, ps[:, 4, :], ACT.Abs))
                    if ck == 0:
                        m_c.wait(s, l, 1)
                        m_cev.by(s.activation(m_C, ps[:, 6, :], ACT.Copy))
                        m_cev.by(s.activation(m_n, ps[:, 7, :], ACT.Copy))
                    m_h.wait(s, l, ck + 1)
                    m_hsq.by(s.activation(m_tb, m_hb, ACT.Square))
                    m_ss.wait(s, l, ck + 1)
                    m_rs.by(s.activation(m_e2, ps[:, 2, :], ACT.Sqrt, bias=K("eps"), scale=1.0 / HD))

                s.wait_ge(w_used, l * CHUNKS + C_UP)
                rms(1, lambda t: psf[:, t * D:(t + 1) * D])
                x_ready.wait(s, l, 2)
                rms(2, lambda t: xs[:, t, :])
                h_evac(1)

                def gelu(i, k):
                    s.wait_ge(ff_conv, (l * FT + i * 5 + k) * 3 + 3)
                    t = mix[:, bass.ds(i * 5 + k, 1), :].rearrange("p a b -> p (a b)")
                    s.activation(t, t, ACT.Gelu_apprx_tanh).then_inc(ff_gelu, 1)
                with s.Fori(0, 8) as i:
                    for k in range(5):
                        gelu(i, k)
                for k in range(3):
                    s.wait_ge(ff_conv, (l * FT + 40 + k) * 3 + 3)
                    s.activation(mix[:, 40 + k, :], mix[:, 40 + k, :], ACT.Gelu_apprx_tanh).then_inc(ff_gelu, 1)
                gt_evac(1)
                s.wait_ge(w_used, (l + 1) * CHUNKS)
                rms(3, lambda t: psf[:, t * D:(t + 1) * D])
                x_ready.wait(s, l, 4)

        @block.vector
        def _(v):
            def tt(o, a, b, op):
                return v.tensor_tensor(o, a, b, op)

            def ts(o, a, s1, s2, op0, op1):
                return v.tensor_scalar(o, a, s1, s2, op0, op1)

            def stt(o, a, s, b, op0, op1):
                return v.scalar_tensor_tensor(o, a, s, b, op0, op1)

            def reduced_angle(step, src, k, r, shifted, scratch):
                step(ts(k, src, TURN, MAGIC, ALU.mult, ALU.add))
                step(ts(k, k, -MAGIC, None, ALU.add, ALU.bypass))
                step(stt(r, k, -PI_1, src, ALU.mult, ALU.add))
                step(stt(r, k, -PI_2, r, ALU.mult, ALU.add))
                step(stt(r, k, -PI_3, r, ALU.mult, ALU.add))
                step(ts(r, r, PI_IN, -PI_IN, ALU.min, ALU.max))
                step(ts(shifted, r, TWO_PI / 4, None, ALU.add, ALU.bypass))
                step(ts(scratch, shifted, PI_IN, -TWO_PI, ALU.is_gt, ALU.mult))
                step(tt(shifted, shifted, scratch, ALU.add))
                step(ts(shifted, shifted, PI_IN, -PI_IN, ALU.min, ALU.max))

            done = [0]

            def pro(ins):
                done[0] += 1
                ins.then_inc(rope_dve, 1)
                v.wait_ge(rope_dve, done[0])

            v.wait_ge(cst_in, 16)
            v.wait_ge(pos_in, 16)
            pro(v.tensor_copy(mix[:, 0, :], posi[:, :]))
            pro(ts(mix[:, 0, :], mix[:, 0, :], K("inv_freq"), None, ALU.mult, ALU.bypass))
            reduced_angle(pro, mix[:, 0, :], mix[:, 1, :], mix[:, 2, :], mix[:, 3, :], mix[:, 4, :])
            assert done[0] == ROPE_STEPS[1]
            v.wait_ge(cs_ready, 1)

            def ada_chunk(u, j):
                if j == 0:
                    v.wait_ge(acc_bias, u * 16 + 16)
                v.wait_ge(ada_full[j % 2], u * (UCH // 2 * 16) + 16 * (j // 2) + 16)
                for k in range(2):
                    stt(ada_acc[:, :], ada_w[:, j % 2, k, :], cs[:, 2 * j + k:2 * j + k + 1], ada_acc[:, :],
                        ALU.mult, ALU.add).then_inc(ada_step, 1)
                    v.wait_ge(ada_step, u * (2 * UCH) + 2 * j + k + 1)

            def ada_finish(u, col):
                v.wait_ge(ada_red, u + 1)
                v.tensor_copy(col, ps[:, 7, 0:UG]).then_inc(mod_ready, 1)

            modf = mod[:, :, :].rearrange("p a b -> p (a b)")
            with v.Fori(0, 4) as i:
                for j in range(UCH):
                    ada_chunk(i, j)
                ada_finish(i, modf[:, bass.ds(i * UG + 2 * UG, UG)])
            v.wait_ge(x_in, 16)
            v.wait_ge(rope_act, 2)

            with v.Fori(0, DEPTH) as l:
                step = lambda ins: dve.chain(v, l, ins)

                def norm_in(n, gain):
                    v.wait_ge(mod_ready, l * UNITS + (4 if n == 0 else 10))
                    modA_ready.by(stt(modA[:, :], mod[:, 2, :], 1.0, A(gain), ALU.add, ALU.mult))
                    for t in range(TT):
                        rstd.wait(v, l, 4 * n + t + 1)
                        step(v.reciprocal(stat[:, 4 + t:5 + t], stat[:, 2 + t:3 + t]))
                        xn_ready.by(ts(xn[:, t, :], xs[:, t, :], stat[:, 4 + t:5 + t], None, ALU.mult, ALU.bypass))
                    modA_ready.wait(v, l, n + 1)
                    for b in range(1, 8, 2):
                        h_tr.wait(v, l, 8 * n + b + 1)
                        for k in (2 * b, 2 * b + 1):
                            h_dve.by(ts(hT[:, k, :], ps[:, b, k % 2 * SEQ:(k % 2 + 1) * SEQ], modA[:, k:k + 1],
                                        mod[:, 1, k:k + 1], ALU.mult, ALU.add))

                def residual(n):
                    gt_ready.wait(v, l, n + 1)
                    for t in range(TT):
                        rstd.wait(v, l, 4 * n + 2 + t + 1)
                        step(v.reciprocal(stat[:, 6 + t:7 + t], stat[:, 2 + t:3 + t]))
                        tmp = mix[:, 0:8, :].rearrange("p a b -> p (a b)")
                        step(stt(tmp, psf[:, t * D:(t + 1) * D], stat[:, 6 + t:7 + t], gt_row[:, :], ALU.mult, ALU.mult))
                        x_ready.by(tt(xs[:, t, :], xs[:, t, :], tmp, ALU.add))
                        x_ready.wait(v, l, 2 * n + t + 1)

                def gate_gain(n, gain):
                    gg_ready.by(tt(gg[:, :], mod[:, 0, :], A(gain), ALU.mult))

                v.wait_ge(aux_in, l * 16 + 16)
                norm_in(0, "g_pre_mix")
                with v.Fori(0, 6) as i:
                    for j in range(UCH):
                        ada_chunk(l * UNITS + 4 + i, j)
                    ada_finish(l * UNITS + 4 + i, modf[:, bass.ds(i * UG, UG)])
                v.wait_ge(mod_ready, l * UNITS + 10)
                gate_gain(0, "g_post_mix")

                s5_pa.wait(v, l, 1)
                s5_pd.by(tt(SP5(1), A("lam_re"), SP5(0), ALU.mult))
                step(tt(SP5(3), A("lam_im"), SP5(0), ALU.mult))
                reduced_angle(step, SP5(3), SP5(4), SP5(5), SP5(6), SP5(9))
                s5_pd.by(ts(SP5(10), SP5(5), TURN, None, ALU.mult, ALU.bypass))
                s5_pd.by(tt(SP5(11), A("lam_re"), A("lam_re"), ALU.mult))
                step(tt(SP5(12), A("lam_im"), A("lam_im"), ALU.mult))
                step(tt(SP5(11), SP5(11), SP5(12), ALU.add))
                step(v.reciprocal(SP5(11), SP5(11)))
                s5_pa.wait(v, l, 4)
                step(tt(SP5(12), SP5(2), SP5(8), ALU.mult))
                step(tt(SP5(13), SP5(2), SP5(7), ALU.mult))
                step(ts(SP5(12), SP5(12), -1.0, None, ALU.add, ALU.bypass))
                step(tt(SP5(14), SP5(12), A("lam_re"), ALU.mult))
                step(tt(SP5(15), SP5(13), A("lam_im"), ALU.mult))
                step(tt(SP5(14), SP5(14), SP5(15), ALU.add))
                step(tt(SP5(14), SP5(14), SP5(11), ALU.mult))
                step(tt(SP5(15), SP5(13), A("lam_re"), ALU.mult))
                step(tt(SP5(16), SP5(12), A("lam_im"), ALU.mult))
                step(tt(SP5(15), SP5(15), SP5(16), ALU.subtract))
                step(tt(SP5(15), SP5(15), SP5(11), ALU.mult))
                cr = A("s_c_re").rearrange("p (j c) -> p j c", j=ST)
                ci = A("s_c_im").rearrange("p (j c) -> p j c", j=ST)
                zr = s5p[:, 14, :].unsqueeze(2).to_broadcast([P, ST, SC])
                zi = s5p[:, 15, :].unsqueeze(2).to_broadcast([P, ST, SC])
                b5 = [S5T[:, 2 * i:2 * i + 2, :].rearrange("p a b -> p (a b)").rearrange("p (j c) -> p j c", j=ST)
                      for i in range(4)]
                step(tt(b5[0], cr, zr, ALU.mult))
                step(tt(b5[1], ci, zi, ALU.mult))
                step(tt(b5[2], cr, zi, ALU.mult))
                step(tt(b5[3], ci, zr, ALU.mult))
                s5_pd.by(tt(cr, b5[0], b5[1], ALU.subtract))
                s5_pd.by(stt(ci, b5[2], -1.0, b5[3], ALU.mult, ALU.subtract))
                s5_pd.wait(v, l, 5)
                pv = S5T[:, 0:8, :].rearrange("p a b -> p (a b)").rearrange("p (i n) -> p i n", i=4)
                for u in range(UT):
                    if u:
                        s5_c.wait(v, l, 2 * u)
                    turns = s5p[:, 10, SQ * u:SQ * (u + 1)].unsqueeze(2).to_broadcast([P, SQ, SEQ])
                    stepb = K("steps").unsqueeze(1).to_broadcast([P, SQ, SEQ])
                    step(tt(s5_pt, turns, stepb, ALU.mult))
                    step(ts(s5_S, s5_pt, MAGIC, None, ALU.add, ALU.bypass))
                    step(ts(s5_k, s5_pt, 0.25, MAGIC, ALU.add, ALU.add))
                    fl = lambda a: a.rearrange("p a b -> p (a b)")
                    step(stt(fl(s5_k), fl(s5_k), -MAGIC, fl(s5_pt), ALU.add, ALU.subtract))
                    s5_nf.by(stt(fl(s5_pt), fl(s5_S), -MAGIC, fl(s5_pt), ALU.add, ALU.subtract))
                    s5_tab.wait(v, l, u + 1)
                    for hq in range(2):
                        q = 2 * u + hq
                        Cq = fl(s5_C[:, 2 * hq:2 * hq + 2, :])
                        Sq = fl(s5_S[:, 2 * hq:2 * hq + 2, :])
                        t0, t2, t1, t3 = (pv[:, i, :] for i in range(4))
                        s5_b.wait(v, l, q + 1)
                        if hq:
                            s5_c.wait(v, l, q)
                        two = lambda a: a.rearrange("p (a b) -> p a b", a=2)
                        wr, wi = ps[:, 0:2, 0:SEQ], ps[:, 2:4, 0:SEQ]
                        C3, S3 = s5_C[:, 2 * hq:2 * hq + 2, :], s5_S[:, 2 * hq:2 * hq + 2, :]
                        step(tt(two(t0), wr, C3, ALU.mult))
                        step(tt(two(t1), wi, S3, ALU.mult))
                        step(tt(t0, t0, t1, ALU.add))
                        step(tt(two(t1), wi, C3, ALU.mult))
                        s5_bv.by(tt(two(t2), wr, S3, ALU.mult))
                        s5_bv.wait(v, l, q + 1)
                        step(tt(t1, t1, t2, ALU.subtract))
                        for half in range(2):
                            j = 2 * q + half
                            hs = slice(half * SEQ, (half + 1) * SEQ)
                            a = s5p[:, 2, j:j + 1].to_broadcast([P, SEQ])
                            v.tensor_tensor_scan(t2[:, hs], a, t0[:, hs], 0.0, ALU.mult, ALU.add)
                            step(v.tensor_tensor_scan(t3[:, hs], a, t1[:, hs], 0.0, ALU.mult, ALU.add))
                        step(tt(t0, t2, Cq, ALU.mult))
                        step(tt(t1, t3, Sq, ALU.mult))
                        step(tt(t0, t0, t1, ALU.subtract))
                        step(tt(t1, t2, Sq, ALU.mult))
                        step(tt(t2, t3, Cq, ALU.mult))
                        s5_h.by(tt(t1, t1, t2, ALU.add))
                    s5_c.wait(v, l, 2 * u + 2)
                    o = A_OFF["s_d"][0] + u
                    s5_y.by(stt(mix[:, T_U + u, :], mix[:, T_U + u, :], aux[:, o:o + 1], ps[:, 6, 0:SEQ], ALU.mult, ALU.add))
                glu_z.wait(v, l, 4)
                glu_y.by(tt(mix[:, T_U:T_U + 4, :], mix[:, T_U:T_U + 4, :], S5T[:, 0:4, :], ALU.mult))

                rc = rope_c[:, :].unsqueeze(1).to_broadcast([P, 2, SEQ])
                rs = rope_s[:, :].unsqueeze(1).to_broadcast([P, 2, SEQ])
                rt = rp_t.rearrange("p (a b) -> p a b", a=2)
                for n, t in enumerate(ROPE_TILES):
                    rp_mm.wait(v, l, n + 1)
                    if n:
                        rp_d.wait(v, l, n)
                    step(tt(rt, ps[:, 4 + n % 2, :].rearrange("p (a b) -> p a b", a=2), rs, ALU.mult))
                    step(tt(mix[:, t:t + 2, :], mix[:, t:t + 2, :], rc, ALU.mult))
                    rp_d.by(tt(mix[:, t:t + 2, :], mix[:, t:t + 2, :], rt, ALU.add))
                rp_d.wait(v, l, 7)
                for kv in range(2):
                    for h in range(NKV):
                        x3 = mix[:, (T_KC, T_VC)[kv] + h, :].rearrange("p (n s) -> p s n", s=CS)
                        for hf in range(2):
                            o = A_OFF["cmp_pos"][0] + kv * CB + hf * CS
                            e = aux[:, o:o + CS].unsqueeze(2).to_broadcast([P, CS, NC])
                            b = tt(blk[:, kv, hf * CS:(hf + 1) * CS, h, :], x3[:, :, hf:hf + NC], e, ALU.add)
                    blk_ready.by(b)
                for n, (g, qt, kind) in enumerate(ITEMS):
                    b = 2 * (n % 2)
                    nk = NC if kind == 0 else (qt + 1) * P
                    p3 = pr[:, n % 2, :, 0:nk]
                    st3 = att_s[:, n % 2, :]
                    ns_s.wait(v, l, n + 1)
                    if n >= 2:
                        ns_t.wait(v, l, n - 1)
                    if kind == 0:
                        s3 = ps[:, b, 0:64].rearrange("p (h s) -> p h s", h=GQ)[:, :, 0:NC]
                        m3 = K("cmp_mask", qt * NC, (qt + 1) * NC)
                    else:
                        s3 = ps[:, b:b + 2, :].rearrange("p a (c s) -> p (a c) s", c=2)[:, :, 0:nk]
                        m3 = K("mask", (1 - qt) * P, 2 * P)
                    step(stt(p3, s3, SCALE, m3.unsqueeze(1).to_broadcast([P, GQ, nk]), ALU.mult, ALU.add))
                    ns_m.by(v.tensor_reduce(st3[:, 0:4], p3, AX.X, ALU.max, negate=True))
                    ns_e.wait(v, l, n + 1)
                    step(v.reciprocal(st3[:, 8:12], st3[:, 4:8]))
                    step(tt(st3[:, 8:12], st3[:, 8:12],
                            gates_t[:, qt, :].rearrange("p (h c) -> p h c", c=3)[:, GQ * g:GQ * (g + 1), kind], ALU.mult))
                    w3 = st3[:, 8:12].unsqueeze(2).to_broadcast([P, GQ, nk])
                    if kind == 0:
                        step(tt(p3, p3, w3, ALU.mult))
                        ok = K("cmp_valid", qt * NC, (qt + 1) * NC).unsqueeze(1).to_broadcast([P, GQ, nk])
                        ns_p.by(tt(p3, p3, ok, ALU.mult))
                    else:
                        ns_p.by(tt(p3, p3, w3, ALU.mult))

                cw, cb = A_OFF["m_conv_w"][0], A_OFF["m_conv_b"][0]
                for i in range(8):
                    src = mix[:, T_QK + i, :]
                    dst = m_cv(i)
                    wj = lambda j: aux[:, cw + 4 * i + j:cw + 4 * i + j + 1]
                    step(ts(dst, src, wj(3), aux[:, cb + i:cb + i + 1], ALU.mult, ALU.add))
                    for j in (1, 2, 3):
                        (step if j < 3 else mc_d.by)(
                            stt(dst[:, j:SEQ], src[:, 0:SEQ - j], wj(3 - j), dst[:, j:SEQ], ALU.mult, ALU.add))
                mg_a.wait(v, l, 1)
                step(ts(rows[:, 9, :], rows[:, 1, :], 0.0, None, ALU.min, ALU.bypass))
                step(tt(rows[:, 1, :], rows[:, 9, :], rows[:, 2, :], ALU.subtract))
                for ck in range(2):
                    cs_ = slice(ck * P, (ck + 1) * P)
                    g = v.tensor_tensor_scan(rows[:, 9, cs_], K("ones", p=4), rows[:, 1, cs_], 0.0, ALU.mult, ALU.add)
                step(g)
                mg_d.by(tt(rows[:, 3, :], rows[:, 0, :], rows[:, 9, :], ALU.subtract))
                mg_d.wait(v, l, 1)
                for ck in range(2):
                    cs_ = slice(ck * P, (ck + 1) * P)
                    step(v.tensor_tensor_scan(rows[:, 4, cs_], rows[:, 3, cs_], rows[:, 3, cs_],
                                              rcol[:, 0:1] if ck else 0.0, ALU.max, ALU.max))
                    step(tt(rows[:, 5, cs_], rows[:, 9, cs_], rows[:, 4, cs_], ALU.add))
                    if ck == 0:
                        step(v.tensor_copy(rcol[:, 0:1], rows[:, 5, P - 1:P]))
                mg_d.by(ts(rows[:, 6, :], rows[:, 4, :], -1.0, None, ALU.mult, ALU.bypass))
                for ck in range(2):
                    h4 = range(MH)
                    mb_ev.wait(v, l, 1)
                    (m_kt if ck == 0 else m_qi).wait(v, l, 1)
                    for h in h4:
                        hs = slice(h * P, (h + 1) * P)
                        d = stt(m_dt[ck][:, hs], ps[:, 0, hs], bcol[:, ck, h:h + 1], K("mask_t"), ALU.add, ALU.add)
                    m_dlog.by(d)
                    if ck == 1:
                        m_qib_ready.by(tt(m_qib.rearrange("p (h t) -> p h t", h=MH), mix[:, T_QK:T_QK + 4, P:SEQ],
                                          ps[:, 5, :].rearrange("p (h t) -> p h t", h=MH), ALU.mult))
                    m_exp.wait(v, l, ck + 1)
                    m_sw.by(stt(m_swb[ck], ps[:, 2, :], SCALE, m_dt[ck], ALU.mult, ALU.mult))
                    if ck == 0:
                        for h in h4:
                            hs = slice(h * P, (h + 1) * P)
                            d = ts(m_kwb[:, hs], ps[:, 5, hs], m_dt[0][:, h * P + P - 1:h * P + P], SCALE, ALU.mult, ALU.mult)
                        m_kw.by(d)
                    m_abs.wait(v, l, ck + 1)
                    step(tt(m_e1, m_e1, ps[:, 1, :], ALU.max))
                    step(v.reciprocal(m_e1, m_e1))
                    m_h.by(tt(m_hb, ps[:, 3, :], m_e1, ALU.mult))
                    m_rs.wait(v, l, ck + 1)
                    step(v.reciprocal(m_e2, m_e2))
                    step(tt(m_hb, m_hb, m_e2, ALU.mult))
                    m_sig.wait(v, l, 1)
                    for h in h4:
                        o = A_OFF["m_norm_g"][0] + h
                        yt = mix[:, T_O + h, ck * P:(ck + 1) * P]
                        d = stt(yt, m_hb[:, h * P:(h + 1) * P], aux[:, o:o + 1], yt, ALU.mult, ALU.mult)
                    m_out.by(d)

                residual(0)
                norm_in(1, "g_pre_ffn")

                wo, bo = A_OFF["f_conv_w"][0], A_OFF["f_conv_b"][0]

                def conv(i, k):
                    t = i * 5 + k
                    v.wait_ge(w_used, l * CHUNKS + i * 10 + (C_UP + 2 * k + 2))
                    if isinstance(t, int):
                        g, w, b = mix[:, t, :], aux[:, wo + 3 * t:wo + 3 * t + 3], aux[:, bo + t:bo + t + 1]
                    else:
                        g = mix[:, bass.ds(t, 1), :].rearrange("p a b -> p (a b)")
                        w = aux[:, bass.ds(t * 3 + wo, 3)]
                        b = aux[:, bass.ds(t + bo, 1)]
                    a = ps[:, k, 0:SEQ]
                    n0 = (l * FT + i * 5 + k) * 3
                    ts(g, a, w[:, 2:3], b, ALU.mult, ALU.add).then_inc(ff_conv, 1)
                    for j in (1, 2):
                        v.wait_ge(ff_conv, n0 + j)
                        stt(g[:, j:SEQ], a[:, 0:SEQ - j], w[:, 2 - j:3 - j], g[:, j:SEQ], ALU.mult,
                            ALU.add).then_inc(ff_conv, 1)

                def gated(i, k):
                    t = i * 5 + k
                    g = mix[:, t, :] if isinstance(t, int) else mix[:, bass.ds(t, 1), :].rearrange("p a b -> p (a b)")
                    v.wait_ge(ff_gelu, l * FT + i * 5 + k + 1)
                    tt(g, g, ps[:, k, SEQ:2 * SEQ], ALU.mult).then_inc(ff_mul, 1)

                def up(i, n, u=None):
                    for k in range(n):
                        conv(i, k)
                        if k:
                            gated(i, k - 1)
                        if u is not None:
                            for j in range(2 * k, min(2 * k + 2, UCH)):
                                ada_chunk(u, j)
                    gated(i, n - 1)
                    if u is not None:
                        ada_finish(u, modf[:, bass.ds(i * UG, UG)])

                with v.Fori(0, 2) as i:
                    up(i, 5, l * UNITS + 10 + i)
                with v.Fori(2, 6) as i:
                    up(i, 5)
                    with v.If(l < DEPTH - 1):
                        u = l * UNITS + 10 + i
                        for j in range(UCH):
                            ada_chunk(u, j)
                        ada_finish(u, modf[:, bass.ds(i * UG, UG)])
                with v.Fori(6, 8) as i:
                    up(i, 5)
                up(8, 3)
                v.wait_ge(mod_ready, l * UNITS + 12)
                gate_gain(1, "g_post_ffn")
                residual(1)

        wrong = [(str(sg.sem), sg.given, sg.per_layer) for sg in every if sg.given != sg.per_layer]
        assert not wrong, wrong


ROPE_TILES = [T_Q, T_Q + 2, T_Q + 4, T_Q + 6, T_KC, T_KS, T_KW]
ROPE_STEPS = (8, 12)
DVE_STEPS, ACT_STEPS = 247, 2



def _columns(a, n):
    return a.reshape(a.shape[0], n, P).transpose(0, 2, 1)


def _weights(i):
    out = np.empty((DEPTH, CHUNKS, P, CH), np.float32)

    def columns(w, c0, n):
        return w[:, :, c0:c0 + n * P].reshape(DEPTH, KT, P, n, P).transpose(0, 3, 2, 1, 4).reshape(DEPTH, n, P, CH)

    w_in = i["w_in"]
    at = 0
    for c0, n in ((2056, 4), (2568, 8), (3592, 12), (0, 8), (1024, 4), (1536, 4)):
        out[:, at:at + n] = columns(w_in, c0, n)
        at += n
    out[:, C_GLU] = i["s_w_glu"].reshape(DEPTH, 4, P, 512).transpose(0, 2, 1, 3).reshape(DEPTH, P, CH)
    out[:, C_CMP:C_CMP + 4] = i["n_cmp_w1"].reshape(DEPTH, 4, 16, P, P).transpose(0, 1, 3, 2, 4).reshape(DEPTH, 4, P, CH)
    out[:, C_OUT:C_OUT + KT] = i["w_out"].reshape(DEPTH, KT, P, D)
    out[:, C_UP:C_DOWN:2] = columns(i["f_w_up"], 0, FT)
    out[:, C_UP + 1:C_DOWN:2] = columns(i["f_w_up"], DFF, FT)
    out[:, C_DOWN:] = i["f_w_down"].reshape(DEPTH, FT, P, D)
    return out.reshape(DEPTH * CHUNKS, P, CH)


def _params(i):
    out = np.zeros((DEPTH, P, A_W), np.float32)

    def put(name, a):
        o, w = A_OFF[name]
        out[:, :a.shape[1], o:o + w] = a.reshape(DEPTH, a.shape[1], w)

    for n in ("g_pre_mix", "g_post_mix", "g_pre_ffn", "g_post_ffn"):
        put(n, _columns(i[n], KT))
    put("m_conv_w", i["m_conv_w"].reshape(DEPTH, 4, 8, P).transpose(0, 3, 2, 1))
    put("m_conv_b", _columns(i["m_conv_b"], 8))
    put("m_norm_g", i["m_norm_g"].transpose(0, 2, 1))
    put("s_d", _columns(i["s_d"], 4))
    put("s_b_glu", _columns(i["s_b_glu"], 4))
    for n in ("lam_re", "lam_im"):
        put(n, i["s_" + n].reshape(DEPTH, ST, P).transpose(0, 2, 1))
    put("log_dt", np.repeat(i["s_log_dt"].reshape(DEPTH, ST, 2).transpose(0, 2, 1), S_STATE, axis=1))
    put("f_conv_w", i["f_conv_w"].reshape(DEPTH, 3, FT, P).transpose(0, 3, 2, 1))
    put("f_conv_b", _columns(i["f_conv_b"], FT))
    put("i_bias", i["m_i_bias"].reshape(DEPTH, 4, 1))
    put("f_bias", i["m_f_bias"].reshape(DEPTH, 4, 1))
    put("cmp_pos", i["n_cmp_pos"].transpose(0, 3, 1, 2))
    w = i["w_in"].reshape(DEPTH, KT, P, -1).transpose(0, 2, 1, 3)
    put("w_gates", np.concatenate([w[..., 2048:2056], w[..., 5128:5152]], axis=3))
    put("cmp_w2", i["n_cmp_w2"].transpose(0, 2, 1, 3))
    for part in ("re", "im"):
        ob, oc = A_OFF["s_b_" + part][0], A_OFF["s_c_" + part][0]
        for g in range(S_GROUPS):
            j, hb = g // 2, g % 2
            r, c = SC * (j % SQ) + S_GROUP * hb, ob + P * (j // SQ) + S_STATE * hb
            out[:, r:r + S_GROUP, c:c + S_STATE] = i["s_b_" + part][:, g].transpose(0, 2, 1)
            c = oc + SC * j + S_GROUP * hb
            out[:, S_STATE * hb:S_STATE * (hb + 1), c:c + S_GROUP] = i["s_c_" + part][:, g].transpose(0, 2, 1)
    return out


def _constants():
    out = np.zeros((P, K_W), np.float32)

    def put(name, a, rows=P):
        o, w = K_OFF[name]
        out[:rows, o:o + w] = np.asarray(a).reshape(rows, w)

    r = np.arange(P)
    put("ident", np.eye(P))
    put("ones", np.ones((P, P)))
    rot = np.zeros((P, P))
    rot[r[64:], r[:64]] = -1.0
    rot[r[:64], r[64:]] = 1.0
    put("rot", rot)
    put("mask", np.concatenate([np.zeros((P, P)), np.where(r[None] <= r[:, None], 0.0, NEG)], 1))
    put("mask_t", np.where(r[:, None] <= r[None], 0.0, NEG))
    t = r[:, None, None] + P * np.arange(TT)[None, :, None]
    ok = CS * np.arange(NC)[None, None] + CB - 1 <= t
    put("cmp_mask", np.where(ok, 0.0, NEG))
    put("cmp_valid", ok * 1.0)
    put("sel", (np.arange(MH)[:, None, None] == np.arange(MH)[None, :, None]) * np.ones((1, 1, P)), MH)
    put("steps", np.broadcast_to(np.arange(SEQ), (P, SEQ)))
    put("inv_freq", np.float32(10000.0) ** (-(r % 64).astype(np.float32) / np.float32(64)))
    put("half_pi", np.full(P, TWO_PI / 4))
    put("eps", np.full(P, EPS))
    return out


def kernel(**inputs):
    import concourse.bacc as bacc
    from concourse.bass_utils import run_bass_kernel_spmd

    i = {k: np.asarray(v) for k, v in inputs.items()}
    ada = i["w_ada"].reshape(DEPTH, UCH, 2, P, UNITS, UC).transpose(0, 4, 1, 3, 2, 5)
    arrays = {
        "x": i["x"],
        "c_cols": i["c"].reshape(KT, P).T,
        "pos": np.broadcast_to(i["positions"], (P, SEQ)),
        "consts": _constants(),
        "aux_d": _params(i),
        "ada_d": ada.reshape(DEPTH * UNITS * UCH, P, 2 * UC),
        "ada_b": i["b_ada"].reshape(DEPTH * UNITS, UC),
        "stream": _weights(i),
    }
    arrays = {k: np.ascontiguousarray(a) for k, a in arrays.items()}
    nc = bacc.Bacc("TRN2", target_bir_lowering=False, num_devices=1)
    args = [nc.dram_tensor(k, a.shape, mybir.dt.from_np(a.dtype), kind="ExternalInput").ap() for k, a in arrays.items()]
    args.append(nc.dram_tensor("out", (1, SEQ, D), F32, kind="ExternalOutput").ap())
    trunk(nc, *args)
    r = run_bass_kernel_spmd(nc, [arrays], core_ids=[0])
    return r.results[0]["out"]
```

```python
import numpy as np
import concourse.bass as bass
from concourse import mybir
from concourse.alu_op_type import AluOpType as ALU
from contextlib import ExitStack

F32 = mybir.dt.float32
F32R = mybir.dt.float32r
I32 = mybir.dt.int32
ACT = mybir.ActivationFunctionType
AX = mybir.AxisListType

P = 128
D, SEQ, DEPTH = 2048, 256, 2
EPS = 1e-6
KT = D // P
TT = SEQ // P
HD = 128
MH = 4
S_GROUPS, S_STATE, S_GROUP = 32, 64, 16
ST = S_GROUPS * S_STATE // P
UT = S_GROUPS * S_GROUP // P
SQ = ST // UT
SC = 2 * S_GROUP
NH, NKV = 8, 2
GQ = NH // NKV
CB, CS = 32, 16
NC = SEQ // CS - 1
DFF = ((8 * D // 3 + 127) // 128) * 128
FT = DFF // P
SCALE = float(HD) ** -0.5
NEG = -1e30
TWO_PI = 6.283185307179586
TURN = 1.0 / TWO_PI
MAGIC = 12582912.0
PI_1, PI_2 = 6.28125, 0.0019350051879882812
PI_3 = TWO_PI - PI_1 - PI_2
PI_IN = 3.1415925
TWO_PI_IN = 6.283185

CH = KT * P // 2
KH = KT // 2
RING = 5
SPLIT = 4
AHEAD = SPLIT
C_IN = 0
C_GATES = 80
C_CMP = 82
N_CMP = 8
C_OUT = C_CMP + N_CMP
C_UP = C_OUT + 2 * KT
C_DOWN = C_UP + 4 * FT
CHUNKS = C_DOWN + 2 * FT
NSPLIT = CHUNKS - N_CMP
BODY = 20
assert CHUNKS % RING == 0 and CHUNKS % SPLIT == 0 and BODY % RING == 0 and BODY % SPLIT == 0
CYCLES = CHUNKS // RING
G_I, G_F, G_N = 0, 32, 64
NXS = KT + FT
FREE = 5

T_O, T_U, T_Q, T_KV, T_QK, T_V = 0, 4, 8, 16, 28, 36
NPROJ = 40
T_KC, T_VC, T_KS, T_VS, T_KW, T_VW = (T_KV + 2 * j for j in range(6))
W_S5 = NPROJ
NMIX = 56

UC = 1024
UNITS = 6 * D // UC
UG = UC // P
UCH = KT
ASLOT = 4

A_OFF, _o = {}, 0
for _name, _w in (("g_pre_mix", KT), ("g_post_mix", KT), ("g_pre_ffn", KT), ("g_post_ffn", KT), ("m_conv_w", 32),
                  ("m_conv_b", 8), ("m_norm_g", 4), ("s_d", 4), ("s_b_glu", 4), ("lam_re", ST), ("lam_im", ST),
                  ("log_dt", ST), ("f_conv_w", 3 * FT), ("f_conv_b", FT), ("i_bias", 1), ("f_bias", 1),
                  ("cmp_pos", 2 * CB), ("s_b_re", UT * P), ("s_b_im", UT * P), ("s_c_re", ST * SC),
                  ("s_c_im", ST * SC), ("cmp_w2", 2 * P)):
    A_OFF[_name] = (_o, _w)
    _o += _w
A_W = _o
K_OFF, _o = {}, 0
for _name, _w in (("ident", P), ("ones", P), ("rot", P), ("mask", 2 * P), ("mask_t", P), ("cmp_mask", TT * NC),
                  ("cmp_valid", TT * NC), ("sel", MH * P), ("steps", SEQ), ("inv_freq", 1), ("half_pi", 1), ("eps", 1)):
    K_OFF[_name] = (_o, _w)
    _o += _w
K_W = _o


def trunk(nc, x, c_cols, pos, consts, aux_d, ada_d, ada_b, glu_d, stream, out):
    with ExitStack() as ctx:
        def sb(name, shape, dt=F32):
            return ctx.enter_context(nc.sbuf_tensor(name, shape, dt))

        xs = sb("xs", [P, TT, D])
        hs = sb("hs", [P, 2 * KT * SEQ])
        at = nc.sbuf_base - 2 * KT * SEQ * 4
        hT_hi = nc.alloc_sbuf_tensor_at("hT_hi", [P, KT, SEQ], F32R, offset=at, align_bytes=32)
        hT_lo = nc.alloc_sbuf_tensor_at("hT_lo", [P, KT, SEQ], F32R, offset=at + KT * SEQ * 4,
                                        align_bytes=32)
        mix = sb("mix", [P, NMIX, SEQ])
        ring = sb("ring", [P, RING, CH])
        w_hi = sb("w_hi", [P, SPLIT, CH], F32R)
        w_lo = sb("w_lo", [P, SPLIT, CH], F32R)
        x_hi = sb("x_hi", [P, 2, SEQ], F32R)
        x_lo = sb("x_lo", [P, 2, SEQ], F32R)
        ada_w = sb("ada_w", [P, ASLOT, UC])
        ada_acc = sb("ada_acc", [P, UC])
        gt_row = hs[:, 3 * D:4 * D]
        aux = sb("aux", [P, A_W])
        cst = sb("cst", [P, K_W])
        posi = sb("posi", [P, SEQ], I32)
        rope_c = sb("rope_c", [P, SEQ])
        rope_s = sb("rope_s", [P, SEQ])
        mod = sb("mod", [P, 3, KT])
        modA = sb("modA", [P, KT])
        gg = sb("gg", [P, KT])
        cs = sb("cs", [P, KT])
        craw = sb("craw", [P, KT])
        stat = sb("stat", [P, 8])
        s5p = sb("s5p", [P, 20, ST])
        gates_t = sb("gates_t", [P, TT, 3 * NH])
        rows = hs[0:MH, 2 * D:3 * D].rearrange("p (r s) -> p r s", r=8)
        rcol = sb("rcol", [4, 4])
        bcol = sb("bcol", [P, 2, MH])
        att_s = sb("att_s", [P, 2, 16])
        sg24 = sb("sg24", [3 * NH, SEQ])
        ps = ctx.enter_context(nc.psum_tensor("ps", [P, 8, 512], F32))

        def A(name, a=None, b=None, p=P):
            o, w = A_OFF[name]
            return aux[0:p, o + (a or 0):o + (w if b is None else b)]

        def K(name, a=None, b=None, p=P):
            o, w = K_OFF[name]
            return cst[0:p, o + (a or 0):o + (w if b is None else b)]

        ident, ones = K("ident"), K("ones")

        class Signal:
            def __init__(self, name, per_layer=None):
                self.sem = ctx.enter_context(nc.semaphore(name))
                self.per_layer = per_layer
                self.given = 0

            def by(self, ins, n=1):
                self.given += n
                ins.then_inc(self.sem, n)
                return ins

            def wait(self, eng, l, k):
                eng.wait_ge(self.sem, l * self.per_layer + k)

            def chain(self, eng, l, ins):
                self.by(ins)
                self.wait(eng, l, self.given)


        def sem(name):
            return ctx.enter_context(nc.semaphore(name))

        cst_in, x_in, c_in, pos_in = sem("cst_in"), sem("x_in"), sem("c_in"), sem("pos_in")
        aux_in = sem("aux_in")
        ring_full = [sem(f"ring_full{s}") for s in range(RING)]
        ada_full = [sem(f"ada_full{s}") for s in range(ASLOT)]
        glu_in = sem("glu_in")
        out_done = sem("out_done")
        w_used = sem("w_used")
        hi_ready = sem("hi_ready")
        raw_free = sem("raw_free")
        xhi_ready, xlo_ready = sem("xhi_ready"), sem("xlo_ready")
        acc_zero, acc_bias = sem("acc_zero"), sem("acc_bias")
        ada_step = sem("ada_step")
        ada_red = sem("ada_red")
        mod_ready = sem("mod_ready")
        cs_ready, rope_dve, rope_act = sem("cs_ready"), sem("rope_dve"), sem("rope_act")
        rms_act = Signal("rms_act", 8)
        rstd = Signal("rstd", 8)
        dve = Signal("dve", DVE_STEPS)
        act = Signal("act", ACT_STEPS)
        x_ready = Signal("x_ready", 4)
        xn_ready = Signal("xn_ready", 4)
        h_tr = Signal("h_tr", 16)
        modA_ready = Signal("modA_ready", 2)
        h_hi = Signal("h_hi", 2 * KT)
        h_tmp = Signal("h_tmp", 16)
        h_lo = Signal("h_lo", 16)
        gg_ready = Signal("gg_ready", 2)
        gt_mm = Signal("gt_mm", 2)
        gt_ready = Signal("gt_ready", 2)
        in_ev = sem("in_ev")
        gate_ev = Signal("gate_ev", 3)
        s5_pd, s5_pa = Signal("s5_pd", 5), Signal("s5_pa", 4)
        s5_nf = Signal("s5_nf", UT)
        s5_tab = Signal("s5_tab", UT)
        s5_b = Signal("s5_b", ST // 2)
        s5_h = Signal("s5_h", ST // 2)
        s5_bv = Signal("s5_bv", ST // 2)
        s5_c = Signal("s5_c", ST // 2)
        s5_y = Signal("s5_y", UT)
        s5_g = Signal("s5_g", UT)
        glu_mm, glu_z, glu_y = Signal("glu_mm", 2), Signal("glu_z", 4), Signal("glu_y", 1)
        rp_mm, rp_d = Signal("rp_mm", 7), Signal("rp_d", 7)
        vt_mm, vt_ev = Signal("vt_mm", 5), Signal("vt_ev", 5)
        blk_ready = Signal("blk_ready", 2)
        ch_g, cc_mm, cc_ev = Signal("ch_g", 2), Signal("cc_mm", 1), Signal("cc_ev", 2)
        ITEMS = [(g, qt, kind) for g in range(NKV) for qt in range(TT) for kind in range(3)]
        NI = len(ITEMS)
        ns_s, ns_m, ns_e, ns_p = (Signal(n, NI) for n in ("ns_s", "ns_m", "ns_e", "ns_p"))
        ns_t, ns_pt, ns_o = (Signal(n, NI) for n in ("ns_t", "ns_pt", "ns_o"))
        ns_y = Signal("ns_y", NKV * TT)
        mc_d, mc_a = Signal("mc_d", 8), Signal("mc_a", 8)
        mg_a, mg_d = Signal("mg_a", 1), Signal("mg_d", 2)
        mb_mm, mb_ev = Signal("mb_mm", 1), Signal("mb_ev", 1)
        m_row = Signal("m_row", 2)
        m_dlog, m_exp = Signal("m_dlog", 2), Signal("m_exp", 2)
        m_sw, m_kw, m_kt, m_qi = Signal("m_sw", 2), Signal("m_kw", 1), Signal("m_kt", 1), Signal("m_qi", 1)
        m_c, m_cev = Signal("m_c", 1), Signal("m_cev", 2)
        m_num, m_abs, m_h, m_ss, m_rs, m_out = (Signal(n, 2) for n in ("m_num", "m_abs", "m_h", "m_ss", "m_rs", "m_out"))
        m_sig, m_qib_ready = Signal("m_sig", 1), Signal("m_qib_ready", 1)
        m_hsq = Signal("m_hsq", 2)
        ff_tap, ff_conv, ff_gelu, ff_mul = sem("ff_tap"), sem("ff_conv"), sem("ff_gelu"), sem("ff_mul")

        every = [v for v in list(locals().values()) if isinstance(v, Signal)]
        S5T = mix[:, W_S5:W_S5 + 16, :]
        s5_pt = S5T[:, 0:4, :]
        s5_k = S5T[:, 4:8, :]
        s5_S = S5T[:, 8:12, :]
        s5_C = S5T[:, 12:16, :]
        SP5 = lambda i: s5p[:, i, :]
        xn = mix[:, 0:KT, :].rearrange("p a b -> p (a b)").rearrange("p (t d) -> p t d", t=TT)
        hflat = hs[:, 0:2 * D]
        h_t = mix[:, KT:2 * KT, :]
        junk = h_t.rearrange("p a b -> p (a b)").rearrange("p (t d) -> p t d", t=TT)
        glu_w = hs[:, 0:D]
        mflat = mix[:, :, :].rearrange("p a b -> p (a b)")

        def mtile(t):
            return mix[:, t, :] if isinstance(t, int) else mix[:, bass.ds(t, 1), :].rearrange("p a b -> p (a b)")
        psf = ps[:, :, :].rearrange("p a b -> p (a b)")

        pr = hflat[:, 0:2048].rearrange("p (b h s) -> p b h s", b=2, h=GQ)
        pt = hflat[:, 2048:3072].rearrange("p (s n) -> p s n", s=2)
        vtok = S5T[:, 0:4, :].rearrange("p a b -> p (a b)").rearrange("p (a h s e) -> p a h s e", a=2, h=2, s=2)
        blk = S5T[:, 4:12, :].rearrange("p a b -> p (a b)")[:, 0:2 * CB * 2 * NC].rearrange(
            "p (v s h j) -> p v s h j", v=2, s=CB, h=2)
        hid = hflat[:, 3072:3072 + 60].rearrange("p (v n) -> p v n", v=2)
        kcT = hflat[:, 3136:3136 + 30]
        vct = hflat[0:NC, 3200:3200 + 256].rearrange("p (h e) -> p h e", h=2)
        rp_t = hflat[:, 3584:4096]
        vm = S5T[:, 12:16, :].rearrange("p a b -> p (a b)").rearrange("p (c h e) -> p c h e", c=2, h=MH)
        def m_buf(i):
            return S5T[:, 2 * i:2 * i + 2, :].rearrange("p a b -> p (a b)")
        m_dt = [hflat[:, 512 * i:512 * i + 512] for i in range(2)]
        m_swb = [hflat[:, 1024 + 512 * i:1536 + 512 * i] for i in range(2)]
        m_kwb, m_C, m_n, m_qib = (hflat[:, 2048 + 512 * i:2560 + 512 * i] for i in range(4))
        def m_cv(i):
            return S5T[:, 4 + i, :]
        m_hb, m_tb = m_buf(0), m_buf(1)
        m_e1, m_e2 = m_buf(2), m_buf(3)

        block = ctx.enter_context(nc.Block())

        @block.sync
        def _(sp):
            sp.dma_start(cst[:, :], consts[:, :]).then_inc(cst_in, 16)
            sp.dma_start(xs[:, :, :], x.rearrange("b (t p) d -> p (b t) d", p=P)).then_inc(x_in, 16)
            for s in range(RING):
                sp.dma_start(ring[:, s, :], stream[s, :, :]).then_inc(ring_full[s], 16)
            with sp.Fori(1, DEPTH * CYCLES) as cyc:
                for s in range(RING):
                    at = sp.snap(cyc * RING + s)
                    sp.wait_ge(raw_free, cyc * RING + (s - RING + 1))
                    sp.dma_start(ring[:, s, :], stream[bass.ds(at, 1), :, :].rearrange("a p n -> p (a n)")
                                 ).then_inc(ring_full[s], 16)
            x_ready.wait(sp, DEPTH - 1, 4)
            sp.dma_start(out.rearrange("b (t p) d -> p (b t) d", p=P), xs[:, :, :]).then_inc(out_done, 16)
            sp.wait_ge(out_done, 16)

        @block.gpsimd
        def _(pool):
            def wait(sem_, value):
                value = value if isinstance(value, int) else pool.to_reg(value)
                pool.wait_ge(c_in, 16)
                pool.wait_ge(sem_, value)

            def unit(u, first=False):
                if not first:
                    u = nc.s_assert_within(u, 0, DEPTH * UNITS - 1)
                    wait(ada_red, u)
                pool.memset(ada_acc[:, :], 0.0).then_inc(acc_zero, 1)
                wait(acc_zero, u + 1)
                pool.dma_start(ada_acc[0:1, :], ada_b[bass.ds(u, 1), :]).then_inc(acc_bias, 16)
                for j in range(UCH):
                    s = j % ASLOT
                    if not (first and j < ASLOT):
                        wait(ada_step, UCH * u + (j - ASLOT + 1))
                    pool.dma_start(ada_w[:, s, :],
                                   ada_d[bass.ds(u * UCH + j, 1), :, :].rearrange("a p n -> p (a n)")).then_inc(ada_full[s], 16)

            pool.dma_start(craw[:, :], c_cols[:, :]).then_inc(c_in, 16)
            pool.dma_start(posi[:, :], pos[:, :]).then_inc(pos_in, 16)
            pool.dma_start(aux[:, :], aux_d[0, :, :]).then_inc(aux_in, 16)
            unit(0, first=True)
            with pool.Fori(1, 4) as i:
                unit(i)
            with pool.Fori(0, DEPTH) as l:
                with pool.Fori(0, 6) as i:
                    unit(l * UNITS + 4 + i)
                wait(w_used, l * CHUNKS + C_CMP)
                pool.dma_start(glu_w, glu_d[bass.ds(l, 1), :, :].rearrange("a p n -> p (a n)")).then_inc(glu_in, 16)
                with pool.Fori(0, 2) as i:
                    unit(l * UNITS + 10 + i)
                with pool.If(l < DEPTH - 1):
                    with pool.Fori(2, 6) as i:
                        unit(l * UNITS + 10 + i)
                    nxt = nc.s_assert_within(l + 1, 1, DEPTH - 1)
                    wait(w_used, l * CHUNKS + C_DOWN + 1)
                    pool.dma_start(aux[:, :], aux_d[bass.ds(nxt, 1), :, :].rearrange("a p n -> p (a n)")
                                   ).then_inc(aux_in, 16)

        @block.tensor
        def _(pe):
            def full(c, cyc):
                pe.wait_ge(ring_full[c % RING], cyc * 16 + 16)

            def split_ready(n):
                pe.wait_ge(raw_free, n + 1)

            def reduce_unit(u):
                pe.wait_ge(ada_step, u * UCH + UCH)
                for k in range(UG):
                    m = pe.matmul(ps[:, 7, k:k + 1], ada_acc[:, k * P:(k + 1) * P], ones[:, 0:1], start=True, stop=True)
                m.then_inc(ada_red, 1)

            def norm_transposes(l, n):
                xn_ready.wait(pe, l, 2 * n + 2)
                for b in range(8):
                    for k in range(2):
                        for t in range(TT):
                            m = pe.transpose(ps[:, b, k * SEQ + t * P:k * SEQ + (t + 1) * P],
                                             xn[:, t, (2 * b + k) * P:(2 * b + k + 1) * P], ident)
                    h_tr.by(m)

            def proj(n, c, bank, col=0, wait_ev=None, h_part=None):
                for half in range(2):
                    split_ready(n + half)
                    if wait_ev is not None and half == 0:
                        pe.wait_ge(*wait_ev)
                    if h_part is not None:
                        h_part(half)
                    s = (c + half) % SPLIT
                    for kk in range(KH):
                        k = half * KH + kk
                        ks = slice(kk * P, (kk + 1) * P)
                        for p, (w, h) in enumerate(((w_hi, hT_hi), (w_hi, hT_lo), (w_lo, hT_hi))):
                            m = pe.matmul(ps[:, bank, col:col + SEQ], w[:, s, ks], h[:, k, :],
                                          start=k == 0 and p == 0, stop=k == KT - 1 and p == 2)
                    m.then_inc(w_used, 1)

            def gate_rows(l, n):
                gg_ready.wait(pe, l, n + 1)
                for k in range(KT):
                    m = pe.matmul(ps[:, k // 4, (k % 4) * P:(k % 4 + 1) * P], gg[:, k:k + 1].to_broadcast([P, P]),
                                  ident, start=True, stop=True)
                gt_mm.by(m)

            def to_tokens(n, x0, c, k, last):
                xs_ = k % 2
                pe.wait_ge(xlo_ready, x0 + 1)
                for half in range(2):
                    split_ready(n + half)
                    s = (c + half) % SPLIT
                    for t in range(TT):
                        ts_ = slice(t * P, (t + 1) * P)
                        for p, (xx, w) in enumerate(((x_hi, w_hi), (x_hi, w_lo), (x_lo, w_hi))):
                            for b in range(2):
                                m = pe.matmul(ps[:, 4 * t + 2 * half + b, :], xx[:, xs_, ts_], w[:, s, b * 512:(b + 1) * 512],
                                              start=k == 0 and p == 0, stop=last and p == 2)
                    m.then_inc(w_used, 1)

            pe.wait_ge(cst_in, 16)
            reduce_unit(0)
            with pe.Fori(1, 4) as i:
                reduce_unit(i)

            with pe.Fori(0, DEPTH) as l:
                norm_transposes(l, 0)
                with pe.Fori(0, 2) as i:
                    for s in range(BODY):
                        c = 2 * s
                        hp = (lambda half: h_lo.wait(pe, l, 4 + 4 * half)) if s == 0 else None
                        proj(l * CHUNKS + i * (2 * BODY) + c, c, s % 5, 0,
                             (in_ev, l * (FREE + NPROJ) + i * BODY + (s + 1)), hp)
                        if s in ADA_IN_PE:
                            reduce_unit(l * UNITS + i * 3 + (4 + ADA_IN_PE.index(s)))
                proj(l * CHUNKS + C_GATES, C_GATES, 5)
                pe.wait_ge(in_ev, (l + 1) * (FREE + NPROJ))
                gate_rows(l, 0)

                s5_pd.wait(pe, l, 5)
                gate_ev.wait(pe, l, 3)
                for q in range(ST // 2):
                    ut = q // 2
                    if q >= 1:
                        s5_bv.wait(pe, l, q)
                    else:
                        gt_ready.wait(pe, l, 1)
                    for part, name in ((0, "s_b_re"), (1, "s_b_im")):
                        for half in range(2):
                            r = SC * (2 * (q % 2) + half)
                            o = A_OFF[name][0] + ut * P
                            m = pe.matmul(ps[:, 2 * part + half, 0:SEQ], aux[r:r + SC, o:o + P],
                                          mix[r:r + SC, T_U + ut, :], start=True, stop=True)
                    s5_b.by(m)
                    s5_h.wait(pe, l, q + 1)
                    if q % 2 == 0 and ut >= 1:
                        s5_y.wait(pe, l, ut)
                    for half in range(2):
                        j = 2 * q + half
                        r = SC * (j % SQ)
                        for part, name in ((0, "s_c_re"), (1, "s_c_im")):
                            o = A_OFF[name][0] + j * SC
                            hh = s5_pt if part == 0 else s5_k
                            m = pe.matmul(ps[r:r + SC, 6, 0:SEQ], aux[:, o:o + SC], hh[:, half, :],
                                          start=part == 0, stop=part == 1)
                    s5_c.by(m)
                pe.wait_ge(glu_in, l * 16 + 16)
                s5_g.wait(pe, l, UT)
                for n in range(4):
                    for k in range(4):
                        m = pe.matmul(ps[:, n // 2, (n % 2) * SEQ:(n % 2 + 1) * SEQ],
                                      glu_w[:, k * 512 + n * P:k * 512 + (n + 1) * P],
                                      mix[:, T_U + k, :], start=k == 0, stop=k == 3)
                    if n % 2:
                        glu_mm.by(m)

                for n, t in enumerate(ROPE_TILES):
                    if n >= 2:
                        rp_d.wait(pe, l, n - 1)
                    m = pe.matmul(ps[:, 4 + n % 2, :], K("rot"), mix[:, t:t + 2, :], start=True, stop=True)
                    rp_mm.by(m)
                glu_z.wait(pe, l, 4)
                for a, t0 in enumerate((T_VS, T_VW)):
                    for h in range(2):
                        for s in range(2):
                            m = pe.transpose(ps[:, a, (2 * h + s) * P:(2 * h + s + 1) * P],
                                             mix[:, t0 + h, s * P:(s + 1) * P], ident)
                    vt_mm.by(m)
                for ck in range(2):
                    for h in range(MH):
                        m = pe.transpose(ps[:, 2 + ck, h * P:(h + 1) * P], mix[:, T_V + h, ck * P:(ck + 1) * P], ident)
                    vt_mm.by(m)
                pe.wait_ge(cst_in, 16)
                s5_y.wait(pe, l, UT)
                for t in range(TT):
                    m = pe.transpose(ps[:, 6, 32 * t:32 * t + 24], sg24[:, t * P:(t + 1) * P], K("ident", 0, 24, 24))
                vt_mm.by(m)
                for v in range(2):
                    blk_ready.wait(pe, l, v + 1)
                    for qr in range(4):
                        c = C_CMP + 4 * v + qr
                        full(c, l * CYCLES + c // RING)
                        for j in range(8):
                            pos_i = 8 * qr + j
                            m = pe.matmul(ps[:, 7, 64 * v:64 * v + 30], ring[:, c % RING, j * P:(j + 1) * P],
                                          blk[:, v, pos_i, :, :], start=pos_i == 0, stop=pos_i == CB - 1)
                        m.then_inc(w_used, 1)
                ch_g.wait(pe, l, 2)
                w2o = A_OFF["cmp_w2"][0]
                pe.matmul(ps[:, 7, 128:158], aux[:, w2o:w2o + P], hid[:, 0, :], start=True, stop=True)
                for h in range(NKV):
                    m = pe.matmul(ps[0:NC, 7, 256 + h * P:384 + h * P], hid[:, 1, h * NC:(h + 1) * NC],
                                  aux[:, w2o + P:w2o + 2 * P], start=True, stop=True)
                cc_mm.by(m)

                def scores(n):
                    g, qt, kind = ITEMS[n]
                    if n >= 2:
                        ns_m.wait(pe, l, n - 1)
                    b = 2 * (n % 2)
                    for h in range(GQ):
                        q = mix[:, T_Q + GQ * g + h, qt * P:(qt + 1) * P]
                        if kind == 0:
                            m = pe.matmul(ps[:, b, h * 16:h * 16 + NC], q, kcT[:, g * NC:(g + 1) * NC],
                                          start=True, stop=True)
                        else:
                            kt = (T_KS if kind == 1 else T_KW) + g
                            nk = (qt + 1) * P
                            m = pe.matmul(ps[:, b + h // 2, (h % 2) * SEQ:(h % 2) * SEQ + nk], q, mix[:, kt, 0:nk],
                                          start=True, stop=True)
                    ns_s.by(m)

                rp_d.wait(pe, l, 7)
                cc_ev.wait(pe, l, 2)
                vt_ev.wait(pe, l, 5)
                scores(0)
                for n, (g, qt, kind) in enumerate(ITEMS):
                    if n + 1 < NI:
                        scores(n + 1)
                    ns_p.wait(pe, l, n + 1)
                    if n >= 1:
                        ns_pt.wait(pe, l, n)
                    nst = 1 if kind == 0 else qt + 1
                    for s in range(nst):
                        for h in range(GQ):
                            if kind == 0:
                                m = pe.transpose(ps[0:NC, 4, h * P:(h + 1) * P], pr[:, n % 2, h, 0:NC], ident)
                            else:
                                m = pe.transpose(ps[:, 4 + s, h * P:(h + 1) * P], pr[:, n % 2, h, s * P:(s + 1) * P], ident)
                    ns_t.by(m)
                    ns_pt.wait(pe, l, n + 1)
                    if kind == 0 and n >= 3:
                        ns_y.wait(pe, l, n // 3)
                    if kind == 0:
                        m = pe.matmul(ps[:, 6, :], vct[:, g, :], pt[0:NC, 0, :], start=True, stop=False)
                    else:
                        for s in range(nst):
                            m = pe.matmul(ps[:, 6, :], vtok[:, kind - 1, g, s, :], pt[:, s, :], start=False,
                                          stop=kind == 2 and s == nst - 1)
                    ns_o.by(m)

                pe.wait_ge(cst_in, 16)
                mg_d.wait(pe, l, 1)
                for ck in range(2):
                    m = pe.transpose(ps[:, 7, 4 * ck:4 * ck + 4], rows[:, 3, ck * P:(ck + 1) * P], K("ident", 0, 4, 4))
                mb_mm.by(m)
                mc_a.wait(pe, l, 8)
                ns_y.wait(pe, l, 4)
                for ck in range(2):
                    m_row.wait(pe, l, ck + 1)
                    if ck == 1:
                        m_out.wait(pe, l, 1)
                        mb_ev.wait(pe, l, 1)
                    for b, r in ((0, 6), (1, 0)) + (((5, 2),) if ck else ()):
                        for h in range(MH):
                            m = pe.matmul(ps[:, b, h * P:(h + 1) * P], K("sel", h * P, (h + 1) * P, 4),
                                          rows[:, r, ck * P:(ck + 1) * P], start=True, stop=True)
                    for h in range(MH):
                        m = pe.matmul(ps[:, 2, h * P:(h + 1) * P], mix[:, T_QK + 4 + h, ck * P:(ck + 1) * P],
                                      mix[:, T_QK + h, ck * P:(ck + 1) * P], start=True, stop=True)
                    if ck == 0:
                        for h in range(MH):
                            m = pe.transpose(ps[:, 5, h * P:(h + 1) * P], mix[:, T_QK + 4 + h, 0:P], ident)
                    m_kt.by(m) if ck == 0 else m_qi.by(m)
                    m_sw.wait(pe, l, ck + 1)
                    if ck == 1:
                        m_qib_ready.wait(pe, l, 1)
                        m_cev.wait(pe, l, 2)
                    for h in range(MH):
                        hs = slice(h * P, (h + 1) * P)
                        pe.matmul(ps[:, 3, hs], vm[:, ck, h, :], m_swb[ck][:, hs], start=True, stop=ck == 0)
                        if ck:
                            pe.matmul(ps[:, 3, hs], m_C[:, hs], m_qib[:, hs], start=False, stop=True)
                        m = pe.matmul(ps[:, 4, hs], ones, m_swb[ck][:, hs], start=True, stop=ck == 0)
                        if ck:
                            m = pe.matmul(ps[:, 4, hs], m_n[:, hs], m_qib[:, hs], start=False, stop=True)
                    m_num.by(m)
                    if ck == 0:
                        m_kw.wait(pe, l, 1)
                        for h in range(MH):
                            hs = slice(h * P, (h + 1) * P)
                            pe.matmul(ps[:, 6, hs], m_kwb[:, hs], vm[:, 0, h, :], start=True, stop=True)
                            m = pe.matmul(ps[:, 7, hs], m_kwb[:, hs], ones, start=True, stop=True)
                        m_c.by(m)
                    m_hsq.wait(pe, l, ck + 1)
                    m = pe.matmul(ps[:, 2, :], ones, m_tb, start=True, stop=True)
                    m_ss.by(m)

                for k in range(KT):
                    to_tokens(l * CHUNKS + (C_OUT + 2 * k), l * NXS + k, C_OUT + 2 * k, k, k == KT - 1)
                norm_transposes(l, 1)

                def up(i, k):
                    for col in range(2):
                        c = C_UP + 4 * k + 2 * col
                        proj(l * CHUNKS + i * BODY + c, c, k, col * SEQ,
                             (ff_mul, l * (FREE + FT) + i * 5 + (k + 1)) if col == 0 else None,
                             (lambda half: h_lo.wait(pe, l, 12 + 4 * half)) if k == col == 0 else None)

                with pe.Fori(0, 6) as i:
                    for k in range(5):
                        up(i, k)
                    with pe.If(i + l * 4 < 4 * DEPTH - 2):
                        reduce_unit(l * UNITS + 10 + i)
                with pe.Fori(6, 8) as i:
                    for k in range(5):
                        up(i, k)
                for k in range(3):
                    up(8, k)
                pe.wait_ge(ff_mul, (l + 1) * (FREE + FT))
                gate_rows(l, 1)
                gt_ready.wait(pe, l, 2)
                def down(i, k, peeled=False, last=False):
                    c = C_DOWN + 2 * k
                    to_tokens(l * CHUNKS + i * BODY + c, l * NXS + i * 10 + (KT + k), c, k if peeled else k + 2, last)
                for k in range(10):
                    down(0, k, peeled=True)
                with pe.Fori(1, 4) as i:
                    for k in range(10):
                        down(i, k)
                for k in range(3):
                    down(4, k, last=k == 2)

        @block.scalar
        def _(s):
            s.wait_ge(c_in, 16)
            s.activation(cs[:, :], craw[:, :], ACT.Silu).then_inc(cs_ready, 1)
            for n, dst in enumerate((rope_s, rope_c)):
                s.wait_ge(rope_dve, ROPE_STEPS[n])
                s.activation(dst[:, :], mix[:, 2 + n, :], ACT.Sin).then_inc(rope_act, 1)
            s.wait_ge(x_in, 16)

            def apart(sem_, value):
                value = value if isinstance(value, int) else s.to_reg(value)
                s.wait_ge(c_in, 16)
                s.wait_ge(sem_, value)

            with s.Fori(0, DEPTH) as l:
                def w_head(c, i=0, used=True):
                    s.wait_ge(ring_full[c % RING], l * (CYCLES * 16) + i * (BODY // RING * 16) + (c // RING * 16 + 16))
                    if used:
                        s.wait_ge(w_used, l * CHUNKS + i * BODY + (c - SPLIT + 1))
                    s.activation(w_hi[:, c % SPLIT, :], ring[:, c % RING, :], ACT.Copy).then_inc(hi_ready, 1)

                def x_head(k, t, used=None):
                    src = mtile(t)
                    if used is not None:
                        apart(w_used, used)
                    s.activation(x_hi[:, k % 2, :], src, ACT.Copy).then_inc(xhi_ready, 1)

                def rms(n, src):
                    for t in range(TT):
                        rms_act.by(s.activation(junk[:, t, :], src(t), ACT.Square, accum_out=stat[:, t:t + 1]))
                    rms_act.wait(s, l, 2 * n + 2)
                    for t in range(TT):
                        rstd.by(s.activation(stat[:, 2 + t:3 + t], stat[:, t:t + 1], ACT.Sqrt, bias=K("eps"),
                                             scale=1.0 / D))

                def h_evac(n):
                    modA_ready.wait(s, l, n + 1)
                    for b in range(8):
                        h_tr.wait(s, l, 8 * n + b + 1)
                        for k in (2 * b, 2 * b + 1):
                            h_hi.by(s.activation(hT_hi[:, k, :], ps[:, b, k % 2 * SEQ:(k % 2 + 1) * SEQ], ACT.Identity,
                                                 bias=mod[:, 1, k:k + 1], scale=modA[:, k:k + 1]))

                def gt_evac(n):
                    gt_mm.wait(s, l, n + 1)
                    gt_ready.by(s.activation(gt_row[:, :], psf[:, 0:D], ACT.Copy))

                rms(0, lambda t: xs[:, t, :])
                for c in range(AHEAD):
                    w_head(c, used=False)
                h_evac(0)
                s.sem_inc(in_ev, FREE)
                def in_tile(i, k, dst, head=True):
                    s.wait_ge(w_used, l * CHUNKS + i * (2 * BODY) + (2 * k + 2))
                    s.activation(dst, ps[:, k % 5, 0:SEQ], ACT.Copy).then_inc(in_ev, 1)
                    if head:
                        for c in (2 * k + AHEAD, 2 * k + AHEAD + 1):
                            w_head(c, i * 2)
                for k in range(BODY):
                    in_tile(0, k, mix[:, k + T_U, :])
                for k in range(BODY):
                    in_tile(1, k, mix[:, (BODY + k + T_U) % NPROJ, :], head=k < BODY - 1)
                s.wait_ge(w_used, l * CHUNKS + C_CMP)
                gate_ev.by(s.activation(rows[:, 0, :], ps[G_I:G_I + MH, 5, 0:SEQ], ACT.Identity, bias=A("i_bias", p=4)))
                gate_ev.by(s.activation(rows[:, 1, :], ps[G_F:G_F + MH, 5, 0:SEQ], ACT.Identity, bias=A("f_bias", p=4)))
                gate_ev.by(s.activation(sg24[:, :], ps[G_N:G_N + 3 * NH, 5, 0:SEQ], ACT.Sigmoid))
                gt_evac(0)

                s5_pa.by(s.activation(SP5(0), A("log_dt"), ACT.Exp))
                s5_pd.wait(s, l, 1)
                s5_pa.by(s.activation(SP5(2), SP5(1), ACT.Exp))
                s5_pd.wait(s, l, 2)
                s5_pa.by(s.activation(SP5(7), SP5(5), ACT.Sin))
                s5_pd.wait(s, l, 3)
                s5_pa.by(s.activation(SP5(8), SP5(6), ACT.Sin))
                for u in range(UT):
                    s5_nf.wait(s, l, u + 1)
                    s.activation(s5_S, s5_pt, ACT.Sin, scale=-TWO_PI_IN)
                    s5_tab.by(s.activation(s5_C, s5_k, ACT.Sin, scale=-TWO_PI_IN, bias=K("half_pi")))
                    if u:
                        s5_y.wait(s, l, u)
                        s5_g.by(s.activation(mix[:, T_U + u - 1, :], mix[:, T_U + u - 1, :], ACT.Gelu_apprx_tanh))
                s5_y.wait(s, l, UT)
                s5_g.by(s.activation(mix[:, T_U + UT - 1, :], mix[:, T_U + UT - 1, :], ACT.Gelu_apprx_tanh))
                for n in range(4):
                    if n % 2 == 0:
                        glu_mm.wait(s, l, n // 2 + 1)
                    o = A_OFF["s_b_glu"][0]
                    glu_z.by(s.activation(S5T[:, n, :], ps[:, n // 2, (n % 2) * SEQ:(n % 2 + 1) * SEQ], ACT.Sigmoid,
                                          bias=aux[:, o + n:o + n + 1]))

                glu_y.wait(s, l, 1)
                for a in range(2):
                    vt_mm.wait(s, l, a + 1)
                    vt_ev.by(s.activation(vtok[:, a, :, :, :].rearrange("p h s e -> p (h s e)"), ps[:, a, :], ACT.Copy))
                for ck in range(2):
                    vt_mm.wait(s, l, 3 + ck)
                    vt_ev.by(s.activation(vm[:, ck, :, :].rearrange("p h e -> p (h e)"), ps[:, 2 + ck, :], ACT.Copy))
                vt_mm.wait(s, l, 5)
                vt_ev.by(s.activation(gates_t[:, :, :], ps[:, 6, 0:64].rearrange("p (t n) -> p t n", t=2)[:, :, 0:24],
                                      ACT.Copy))
                s.wait_ge(w_used, l * CHUNKS + C_OUT)
                for v in range(2):
                    ch_g.by(s.activation(hid[:, v, :], ps[:, 7, 64 * v:64 * v + 30], ACT.Gelu_apprx_tanh))
                cc_mm.wait(s, l, 1)
                cc_ev.by(s.activation(kcT, ps[:, 7, 128:158], ACT.Copy))
                cc_ev.by(s.activation(vct[:, :, :].rearrange("p h e -> p (h e)"), ps[0:NC, 7, 256:512], ACT.Copy))
                for n, (g, qt, kind) in enumerate(ITEMS):
                    nk = NC if kind == 0 else (qt + 1) * P
                    ns_m.wait(s, l, n + 1)
                    for h in range(GQ):
                        e = s.activation(pr[:, n % 2, h, 0:nk], pr[:, n % 2, h, 0:nk], ACT.Exp,
                                         bias=att_s[:, n % 2, h:h + 1], accum_out=att_s[:, n % 2, 4 + h:5 + h])
                    ns_e.by(e)
                    ns_t.wait(s, l, n + 1)
                    if n:
                        ns_o.wait(s, l, n)
                    if kind == 0:
                        ns_pt.by(s.activation(pt[0:NC, 0, :], ps[0:NC, 4, :], ACT.Copy))
                    else:
                        ns_pt.by(s.activation(pt[:, 0:qt + 1, :], ps[:, 4:4 + qt + 1, :], ACT.Copy))
                    if kind == 2:
                        ns_o.wait(s, l, n + 1)
                        ns_y.by(s.activation(mix[:, T_Q + GQ * g:T_Q + GQ * (g + 1), qt * P:(qt + 1) * P],
                                             ps[:, 6, :].rearrange("p (h t) -> p h t", h=GQ), ACT.Copy))

                for c in range(AHEAD):
                    w_head(C_OUT + c)

                for i in range(8):
                    mc_d.wait(s, l, i + 1)
                    mc_a.by(s.activation(mix[:, T_QK + i, :], m_cv(i), ACT.Silu))
                m_sig.by(s.activation(mix[:, T_O:T_O + 4, :], mix[:, T_O:T_O + 4, :], ACT.Sigmoid))
                gate_ev.wait(s, l, 3)
                act.chain(s, l, s.activation(rows[:, 2, :], rows[:, 1, :], ACT.Abs))
                act.chain(s, l, s.activation(rows[:, 2, :], rows[:, 2, :], ACT.Exp, scale=-1.0))
                mg_a.by(s.activation(rows[:, 2, :], rows[:, 2, :], ACT.Ln, bias=1.0))
                mb_mm.wait(s, l, 1)
                mb_ev.by(s.activation(bcol[:, :, :].rearrange("p c h -> p (c h)"), ps[:, 7, 0:8], ACT.Copy))
                mg_d.wait(s, l, 2)
                m_row.by(s.activation(rows[:, 0, :], rows[:, 5, :], ACT.Exp, scale=-1.0))
                m_row.by(s.activation(rows[:, 2, P:SEQ], rows[:, 4, P:SEQ], ACT.Exp, scale=-1.0, bias=rcol[:, 0:1]))
                for ck in range(2):
                    m_dlog.wait(s, l, ck + 1)
                    m_exp.by(s.activation(m_dt[ck], m_dt[ck], ACT.Exp))
                    m_num.wait(s, l, ck + 1)
                    m_abs.by(s.activation(m_e1, ps[:, 4, :], ACT.Abs))
                    if ck == 0:
                        m_c.wait(s, l, 1)
                        m_cev.by(s.activation(m_C, ps[:, 6, :], ACT.Copy))
                        m_cev.by(s.activation(m_n, ps[:, 7, :], ACT.Copy))
                    m_h.wait(s, l, ck + 1)
                    m_hsq.by(s.activation(m_tb, m_hb, ACT.Square))
                    m_ss.wait(s, l, ck + 1)
                    m_rs.by(s.activation(m_e2, ps[:, 2, :], ACT.Sqrt, bias=K("eps"), scale=1.0 / HD))

                m_out.wait(s, l, 2)
                glu_y.wait(s, l, 1)
                for k in range(2):
                    x_head(k, k)
                for k in range(KT):
                    c = C_OUT + 2 * k + AHEAD
                    w_head(c)
                    w_head(c + 1)
                    if k + 2 < KT:
                        x_head(k + 2, k + 2, l * CHUNKS + C_OUT + 2 * k + 2)

                s.wait_ge(w_used, l * CHUNKS + C_UP)
                rms(1, lambda t: psf[:, t * D:(t + 1) * D])
                x_ready.wait(s, l, 2)
                rms(2, lambda t: xs[:, t, :])
                h_evac(1)

                wo, bo = A_OFF["f_conv_w"][0], A_OFF["f_conv_b"][0]

                def gelu(i, k):
                    t = mtile(i * 5 + k)
                    apart(ff_conv, (l * FT + i * 5 + k) * 2 + 2)
                    s.activation(t, t, ACT.Gelu_apprx_tanh).then_inc(ff_gelu, 1)

                def tap(i, k):
                    t = i * 5 + k
                    w = aux[:, bass.ds(t * 3 + (wo + 2), 1)]
                    b = aux[:, bass.ds(t + bo, 1)]
                    apart(w_used, l * CHUNKS + i * BODY + (C_UP + 4 * k + 4))
                    s.activation(mtile(t), ps[:, k, 0:SEQ], ACT.Identity, scale=w, bias=b).then_inc(ff_tap, 1)

                def up(i, k, first=False):
                    c = C_UP + 4 * k + AHEAD
                    w_head(c, i)
                    if not first:
                        gelu(i, k - 1)
                    for j in (1, 2, 3):
                        w_head(c + j, i)
                    tap(i, k)

                for k in range(5):
                    up(0, k, k == 0)
                with s.Fori(1, 8) as i:
                    for k in range(5):
                        up(i, k)
                for k in range(3):
                    up(8, k)
                gelu(8, 2)
                s.wait_ge(ff_mul, (l + 1) * (FREE + FT))
                for k in range(2):
                    x_head(k, k)
                gt_evac(1)

                def down(i, k, head=True):
                    c = C_DOWN + 2 * k + AHEAD
                    if head:
                        w_head(c, i)
                        w_head(c + 1, i)
                        x_head(k, i * 10 + (k + 2), l * CHUNKS + i * BODY + (C_DOWN + 2 * k + 2))
                with s.Fori(0, 4) as i:
                    for k in range(10):
                        down(i, k)
                down(4, 0)
                s.wait_ge(w_used, (l + 1) * CHUNKS)
                rms(3, lambda t: psf[:, t * D:(t + 1) * D])
                x_ready.wait(s, l, 4)

        @block.vector
        def _(v):
            def tt(o, a, b, op):
                return v.tensor_tensor(o, a, b, op)

            def ts(o, a, s1, s2, op0, op1):
                return v.tensor_scalar(o, a, s1, s2, op0, op1)

            def stt(o, a, s, b, op0, op1):
                return v.scalar_tensor_tensor(o, a, s, b, op0, op1)

            def reduced_angle(step, src, k, r, shifted, scratch):
                step(ts(k, src, TURN, MAGIC, ALU.mult, ALU.add))
                step(ts(k, k, -MAGIC, None, ALU.add, ALU.bypass))
                step(stt(r, k, -PI_1, src, ALU.mult, ALU.add))
                step(stt(r, k, -PI_2, r, ALU.mult, ALU.add))
                step(stt(r, k, -PI_3, r, ALU.mult, ALU.add))
                step(ts(r, r, PI_IN, -PI_IN, ALU.min, ALU.max))
                step(ts(shifted, r, TWO_PI / 4, None, ALU.add, ALU.bypass))
                step(ts(scratch, shifted, PI_IN, -TWO_PI, ALU.is_gt, ALU.mult))
                step(tt(shifted, shifted, scratch, ALU.add))
                step(ts(shifted, shifted, PI_IN, -PI_IN, ALU.min, ALU.max))

            done = [0]

            def pro(ins):
                done[0] += 1
                ins.then_inc(rope_dve, 1)
                v.wait_ge(rope_dve, done[0])

            v.wait_ge(cst_in, 16)
            v.wait_ge(pos_in, 16)
            pro(v.tensor_copy(mix[:, 0, :], posi[:, :]))
            pro(ts(mix[:, 0, :], mix[:, 0, :], K("inv_freq"), None, ALU.mult, ALU.bypass))
            reduced_angle(pro, mix[:, 0, :], mix[:, 1, :], mix[:, 2, :], mix[:, 3, :], mix[:, 4, :])
            assert done[0] == ROPE_STEPS[1]
            v.wait_ge(cs_ready, 1)

            def ada_chunk(u, j):
                if j == 0:
                    v.wait_ge(acc_bias, u * 16 + 16)
                v.wait_ge(ada_full[j % ASLOT], u * (UCH // ASLOT * 16) + (16 * (j // ASLOT) + 16))
                if j:
                    v.wait_ge(ada_step, u * UCH + j)
                stt(ada_acc[:, :], ada_w[:, j % ASLOT, :], cs[:, j:j + 1], ada_acc[:, :], ALU.mult,
                    ALU.add).then_inc(ada_step, 1)

            def ada_finish(u, col):
                v.wait_ge(ada_red, u + 1)
                v.tensor_copy(col, ps[:, 7, 0:UG]).then_inc(mod_ready, 1)

            modf = mod[:, :, :].rearrange("p a b -> p (a b)")
            with v.Fori(0, 4) as i:
                for j in range(UCH):
                    ada_chunk(i, j)
                ada_finish(i, modf[:, bass.ds(i * UG + 2 * UG, UG)])
            v.wait_ge(x_in, 16)
            v.wait_ge(rope_act, 2)

            with v.Fori(0, DEPTH) as l:
                step = lambda ins: dve.chain(v, l, ins)

                def norm_in(n, gain):
                    v.wait_ge(mod_ready, l * UNITS + (4 if n == 0 else 10))
                    modA_ready.by(stt(modA[:, :], mod[:, 2, :], 1.0, A(gain), ALU.add, ALU.mult))
                    for t in range(TT):
                        rstd.wait(v, l, 4 * n + t + 1)
                        step(v.reciprocal(stat[:, 4 + t:5 + t], stat[:, 2 + t:3 + t]))
                        xn_ready.by(ts(xn[:, t, :], xs[:, t, :], stat[:, 4 + t:5 + t], None, ALU.mult, ALU.bypass))
                    modA_ready.wait(v, l, n + 1)
                    for b in range(8):
                        h_hi.wait(v, l, KT * n + 2 * b + 2)
                        for k in (2 * b, 2 * b + 1):
                            w = ts(h_t[:, k, :], ps[:, b, k % 2 * SEQ:(k % 2 + 1) * SEQ], modA[:, k:k + 1],
                                   mod[:, 1, k:k + 1], ALU.mult, ALU.add)
                        h_tmp.by(w)
                        h_tmp.wait(v, l, 8 * n + b + 1)
                        h_lo.by(tt(hT_lo[:, 2 * b:2 * b + 2, :], h_t[:, 2 * b:2 * b + 2, :],
                                   hT_hi[:, 2 * b:2 * b + 2, :].bitcast(F32), ALU.subtract))

                def w_rest(c, i=0):
                    v.wait_ge(hi_ready, l * NSPLIT + i * BODY + (c + 1 - (N_CMP if c >= C_OUT else 0)))
                    tt(w_lo[:, c % SPLIT, :], ring[:, c % RING, :], w_hi[:, c % SPLIT, :].bitcast(F32),
                       ALU.subtract).then_inc(raw_free, 1)

                def x_rest(k, t, n):
                    v.wait_ge(xhi_ready, n + 1)
                    tt(x_lo[:, k % 2, :], mtile(t), x_hi[:, k % 2, :].bitcast(F32), ALU.subtract).then_inc(xlo_ready, 1)

                def residual(n):
                    gt_ready.wait(v, l, n + 1)
                    for t in range(TT):
                        rstd.wait(v, l, 4 * n + 2 + t + 1)
                        step(v.reciprocal(stat[:, 6 + t:7 + t], stat[:, 2 + t:3 + t]))
                        tmp = mix[:, 0:8, :].rearrange("p a b -> p (a b)")
                        step(stt(tmp, psf[:, t * D:(t + 1) * D], stat[:, 6 + t:7 + t], gt_row[:, :], ALU.mult, ALU.mult))
                        x_ready.by(tt(xs[:, t, :], xs[:, t, :], tmp, ALU.add))
                        x_ready.wait(v, l, 2 * n + t + 1)

                def gate_gain(n, gain):
                    gg_ready.by(tt(gg[:, :], mod[:, 0, :], A(gain), ALU.mult))

                v.wait_ge(aux_in, l * 16 + 16)
                norm_in(0, "g_pre_mix")
                for c in range(AHEAD):
                    w_rest(c)
                with v.Fori(0, 2) as i:
                    for k in range(BODY):
                        if k < BODY - 1:
                            for c in (2 * k + AHEAD, 2 * k + AHEAD + 1):
                                w_rest(c, i * 2)
                        else:
                            with v.If(i < 1):
                                for c in (2 * k + AHEAD, 2 * k + AHEAD + 1):
                                    w_rest(c, i * 2)
                        for u in range(3):
                            uu = l * UNITS + i * 3 + (4 + u)
                            first, end = ADA_IN[u], ADA_IN[u] + ADA_STEPS
                            if first <= k < end:
                                for j in range(UCH * (k - first) // ADA_STEPS, UCH * (k + 1 - first) // ADA_STEPS):
                                    ada_chunk(uu, j)
                            if k == ADA_IN_PE[u]:
                                ada_finish(uu, modf[:, bass.ds((i * 3 + u) * UG, UG)])
                v.wait_ge(mod_ready, l * UNITS + 10)
                gate_gain(0, "g_post_mix")

                s5_pa.wait(v, l, 1)
                s5_pd.by(tt(SP5(1), A("lam_re"), SP5(0), ALU.mult))
                step(tt(SP5(3), A("lam_im"), SP5(0), ALU.mult))
                reduced_angle(step, SP5(3), SP5(4), SP5(5), SP5(6), SP5(9))
                s5_pd.by(ts(SP5(10), SP5(5), TURN, None, ALU.mult, ALU.bypass))
                s5_pd.by(tt(SP5(11), A("lam_re"), A("lam_re"), ALU.mult))
                step(tt(SP5(12), A("lam_im"), A("lam_im"), ALU.mult))
                step(tt(SP5(11), SP5(11), SP5(12), ALU.add))
                step(v.reciprocal(SP5(11), SP5(11)))
                s5_pa.wait(v, l, 4)
                step(tt(SP5(12), SP5(2), SP5(8), ALU.mult))
                step(tt(SP5(13), SP5(2), SP5(7), ALU.mult))
                step(ts(SP5(12), SP5(12), -1.0, None, ALU.add, ALU.bypass))
                step(tt(SP5(14), SP5(12), A("lam_re"), ALU.mult))
                step(tt(SP5(15), SP5(13), A("lam_im"), ALU.mult))
                step(tt(SP5(14), SP5(14), SP5(15), ALU.add))
                step(tt(SP5(14), SP5(14), SP5(11), ALU.mult))
                step(tt(SP5(15), SP5(13), A("lam_re"), ALU.mult))
                step(tt(SP5(16), SP5(12), A("lam_im"), ALU.mult))
                step(tt(SP5(15), SP5(15), SP5(16), ALU.subtract))
                step(tt(SP5(15), SP5(15), SP5(11), ALU.mult))
                cr = A("s_c_re").rearrange("p (j c) -> p j c", j=ST)
                ci = A("s_c_im").rearrange("p (j c) -> p j c", j=ST)
                zr = s5p[:, 14, :].unsqueeze(2).to_broadcast([P, ST, SC])
                zi = s5p[:, 15, :].unsqueeze(2).to_broadcast([P, ST, SC])
                b5 = [S5T[:, 2 * i:2 * i + 2, :].rearrange("p a b -> p (a b)").rearrange("p (j c) -> p j c", j=ST)
                      for i in range(4)]
                step(tt(b5[0], cr, zr, ALU.mult))
                step(tt(b5[1], ci, zi, ALU.mult))
                step(tt(b5[2], cr, zi, ALU.mult))
                step(tt(b5[3], ci, zr, ALU.mult))
                s5_pd.by(tt(cr, b5[0], b5[1], ALU.subtract))
                s5_pd.by(stt(ci, b5[2], -1.0, b5[3], ALU.mult, ALU.subtract))
                s5_pd.wait(v, l, 5)
                pv = S5T[:, 0:8, :].rearrange("p a b -> p (a b)").rearrange("p (i n) -> p i n", i=4)
                for u in range(UT):
                    if u:
                        s5_c.wait(v, l, 2 * u)
                    turns = s5p[:, 10, SQ * u:SQ * (u + 1)].unsqueeze(2).to_broadcast([P, SQ, SEQ])
                    stepb = K("steps").unsqueeze(1).to_broadcast([P, SQ, SEQ])
                    step(tt(s5_pt, turns, stepb, ALU.mult))
                    step(ts(s5_S, s5_pt, MAGIC, None, ALU.add, ALU.bypass))
                    step(ts(s5_k, s5_pt, 0.25, MAGIC, ALU.add, ALU.add))
                    fl = lambda a: a.rearrange("p a b -> p (a b)")
                    step(stt(fl(s5_k), fl(s5_k), -MAGIC, fl(s5_pt), ALU.add, ALU.subtract))
                    s5_nf.by(stt(fl(s5_pt), fl(s5_S), -MAGIC, fl(s5_pt), ALU.add, ALU.subtract))
                    s5_tab.wait(v, l, u + 1)
                    for hq in range(2):
                        q = 2 * u + hq
                        Cq = fl(s5_C[:, 2 * hq:2 * hq + 2, :])
                        Sq = fl(s5_S[:, 2 * hq:2 * hq + 2, :])
                        t0, t2, t1, t3 = (pv[:, i, :] for i in range(4))
                        s5_b.wait(v, l, q + 1)
                        if hq:
                            s5_c.wait(v, l, q)
                        two = lambda a: a.rearrange("p (a b) -> p a b", a=2)
                        wr, wi = ps[:, 0:2, 0:SEQ], ps[:, 2:4, 0:SEQ]
                        C3, S3 = s5_C[:, 2 * hq:2 * hq + 2, :], s5_S[:, 2 * hq:2 * hq + 2, :]
                        step(tt(two(t0), wr, C3, ALU.mult))
                        step(tt(two(t1), wi, S3, ALU.mult))
                        step(tt(t0, t0, t1, ALU.add))
                        step(tt(two(t1), wi, C3, ALU.mult))
                        s5_bv.by(tt(two(t2), wr, S3, ALU.mult))
                        s5_bv.wait(v, l, q + 1)
                        step(tt(t1, t1, t2, ALU.subtract))
                        for half in range(2):
                            j = 2 * q + half
                            hs = slice(half * SEQ, (half + 1) * SEQ)
                            a = s5p[:, 2, j:j + 1].to_broadcast([P, SEQ])
                            v.tensor_tensor_scan(t2[:, hs], a, t0[:, hs], 0.0, ALU.mult, ALU.add)
                            step(v.tensor_tensor_scan(t3[:, hs], a, t1[:, hs], 0.0, ALU.mult, ALU.add))
                        step(tt(t0, t2, Cq, ALU.mult))
                        step(tt(t1, t3, Sq, ALU.mult))
                        step(tt(t0, t0, t1, ALU.subtract))
                        step(tt(t1, t2, Sq, ALU.mult))
                        step(tt(t2, t3, Cq, ALU.mult))
                        s5_h.by(tt(t1, t1, t2, ALU.add))
                    s5_c.wait(v, l, 2 * u + 2)
                    o = A_OFF["s_d"][0] + u
                    s5_y.by(stt(mix[:, T_U + u, :], mix[:, T_U + u, :], aux[:, o:o + 1], ps[:, 6, 0:SEQ], ALU.mult, ALU.add))
                glu_z.wait(v, l, 4)
                glu_y.by(tt(mix[:, T_U:T_U + 4, :], mix[:, T_U:T_U + 4, :], S5T[:, 0:4, :], ALU.mult))

                rc = rope_c[:, :].unsqueeze(1).to_broadcast([P, 2, SEQ])
                rs = rope_s[:, :].unsqueeze(1).to_broadcast([P, 2, SEQ])
                rt = rp_t.rearrange("p (a b) -> p a b", a=2)
                for n, t in enumerate(ROPE_TILES):
                    rp_mm.wait(v, l, n + 1)
                    if n:
                        rp_d.wait(v, l, n)
                    step(tt(rt, ps[:, 4 + n % 2, :].rearrange("p (a b) -> p a b", a=2), rs, ALU.mult))
                    step(tt(mix[:, t:t + 2, :], mix[:, t:t + 2, :], rc, ALU.mult))
                    rp_d.by(tt(mix[:, t:t + 2, :], mix[:, t:t + 2, :], rt, ALU.add))
                rp_d.wait(v, l, 7)
                for kv in range(2):
                    for h in range(NKV):
                        x3 = mix[:, (T_KC, T_VC)[kv] + h, :].rearrange("p (n s) -> p s n", s=CS)
                        for hf in range(2):
                            o = A_OFF["cmp_pos"][0] + kv * CB + hf * CS
                            e = aux[:, o:o + CS].unsqueeze(2).to_broadcast([P, CS, NC])
                            b = tt(blk[:, kv, hf * CS:(hf + 1) * CS, h, :], x3[:, :, hf:hf + NC], e, ALU.add)
                    blk_ready.by(b)
                for c in range(C_CMP, C_OUT):
                    v.wait_ge(w_used, l * CHUNKS + c + 1)
                    v.sem_inc(raw_free, 1)
                for n, (g, qt, kind) in enumerate(ITEMS):
                    b = 2 * (n % 2)
                    nk = NC if kind == 0 else (qt + 1) * P
                    p3 = pr[:, n % 2, :, 0:nk]
                    st3 = att_s[:, n % 2, :]
                    ns_s.wait(v, l, n + 1)
                    if n >= 2:
                        ns_t.wait(v, l, n - 1)
                    if kind == 0:
                        s3 = ps[:, b, 0:64].rearrange("p (h s) -> p h s", h=GQ)[:, :, 0:NC]
                        m3 = K("cmp_mask", qt * NC, (qt + 1) * NC)
                    else:
                        s3 = ps[:, b:b + 2, :].rearrange("p a (c s) -> p (a c) s", c=2)[:, :, 0:nk]
                        m3 = K("mask", (1 - qt) * P, 2 * P)
                    step(stt(p3, s3, SCALE, m3.unsqueeze(1).to_broadcast([P, GQ, nk]), ALU.mult, ALU.add))
                    ns_m.by(v.tensor_reduce(st3[:, 0:4], p3, AX.X, ALU.max, negate=True))
                    ns_e.wait(v, l, n + 1)
                    step(v.reciprocal(st3[:, 8:12], st3[:, 4:8]))
                    step(tt(st3[:, 8:12], st3[:, 8:12],
                            gates_t[:, qt, :].rearrange("p (h c) -> p h c", c=3)[:, GQ * g:GQ * (g + 1), kind], ALU.mult))
                    w3 = st3[:, 8:12].unsqueeze(2).to_broadcast([P, GQ, nk])
                    if kind == 0:
                        step(tt(p3, p3, w3, ALU.mult))
                        ok = K("cmp_valid", qt * NC, (qt + 1) * NC).unsqueeze(1).to_broadcast([P, GQ, nk])
                        ns_p.by(tt(p3, p3, ok, ALU.mult))
                    else:
                        ns_p.by(tt(p3, p3, w3, ALU.mult))

                for c in range(AHEAD):
                    w_rest(C_OUT + c)

                cw, cb = A_OFF["m_conv_w"][0], A_OFF["m_conv_b"][0]
                for i in range(8):
                    src = mix[:, T_QK + i, :]
                    dst = m_cv(i)
                    wj = lambda j: aux[:, cw + 4 * i + j:cw + 4 * i + j + 1]
                    step(ts(dst, src, wj(3), aux[:, cb + i:cb + i + 1], ALU.mult, ALU.add))
                    for j in (1, 2, 3):
                        (step if j < 3 else mc_d.by)(
                            stt(dst[:, j:SEQ], src[:, 0:SEQ - j], wj(3 - j), dst[:, j:SEQ], ALU.mult, ALU.add))
                mg_a.wait(v, l, 1)
                step(ts(rows[:, 7, :], rows[:, 1, :], 0.0, None, ALU.min, ALU.bypass))
                step(tt(rows[:, 1, :], rows[:, 7, :], rows[:, 2, :], ALU.subtract))
                for ck in range(2):
                    cs_ = slice(ck * P, (ck + 1) * P)
                    g = v.tensor_tensor_scan(rows[:, 7, cs_], K("ones", p=4), rows[:, 1, cs_], 0.0, ALU.mult, ALU.add)
                step(g)
                mg_d.by(tt(rows[:, 3, :], rows[:, 0, :], rows[:, 7, :], ALU.subtract))
                mg_d.wait(v, l, 1)
                for ck in range(2):
                    cs_ = slice(ck * P, (ck + 1) * P)
                    step(v.tensor_tensor_scan(rows[:, 4, cs_], rows[:, 3, cs_], rows[:, 3, cs_],
                                              rcol[:, 0:1] if ck else 0.0, ALU.max, ALU.max))
                    step(tt(rows[:, 5, cs_], rows[:, 7, cs_], rows[:, 4, cs_], ALU.add))
                    if ck == 0:
                        step(v.tensor_copy(rcol[:, 0:1], rows[:, 5, P - 1:P]))
                mg_d.by(ts(rows[:, 6, :], rows[:, 4, :], -1.0, None, ALU.mult, ALU.bypass))
                for ck in range(2):
                    h4 = range(MH)
                    mb_ev.wait(v, l, 1)
                    (m_kt if ck == 0 else m_qi).wait(v, l, 1)
                    for h in h4:
                        hs = slice(h * P, (h + 1) * P)
                        d = stt(m_dt[ck][:, hs], ps[:, 0, hs], bcol[:, ck, h:h + 1], K("mask_t"), ALU.add, ALU.add)
                    m_dlog.by(d)
                    if ck == 1:
                        m_qib_ready.by(tt(m_qib.rearrange("p (h t) -> p h t", h=MH), mix[:, T_QK:T_QK + 4, P:SEQ],
                                          ps[:, 5, :].rearrange("p (h t) -> p h t", h=MH), ALU.mult))
                    m_exp.wait(v, l, ck + 1)
                    m_sw.by(stt(m_swb[ck], ps[:, 2, :], SCALE, m_dt[ck], ALU.mult, ALU.mult))
                    if ck == 0:
                        for h in h4:
                            hs = slice(h * P, (h + 1) * P)
                            d = ts(m_kwb[:, hs], ps[:, 5, hs], m_dt[0][:, h * P + P - 1:h * P + P], SCALE, ALU.mult, ALU.mult)
                        m_kw.by(d)
                    m_abs.wait(v, l, ck + 1)
                    step(tt(m_e1, m_e1, ps[:, 1, :], ALU.max))
                    step(v.reciprocal(m_e1, m_e1))
                    m_h.by(tt(m_hb, ps[:, 3, :], m_e1, ALU.mult))
                    m_rs.wait(v, l, ck + 1)
                    step(v.reciprocal(m_e2, m_e2))
                    step(tt(m_hb, m_hb, m_e2, ALU.mult))
                    m_sig.wait(v, l, 1)
                    for h in h4:
                        o = A_OFF["m_norm_g"][0] + h
                        yt = mix[:, T_O + h, ck * P:(ck + 1) * P]
                        d = stt(yt, m_hb[:, h * P:(h + 1) * P], aux[:, o:o + 1], yt, ALU.mult, ALU.mult)
                    m_out.by(d)

                ns_y.wait(v, l, 4)
                m_out.wait(v, l, 2)
                glu_y.wait(v, l, 1)
                for k in range(2):
                    x_rest(k, k, l * NXS + k)
                for k in range(KT):
                    c = C_OUT + 2 * k + AHEAD
                    w_rest(c)
                    w_rest(c + 1)
                    if k + 2 < KT:
                        x_rest(k + 2, k + 2, l * NXS + k + 2)
                residual(0)
                norm_in(1, "g_pre_ffn")

                v.sem_inc(ff_mul, FREE)
                wo = A_OFF["f_conv_w"][0]

                def conv(i, k):
                    t = i * 5 + k
                    g = mtile(t)
                    w = aux[:, wo + 3 * t:wo + 3 * t + 3] if isinstance(t, int) else aux[:, bass.ds(t * 3 + wo, 3)]
                    a = ps[:, k, 0:SEQ]
                    v.wait_ge(ff_tap, l * FT + i * 5 + (k + 1))
                    for j in (1, 2):
                        if j == 2:
                            v.wait_ge(ff_conv, (l * FT + i * 5 + k) * 2 + 1)
                        stt(g[:, j:SEQ], a[:, 0:SEQ - j], w[:, 2 - j:3 - j], g[:, j:SEQ], ALU.mult,
                            ALU.add).then_inc(ff_conv, 1)

                def gated(i, k):
                    g = mtile(i * 5 + k)
                    v.wait_ge(ff_gelu, l * FT + i * 5 + (k + 1))
                    tt(g, g, ps[:, k % 5, SEQ:2 * SEQ], ALU.mult).then_inc(ff_mul, 1)

                def up(i, k, first=False, ada=None):
                    c = C_UP + 4 * k + AHEAD
                    w_rest(c, i)
                    if not first:
                        gated(i, k - 1)
                    for j in (1, 2, 3):
                        w_rest(c + j, i)
                    conv(i, k)
                    if ada is not None:
                        u = l * UNITS + 10 + ada
                        with v.If(ada + l * 4 < 4 * DEPTH - 2):
                            if k < 4:
                                for j in range(4 * k, 4 * k + 4):
                                    ada_chunk(u, j)
                            else:
                                ada_finish(u, modf[:, bass.ds(ada * UG, UG)])

                for k in range(5):
                    up(0, k, k == 0, 0)
                with v.Fori(1, 6) as i:
                    for k in range(5):
                        up(i, k, False, i)
                with v.Fori(6, 8) as i:
                    for k in range(5):
                        up(i, k)
                for k in range(3):
                    up(8, k)
                gated(8, 2)
                gate_gain(1, "g_post_ffn")
                v.wait_ge(ff_mul, (l + 1) * (FREE + FT))
                for k in range(2):
                    x_rest(k, k, l * NXS + KT + k)

                def down(i, k):
                    c = C_DOWN + 2 * k + AHEAD
                    w_rest(c, i)
                    w_rest(c + 1, i)
                    x_rest(k, i * 10 + (k + 2), l * NXS + i * 10 + (KT + k + 2))
                with v.Fori(0, 4) as i:
                    for k in range(10):
                        down(i, k)
                down(4, 0)
                residual(1)

        wrong = [(str(sg.sem), sg.given, sg.per_layer) for sg in every if sg.given != sg.per_layer]
        assert not wrong, wrong


ROPE_TILES = [T_Q, T_Q + 2, T_Q + 4, T_Q + 6, T_KC, T_KS, T_KW]
ROPE_STEPS = (8, 12)
DVE_STEPS, ACT_STEPS = 247, 2
ADA_IN, ADA_STEPS, ADA_IN_PE = (0, 7, 14), 6, (6, 13, 19)



def _columns(a, n):
    return a.reshape(a.shape[0], n, P).transpose(0, 2, 1)


def _weights(i):
    out = np.empty((DEPTH, CHUNKS, P, CH), np.float32)

    def columns(w, c0, n):
        w = w[:, :, c0:c0 + n * P].reshape(DEPTH, 2, KH, P, n, P)
        return w.transpose(0, 4, 1, 3, 2, 5).reshape(DEPTH, 2 * n, P, CH)

    def rows(w, n):
        return w.reshape(DEPTH, n, P, 2, CH).transpose(0, 1, 3, 2, 4).reshape(DEPTH, 2 * n, P, CH)

    w_in = i["w_in"]
    at = 0
    for c0, n in ((2056, 4), (2568, 8), (3592, 12), (0, 8), (1024, 4), (1536, 4)):
        out[:, at:at + 2 * n] = columns(w_in, c0, n)
        at += 2 * n
    gates = np.zeros((DEPTH, D, P), np.float32)
    for row, c0, n in ((G_I, 2048, MH), (G_F, 2052, MH), (G_N, 5128, 3 * NH)):
        gates[:, :, row:row + n] = w_in[:, :, c0:c0 + n]
    out[:, C_GATES:C_CMP] = columns(gates, 0, 1)
    out[:, C_CMP:C_OUT] = i["n_cmp_w1"].reshape(DEPTH, 8, 8, P, P).transpose(0, 1, 3, 2, 4).reshape(DEPTH, 8, P, CH)
    out[:, C_OUT:C_UP] = rows(i["w_out"], KT)
    up = out[:, C_UP:C_DOWN].reshape(DEPTH, FT, 2, 2, P, CH)
    for branch in range(2):
        up[:, :, branch] = columns(i["f_w_up"], branch * DFF, FT).reshape(DEPTH, FT, 2, P, CH)
    out[:, C_DOWN:] = rows(i["f_w_down"], FT)
    return out.reshape(DEPTH * CHUNKS, P, CH)


def _params(i):
    out = np.zeros((DEPTH, P, A_W), np.float32)

    def put(name, a):
        o, w = A_OFF[name]
        out[:, :a.shape[1], o:o + w] = a.reshape(DEPTH, a.shape[1], w)

    for n in ("g_pre_mix", "g_post_mix", "g_pre_ffn", "g_post_ffn"):
        put(n, _columns(i[n], KT))
    put("m_conv_w", i["m_conv_w"].reshape(DEPTH, 4, 8, P).transpose(0, 3, 2, 1))
    put("m_conv_b", _columns(i["m_conv_b"], 8))
    put("m_norm_g", i["m_norm_g"].transpose(0, 2, 1))
    put("s_d", _columns(i["s_d"], 4))
    put("s_b_glu", _columns(i["s_b_glu"], 4))
    for n in ("lam_re", "lam_im"):
        put(n, i["s_" + n].reshape(DEPTH, ST, P).transpose(0, 2, 1))
    put("log_dt", np.repeat(i["s_log_dt"].reshape(DEPTH, ST, 2).transpose(0, 2, 1), S_STATE, axis=1))
    put("f_conv_w", i["f_conv_w"].reshape(DEPTH, 3, FT, P).transpose(0, 3, 2, 1))
    put("f_conv_b", _columns(i["f_conv_b"], FT))
    put("i_bias", i["m_i_bias"].reshape(DEPTH, 4, 1))
    put("f_bias", i["m_f_bias"].reshape(DEPTH, 4, 1))
    put("cmp_pos", i["n_cmp_pos"].transpose(0, 3, 1, 2))
    put("cmp_w2", i["n_cmp_w2"].transpose(0, 2, 1, 3))
    for part in ("re", "im"):
        ob, oc = A_OFF["s_b_" + part][0], A_OFF["s_c_" + part][0]
        for g in range(S_GROUPS):
            j, hb = g // 2, g % 2
            r, c = SC * (j % SQ) + S_GROUP * hb, ob + P * (j // SQ) + S_STATE * hb
            out[:, r:r + S_GROUP, c:c + S_STATE] = i["s_b_" + part][:, g].transpose(0, 2, 1)
            c = oc + SC * j + S_GROUP * hb
            out[:, S_STATE * hb:S_STATE * (hb + 1), c:c + S_GROUP] = i["s_c_" + part][:, g].transpose(0, 2, 1)
    return out


def _constants():
    out = np.zeros((P, K_W), np.float32)

    def put(name, a, rows=P):
        o, w = K_OFF[name]
        out[:rows, o:o + w] = np.asarray(a).reshape(rows, w)

    r = np.arange(P)
    put("ident", np.eye(P))
    put("ones", np.ones((P, P)))
    rot = np.zeros((P, P))
    rot[r[64:], r[:64]] = -1.0
    rot[r[:64], r[64:]] = 1.0
    put("rot", rot)
    put("mask", np.concatenate([np.zeros((P, P)), np.where(r[None] <= r[:, None], 0.0, NEG)], 1))
    put("mask_t", np.where(r[:, None] <= r[None], 0.0, NEG))
    t = r[:, None, None] + P * np.arange(TT)[None, :, None]
    ok = CS * np.arange(NC)[None, None] + CB - 1 <= t
    put("cmp_mask", np.where(ok, 0.0, NEG))
    put("cmp_valid", ok * 1.0)
    put("sel", (np.arange(MH)[:, None, None] == np.arange(MH)[None, :, None]) * np.ones((1, 1, P)), MH)
    put("steps", np.broadcast_to(np.arange(SEQ), (P, SEQ)))
    put("inv_freq", np.float32(10000.0) ** (-(r % 64).astype(np.float32) / np.float32(64)))
    put("half_pi", np.full(P, TWO_PI / 4))
    put("eps", np.full(P, EPS))
    return out


def kernel(**inputs):
    import concourse.bacc as bacc
    from concourse.bass_utils import run_bass_kernel_spmd

    i = {k: np.asarray(v) for k, v in inputs.items()}
    ada = i["w_ada"].reshape(DEPTH, UCH, P, UNITS, UC).transpose(0, 3, 1, 2, 4)
    arrays = {
        "x": i["x"],
        "c_cols": i["c"].reshape(KT, P).T,
        "pos": np.broadcast_to(i["positions"], (P, SEQ)),
        "consts": _constants(),
        "aux_d": _params(i),
        "ada_d": ada.reshape(DEPTH * UNITS * UCH, P, UC),
        "ada_b": i["b_ada"].reshape(DEPTH * UNITS, UC),
        "glu_d": i["s_w_glu"].reshape(DEPTH, 4, P, 512).transpose(0, 2, 1, 3).reshape(DEPTH, P, D),
        "stream": _weights(i),
    }
    arrays = {k: np.ascontiguousarray(a) for k, a in arrays.items()}
    nc = bacc.Bacc("TRN2", target_bir_lowering=False, num_devices=1)
    args = [nc.dram_tensor(k, a.shape, mybir.dt.from_np(a.dtype), kind="ExternalInput").ap() for k, a in arrays.items()]
    args.append(nc.dram_tensor("out", (1, SEQ, D), F32, kind="ExternalOutput").ap())
    trunk(nc, *args)
    r = run_bass_kernel_spmd(nc, [arrays], core_ids=[0])
    return r.results[0]["out"]
```

```python
import numpy as np
import concourse.bass as bass
from concourse import mybir
from concourse.alu_op_type import AluOpType as ALU
from contextlib import ExitStack

F32 = mybir.dt.float32
F32R = mybir.dt.float32r
I32 = mybir.dt.int32
ACT = mybir.ActivationFunctionType
AX = mybir.AxisListType

P = 128
D, SEQ, DEPTH = 2048, 256, 2
EPS = 1e-6
KT = D // P
TT = SEQ // P
HD = 128
MH = 4
S_GROUPS, S_STATE, S_GROUP = 32, 64, 16
ST = S_GROUPS * S_STATE // P
UT = S_GROUPS * S_GROUP // P
SQ = ST // UT
SC = 2 * S_GROUP
NH, NKV = 8, 2
GQ = NH // NKV
CB, CS = 32, 16
NC = SEQ // CS - 1
DFF = ((8 * D // 3 + 127) // 128) * 128
FT = DFF // P
SCALE = float(HD) ** -0.5
NEG = -1e30
TWO_PI = 6.283185307179586
TURN = 1.0 / TWO_PI
MAGIC = 12582912.0
PI_1, PI_2 = 6.28125, 0.0019350051879882812
PI_3 = TWO_PI - PI_1 - PI_2
PI_IN = 3.1415925
TWO_PI_IN = 6.283185

CH = KT * P // 2
KH = KT // 2
RING = 5
SPLIT = 4
AHEAD = SPLIT
C_IN = 0
C_GATES = 80
C_CMP = 82
N_CMP = 8
C_OUT = C_CMP + N_CMP
C_UP = C_OUT + 2 * KT
C_DOWN = C_UP + 4 * FT
CHUNKS = C_DOWN + 2 * FT
NSPLIT = CHUNKS - N_CMP
BODY = 20
assert CHUNKS % RING == 0 and CHUNKS % SPLIT == 0 and BODY % RING == 0 and BODY % SPLIT == 0
CYCLES = CHUNKS // RING
G_I, G_F, G_N = 0, 32, 64
NXS = KT + FT
FREE = 5

T_O, T_U, T_Q, T_KV, T_QK, T_V = 0, 4, 8, 16, 28, 36
NPROJ = 40
T_KC, T_VC, T_KS, T_VS, T_KW, T_VW = (T_KV + 2 * j for j in range(6))
W_S5 = NPROJ
NMIX = 56

UC = 1024
UNITS = 6 * D // UC
UG = UC // P
UCH = KT
ASLOT = 4

A_OFF, _o = {}, 0
for _name, _w in (("g_pre_mix", KT), ("g_post_mix", KT), ("g_pre_ffn", KT), ("g_post_ffn", KT), ("m_conv_w", 32),
                  ("m_conv_b", 8), ("m_norm_g", 4), ("s_d", 4), ("s_b_glu", 4), ("lam_re", ST), ("lam_im", ST),
                  ("log_dt", ST), ("f_conv_w", 3 * FT), ("f_conv_b", FT), ("i_bias", 1), ("f_bias", 1),
                  ("cmp_pos", 2 * CB), ("s_b_re", UT * P), ("s_b_im", UT * P), ("s_c_re", ST * SC),
                  ("s_c_im", ST * SC), ("cmp_w2", 2 * P)):
    A_OFF[_name] = (_o, _w)
    _o += _w
A_W = _o
K_OFF, _o = {}, 0
for _name, _w in (("ident", P), ("ones", P), ("rot", P), ("mask", 2 * P), ("mask_t", P), ("cmp_mask", TT * NC),
                  ("cmp_valid", TT * NC), ("sel", MH * P), ("steps", SEQ), ("inv_freq", 1), ("half_pi", 1), ("eps", 1),
                  ("magic", 1), ("quarter", 1)):
    K_OFF[_name] = (_o, _w)
    _o += _w
K_W = _o


def trunk(nc, x, c_cols, pos, consts, aux_d, ada_d, ada_b, glu_d, stream, out):
    with ExitStack() as ctx:
        def sb(name, shape, dt=F32):
            return ctx.enter_context(nc.sbuf_tensor(name, shape, dt))

        xs = sb("xs", [P, TT, D])
        scratch = sb("scratch", [P, 2 * KT * SEQ])
        at = nc.sbuf_base - 2 * KT * SEQ * 4
        hT_hi = nc.alloc_sbuf_tensor_at("hT_hi", [P, KT, SEQ], F32R, offset=at, align_bytes=32)
        hT_lo = nc.alloc_sbuf_tensor_at("hT_lo", [P, KT, SEQ], F32R, offset=at + KT * SEQ * 4,
                                        align_bytes=32)
        mix = sb("mix", [P, NMIX, SEQ])
        ring = sb("ring", [P, RING, CH])
        w_hi = sb("w_hi", [P, SPLIT, CH], F32R)
        at_hi = nc.sbuf_base - SPLIT * CH * 4
        w_lo = sb("w_lo", [P, SPLIT, CH], F32R)
        at_lo = nc.sbuf_base - SPLIT * CH * 4
        x_hi = sb("x_hi", [P, 2, SEQ], F32R)
        x_lo = sb("x_lo", [P, 2, SEQ], F32R)
        ada_w = sb("ada_w", [P, ASLOT, UC])
        spare_hi = nc.alloc_sbuf_tensor_at("spare_hi", [P, SPLIT, CH], F32, offset=at_hi, align_bytes=32)
        spare_lo = nc.alloc_sbuf_tensor_at("spare_lo", [P, SPLIT, CH], F32, offset=at_lo, align_bytes=32)
        ada_acc = sb("ada_acc", [P, 2, UC])
        gt_row = scratch[:, 3 * D:4 * D]
        aux = sb("aux", [P, A_W])
        cst = sb("cst", [P, K_W])
        posi = sb("posi", [P, SEQ], I32)
        rope_c = sb("rope_c", [P, SEQ])
        rope_s = sb("rope_s", [P, SEQ])
        mod = sb("mod", [P, 3, KT])
        modA = sb("modA", [P, KT])
        gg = sb("gg", [P, KT])
        cs = sb("cs", [P, KT])
        craw = sb("craw", [P, KT])
        stat = sb("stat", [P, 8])
        s5p = sb("s5p", [P, 20, ST])
        gates_t = sb("gates_t", [P, TT, 3 * NH])
        rows = scratch[0:MH, 2 * D:3 * D].rearrange("p (r s) -> p r s", r=8)
        rcol = sb("rcol", [4, 4])
        bcol = sb("bcol", [P, 2, MH])
        att_s = sb("att_s", [P, 2, 16])
        sg24 = sb("sg24", [3 * NH, SEQ])
        ps = ctx.enter_context(nc.psum_tensor("ps", [P, 8, 512], F32))

        def A(name, a=None, b=None, p=P):
            o, w = A_OFF[name]
            return aux[0:p, o + (a or 0):o + (w if b is None else b)]

        def K(name, a=None, b=None, p=P):
            o, w = K_OFF[name]
            return cst[0:p, o + (a or 0):o + (w if b is None else b)]

        ident, ones = K("ident"), K("ones")

        class Signal:
            def __init__(self, name, per_layer=None):
                self.sem = ctx.enter_context(nc.semaphore(name))
                self.per_layer = per_layer
                self.given = 0

            def by(self, ins, n=1):
                self.given += n
                ins.then_inc(self.sem, n)
                return ins

            def wait(self, eng, l, k):
                eng.wait_ge(self.sem, l * self.per_layer + k)

            def chain(self, eng, l, ins):
                self.by(ins)
                self.wait(eng, l, self.given)


        def sem(name):
            return ctx.enter_context(nc.semaphore(name))

        cst_in, x_in, c_in, pos_in = sem("cst_in"), sem("x_in"), sem("c_in"), sem("pos_in")
        aux_in = sem("aux_in")
        ring_full = [sem(f"ring_full{s}") for s in range(RING)]
        ada_full = [sem(f"ada_full{s}") for s in range(ASLOT)]
        glu_in = sem("glu_in")
        out_done = [sem(f"out_done{t}") for t in range(TT)]
        w_used = sem("w_used")
        hi_ready = sem("hi_ready")
        raw_free = sem("raw_free")
        xhi_ready, xlo_ready = sem("xhi_ready"), sem("xlo_ready")
        acc_zero, acc_bias = sem("acc_zero"), sem("acc_bias")
        ada_step = sem("ada_step")
        ada_red = sem("ada_red")
        mod_ready = sem("mod_ready")
        cs_ready, rope_dve, rope_act = sem("cs_ready"), sem("rope_dve"), sem("rope_act")
        rms_act = Signal("rms_act", 8)
        rstd = Signal("rstd", 8)
        dve = Signal("dve", DVE_STEPS)
        act = Signal("act", ACT_STEPS)
        x_ready = Signal("x_ready", 4)
        xn_ready = Signal("xn_ready", 4)
        h_tr = Signal("h_tr", 16)
        modA_ready = Signal("modA_ready", 2)
        h_hi = Signal("h_hi", 2 * KT)
        h_tmp = Signal("h_tmp", 2 * (8 - len(H_BY_ACT)))
        h_lo = Signal("h_lo", 16)
        gg_ready = Signal("gg_ready", 2)
        gt_mm = Signal("gt_mm", 2)
        gt_ready = Signal("gt_ready", 2)
        in_ev = sem("in_ev")
        gate_ev = Signal("gate_ev", 3)
        s5_pd, s5_pa = Signal("s5_pd", 5), Signal("s5_pa", 4)
        s5_ph = Signal("s5_ph", 2 * UT)
        s5_nf1, s5_nf = Signal("s5_nf1", 2 * UT), Signal("s5_nf", UT)
        s5_ai = Signal("s5_ai", 2 * UT)
        s5_tab = Signal("s5_tab", UT)
        s5_b = Signal("s5_b", ST // 2)
        s5_h = Signal("s5_h", ST // 2)
        s5_bv = Signal("s5_bv", ST // 2)
        s5_c = Signal("s5_c", ST // 2)
        s5_y = Signal("s5_y", UT)
        s5_g = Signal("s5_g", UT)
        glu_mm, glu_z, glu_y = Signal("glu_mm", 2), Signal("glu_z", 4), Signal("glu_y", 1)
        rp_mm, rp_ev, rp_t, rp_d = (Signal(n, 7) for n in ("rp_mm", "rp_ev", "rp_t", "rp_d"))
        vt_mm, vt_ev = Signal("vt_mm", 5), Signal("vt_ev", 5)
        blk_ready = Signal("blk_ready", 2)
        ch_g, cc_mm, cc_ev = Signal("ch_g", 2), Signal("cc_mm", 1), Signal("cc_ev", 2)
        ITEMS = [(g, qt, kind) for g in range(NKV) for qt in range(TT) for kind in range(3)]
        NI = len(ITEMS)
        ns_s, ns_m, ns_e, ns_p = (Signal(n, NI) for n in ("ns_s", "ns_m", "ns_e", "ns_p"))
        ns_t, ns_pt, ns_o = (Signal(n, NI) for n in ("ns_t", "ns_pt", "ns_o"))
        ns_y = Signal("ns_y", NKV * TT)
        mc_d, mc_p, mc_a = Signal("mc_d", 4), Signal("mc_p", 4 + 5 * 3), Signal("mc_a", 2)
        mg_a, mg_d = Signal("mg_a", 1), Signal("mg_d", 2)
        mb_mm, mb_ev = Signal("mb_mm", 1), Signal("mb_ev", 1)
        m_row = Signal("m_row", 2)
        m_dlog, m_exp = Signal("m_dlog", 2), Signal("m_exp", 2)
        m_sw, m_kw, m_kt, m_qi = Signal("m_sw", 2), Signal("m_kw", 1), Signal("m_kt", 1), Signal("m_qi", 1)
        m_c, m_cev = Signal("m_c", 1), Signal("m_cev", 2)
        m_num, m_abs, m_h, m_ss, m_rs, m_out = (Signal(n, 2) for n in ("m_num", "m_abs", "m_h", "m_ss", "m_rs", "m_out"))
        m_sig, m_qib_ready = Signal("m_sig", 1), Signal("m_qib_ready", 1)
        m_hsq = Signal("m_hsq", 2)
        ff_tap, ff_conv, ff_gelu, ff_mul = sem("ff_tap"), sem("ff_conv"), sem("ff_gelu"), sem("ff_mul")

        every = [v for v in list(locals().values()) if isinstance(v, Signal)]
        S5T = mix[:, W_S5:W_S5 + 16, :]
        s5_pt = S5T[:, 0:4, :]
        spare_t = scratch[:, D:2 * D].rearrange("p (a b) -> p a b", b=SEQ)
        s5_S = (S5T[:, 8:12, :], spare_t[:, 0:4, :])
        s5_C = (S5T[:, 12:16, :], spare_t[:, 4:8, :])

        def s5_phase(u):
            return s5_pt if u == 0 else spare_hi[:, u - 1, :].rearrange("p (a b) -> p a b", b=SEQ)

        def s5_hb(q, part):
            return spare_lo[:, q % 2, part * 2 * SEQ:(part + 1) * 2 * SEQ]
        SP5 = lambda i: s5p[:, i, :]
        xn = mix[:, 0:KT, :].rearrange("p a b -> p (a b)").rearrange("p (t d) -> p t d", t=TT)
        hflat = scratch[:, 0:2 * D]
        h_t = mix[:, KT:2 * KT, :]
        junk = h_t.rearrange("p a b -> p (a b)").rearrange("p (t d) -> p t d", t=TT)
        glu_w = spare_lo[:, 2:4, :].rearrange("p a b -> p (a b)")

        def mtile(t):
            return mix[:, t, :] if isinstance(t, int) else mix[:, bass.ds(t, 1), :].rearrange("p a b -> p (a b)")
        psf = ps[:, :, :].rearrange("p a b -> p (a b)")

        pr = hflat[:, 0:2048].rearrange("p (b h s) -> p b h s", b=2, h=GQ)
        pt = hflat[:, 2048:3072].rearrange("p (s n) -> p s n", s=2)
        vtok = S5T[:, 0:4, :].rearrange("p a b -> p (a b)").rearrange("p (a h s e) -> p a h s e", a=2, h=2, s=2)
        blk = scratch[:, 0:2 * CB * 2 * NC].rearrange(
            "p (v s h j) -> p v s h j", v=2, s=CB, h=2)
        hid = hflat[:, 3072:3072 + 60].rearrange("p (v n) -> p v n", v=2)
        kcT = hflat[:, 3136:3136 + 30]
        vct = hflat[0:NC, 3200:3200 + 256].rearrange("p (h e) -> p h e", h=2)
        def rp_buf(n):
            return spare_hi[:, 3, (n % 2) * 2 * SEQ:(n % 2 + 1) * 2 * SEQ].rearrange("p (a b) -> p a b", a=2)
        vm = S5T[:, 12:16, :].rearrange("p a b -> p (a b)").rearrange("p (c h e) -> p c h e", c=2, h=MH)
        def m_buf(i):
            return S5T[:, 2 * i:2 * i + 2, :].rearrange("p a b -> p (a b)")
        m_dt = [hflat[:, 512 * i:512 * i + 512] for i in range(2)]
        m_swb = [hflat[:, 1024 + 512 * i:1536 + 512 * i] for i in range(2)]
        m_kwb, m_C, m_n, m_qib = (hflat[:, 2048 + 512 * i:2560 + 512 * i] for i in range(4))
        def m_cv(i):
            return scratch[:, i * SEQ:(i + 1) * SEQ]
        m_tap = spare_hi[:, 0, :].rearrange("p (a b) -> p a b", b=SEQ)
        m_hb, m_tb = m_buf(0), m_buf(1)
        m_e1, m_e2 = m_buf(2), m_buf(3)

        block = ctx.enter_context(nc.Block())

        @block.sync
        def _(sp):
            sp.dma_start(cst[:, :], consts[:, :]).then_inc(cst_in, 16)
            sp.dma_start(xs[:, :, :], x.rearrange("b (t p) d -> p (b t) d", p=P)).then_inc(x_in, 16)
            sp.wait_ge(ada_step, 3 * UCH)
            for s in range(RING):
                sp.dma_start(ring[:, s, :], stream[s, :, :]).then_inc(ring_full[s], 16)
            with sp.Fori(1, DEPTH * CYCLES) as cyc:
                for s in range(RING):
                    at = sp.snap(cyc * RING + s)
                    sp.wait_ge(raw_free, cyc * RING + (s - RING + 1))
                    sp.dma_start(ring[:, s, :], stream[bass.ds(at, 1), :, :].rearrange("a p n -> p (a n)")
                                 ).then_inc(ring_full[s], 16)
            for t in range(TT):
                x_ready.wait(sp, DEPTH - 1, 3 + t)
                sp.dma_start(out[0, t * P:(t + 1) * P, :], xs[:, t, :]).then_inc(out_done[t], 16)
            for t in range(TT):
                sp.wait_ge(out_done[t], 16)

        @block.gpsimd
        def _(pool):
            def wait(sem_, value):
                value = value if isinstance(value, int) else pool.to_reg(value)
                pool.wait_ge(c_in, 16)
                pool.wait_ge(sem_, value)

            def unit(u, a, red):
                if not isinstance(u, int):
                    u = nc.s_assert_within(u, 0, DEPTH * UNITS - 1)
                if not isinstance(red, int) or red > 0:
                    wait(ada_red, red)
                pool.memset(ada_acc[:, a, :], 0.0).then_inc(acc_zero, 1)
                wait(acc_zero, u + 1)
                pool.dma_start(ada_acc[0:1, a, :], ada_b[bass.ds(u, 1), :]).then_inc(acc_bias, 16)
                for j in range(UCH):
                    s = j % ASLOT
                    if not isinstance(u, int) or UCH * u + j >= ASLOT:
                        wait(ada_step, UCH * u + (j - ASLOT + 1))
                    pool.dma_start(ada_w[:, s, :],
                                   ada_d[bass.ds(u * UCH + j, 1), :, :].rearrange("a p n -> p (a n)")).then_inc(ada_full[s], 16)

            pool.dma_start(craw[:, :], c_cols[:, :]).then_inc(c_in, 16)
            pool.dma_start(posi[:, :], pos[:, :]).then_inc(pos_in, 16)
            pool.dma_start(aux[:, :], aux_d[0, :, :]).then_inc(aux_in, 16)
            for u in range(4):
                unit(u, u % 2, u - 1)
            with pool.Fori(0, DEPTH) as l:
                with pool.Fori(0, 2) as i:
                    u = l * UNITS + i * 2
                    unit(u + 4, 0, u + 4)
                    unit(u + 5, 1, u + 4)
                def whole_turns(u):
                    for n, (b, first) in enumerate(((s5_S[u % 2], 1), (s5_C[u % 2], 2))):
                        wait(s5_ph.sem, l * s5_ph.per_layer + 2 * u + first)
                        s5_nf1.by(pool.tensor_scalar(b, b, -MAGIC, None, ALU.add, ALU.bypass))
                        wait(s5_nf1.sem, l * s5_nf1.per_layer + 2 * u + n + 1)
                        w = pool.tensor_tensor(b, b, s5_phase(u), ALU.subtract)
                    s5_nf.by(w)

                whole_turns(0)
                wait(w_used, l * CHUNKS + C_CMP)
                pool.dma_start(glu_w, glu_d[bass.ds(l, 1), :, :].rearrange("a p n -> p (a n)")).then_inc(glu_in, 16)

                rc = rope_c[:, :].unsqueeze(1).to_broadcast([P, 2, SEQ])
                rs = rope_s[:, :].unsqueeze(1).to_broadcast([P, 2, SEQ])

                def rope(n):
                    t = ROPE_TILES[n]
                    x2 = mix[:, t:t + 2, :]
                    wait(rp_ev.sem, l * 7 + n + 1)
                    pool.tensor_tensor(rp_buf(n), rp_buf(n), rs, ALU.mult)
                    rp_t.by(pool.tensor_tensor(x2, x2, rc, ALU.mult))
                    wait(rp_t.sem, l * 7 + n + 1)
                    rp_d.by(pool.tensor_tensor(x2, x2, rp_buf(n), ALU.add))

                def blocks(kv):
                    wait(rp_d.sem, l * 7 + 1)
                    for h in range(NKV):
                        x3 = mix[:, (T_KC, T_VC)[kv] + h, :].rearrange("p (n s) -> p s n", s=CS)
                        for hf in range(2):
                            o = A_OFF["cmp_pos"][0] + kv * CB + hf * CS
                            e = aux[:, o:o + CS].unsqueeze(2).to_broadcast([P, CS, NC])
                            b = pool.tensor_tensor(blk[:, kv, hf * CS:(hf + 1) * CS, h, :], x3[:, :, hf:hf + NC], e,
                                                   ALU.add)
                    blk_ready.by(b)

                rope(0)
                blocks(0)
                whole_turns(1)
                rope(1)
                blocks(1)
                whole_turns(2)
                rope(2)
                rope(3)
                whole_turns(3)
                for n in (4, 5, 6):
                    rope(n)
                wait(s5_h.sem, l * s5_h.per_layer + 6)
                cw, cb = A_OFF["m_conv_w"][0], A_OFF["m_conv_b"][0]
                keys = S5T[:, 8:12, :]
                for i in range(4):
                    at_ = cw + 4 * (4 + i)
                    mc_p.by(pool.tensor_scalar(keys[:, i, :], mix[:, T_QK + 4 + i, :], aux[:, at_ + 3:at_ + 4],
                                               aux[:, cb + 4 + i:cb + 5 + i], ALU.mult, ALU.add))
                for j in (1, 2, 3):
                    wait(mc_p.sem, l * mc_p.per_layer + mc_p.given)
                    for i in range(4):
                        at_ = cw + 4 * (4 + i) + 3 - j
                        mc_p.by(pool.tensor_scalar(m_tap[:, i, j:SEQ], mix[:, T_QK + 4 + i, 0:SEQ - j],
                                                   aux[:, at_:at_ + 1], None, ALU.mult, ALU.bypass))
                    wait(mc_p.sem, l * mc_p.per_layer + mc_p.given)
                    mc_p.by(pool.tensor_tensor(keys[:, :, j:SEQ], keys[:, :, j:SEQ], m_tap[:, :, j:SEQ], ALU.add))
                for a in range(2):
                    unit(l * UNITS + (8 + a), a, l * UNITS + (7 + a))
                with pool.Fori(0, 2) as i:
                    unit(l * UNITS + 10 + i, 0, l * UNITS + 10 + i)
                with pool.If(l < DEPTH - 1):
                    with pool.Fori(2, 6) as i:
                        unit(l * UNITS + 10 + i, 0, l * UNITS + 10 + i)
                    nxt = nc.s_assert_within(l + 1, 1, DEPTH - 1)
                    wait(w_used, l * CHUNKS + C_DOWN + 1)
                    pool.dma_start(aux[:, :], aux_d[bass.ds(nxt, 1), :, :].rearrange("a p n -> p (a n)")
                                   ).then_inc(aux_in, 16)

        @block.tensor
        def _(pe):
            def full(c, cyc):
                pe.wait_ge(ring_full[c % RING], cyc * 16 + 16)

            def split_ready(n):
                pe.wait_ge(raw_free, n + 1)

            def reduce_unit(u, a, free, bank=7, col=0):
                if not isinstance(free, int) or free > 0:
                    pe.wait_ge(mod_ready, free)
                pe.wait_ge(ada_step, u * UCH + UCH)
                for k in range(UG):
                    m = pe.matmul(ps[:, bank, col + k:col + k + 1], ada_acc[:, a, k * P:(k + 1) * P], ones[:, 0:1], start=True, stop=True)
                m.then_inc(ada_red, 1)

            def norm_transposes(l, n):
                for t in range(TT):
                    xn_ready.wait(pe, l, 2 * n + t + 1)
                    for b in range(8):
                        for k in range(2):
                            m = pe.transpose(ps[:, b, k * SEQ + t * P:k * SEQ + (t + 1) * P],
                                             xn[:, t, (2 * b + k) * P:(2 * b + k + 1) * P], ident)
                        if t == TT - 1:
                            h_tr.by(m)

            def proj(n, c, bank, col=0, wait_ev=None, h_part=None):
                for half in range(2):
                    split_ready(n + half)
                    if wait_ev is not None and half == 0:
                        pe.wait_ge(*wait_ev)
                    if h_part is not None:
                        h_part(half)
                    s = (c + half) % SPLIT
                    for kk in range(KH):
                        k = half * KH + kk
                        ks = slice(kk * P, (kk + 1) * P)
                        for p, (w, h) in enumerate(((w_hi, hT_hi), (w_hi, hT_lo), (w_lo, hT_hi))):
                            m = pe.matmul(ps[:, bank, col:col + SEQ], w[:, s, ks], h[:, k, :],
                                          start=k == 0 and p == 0, stop=k == KT - 1 and p == 2)
                    m.then_inc(w_used, 1)

            def gate_rows(l, n):
                gg_ready.wait(pe, l, n + 1)
                for k in range(KT):
                    m = pe.matmul(ps[:, k // 4, (k % 4) * P:(k % 4 + 1) * P], gg[:, k:k + 1].to_broadcast([P, P]),
                                  ident, start=True, stop=True)
                gt_mm.by(m)

            def to_tokens(n, x0, c, k, last):
                xs_ = k % 2
                pe.wait_ge(xlo_ready, x0 + 1)
                for half in range(2):
                    split_ready(n + half)
                    s = (c + half) % SPLIT
                    for t in range(TT):
                        ts_ = slice(t * P, (t + 1) * P)
                        for p, (xx, w) in enumerate(((x_hi, w_hi), (x_hi, w_lo), (x_lo, w_hi))):
                            for b in range(2):
                                m = pe.matmul(ps[:, 4 * t + 2 * half + b, :], xx[:, xs_, ts_], w[:, s, b * 512:(b + 1) * 512],
                                              start=k == 0 and p == 0, stop=last and p == 2)
                    m.then_inc(w_used, 1)

            pe.wait_ge(cst_in, 16)
            for u in range(4):
                reduce_unit(u, u % 2, u)

            with pe.Fori(0, DEPTH) as l:
                norm_transposes(l, 0)
                with pe.Fori(0, 2) as i:
                    for s in range(BODY):
                        c = 2 * s
                        hp = (lambda half: h_lo.wait(pe, l, 4 + 4 * half)) if s == 0 else None
                        proj(l * CHUNKS + i * (2 * BODY) + c, c, s % 5, 0,
                             (in_ev, l * (FREE + NPROJ) + i * BODY + (s + 1)), hp)
                        if s in ADA_IN_PE:
                            a = ADA_IN_PE.index(s)
                            u = l * UNITS + i * 2 + (4 + a)
                            reduce_unit(u, a, u)
                proj(l * CHUNKS + C_GATES, C_GATES, 5)
                pe.wait_ge(in_ev, (l + 1) * (FREE + NPROJ))
                gate_rows(l, 0)

                s5_pd.wait(pe, l, 5)
                gate_ev.wait(pe, l, 3)
                def s5_in(q):
                    ut = q // 2
                    if q >= 1:
                        s5_bv.wait(pe, l, q)
                    for part, name in ((0, "s_b_re"), (1, "s_b_im")):
                        for half in range(2):
                            r = SC * (2 * (q % 2) + half)
                            o = A_OFF[name][0] + ut * P
                            m = pe.matmul(ps[:, 2 * part + half, 0:SEQ], aux[r:r + SC, o:o + P],
                                          mix[r:r + SC, T_U + ut, :], start=True, stop=True)
                    s5_b.by(m)

                def rotated(n):
                    if n >= 2:
                        rp_ev.wait(pe, l, n - 1)
                    t = ROPE_TILES[n]
                    rp_mm.by(pe.matmul(ps[:, 4 + n % 2, :], K("rot"), mix[:, t:t + 2, :], start=True, stop=True))

                def compress(i):
                    v, qr = i // 4, i % 4
                    if qr == 0:
                        blk_ready.wait(pe, l, v + 1)
                    c = C_CMP + i
                    full(c, l * CYCLES + c // RING)
                    for j in range(8):
                        pos_i = 8 * qr + j
                        m = pe.matmul(ps[:, 7, 64 * v:64 * v + 30], ring[:, c % RING, j * P:(j + 1) * P],
                                      blk[:, v, pos_i, :, :], start=pos_i == 0, stop=pos_i == CB - 1)
                    m.then_inc(w_used, 1)

                rotated(0)
                rotated(1)
                gt_ready.wait(pe, l, 1)
                s5_in(0)
                for q in range(ST // 2):
                    ut = q // 2
                    if q + 1 < ST // 2:
                        s5_in(q + 1)
                    if q:
                        compress(q - 1)
                    s5_h.wait(pe, l, q + 1)
                    if q % 2 == 0 and ut >= 1:
                        s5_y.wait(pe, l, ut)
                    for half in range(2):
                        j = 2 * q + half
                        r = SC * (j % SQ)
                        for part, name in ((0, "s_c_re"), (1, "s_c_im")):
                            o = A_OFF[name][0] + j * SC
                            m = pe.matmul(ps[r:r + SC, 6, 0:SEQ], aux[:, o:o + SC],
                                          s5_hb(q, part)[:, half * SEQ:(half + 1) * SEQ],
                                          start=part == 0, stop=part == 1)
                    s5_c.by(m)
                    if q + 2 < len(ROPE_TILES):
                        rotated(q + 2)
                compress(N_CMP - 1)
                for a, t0 in enumerate((T_VS, T_VW)):
                    for h in range(2):
                        for s in range(2):
                            m = pe.transpose(ps[:, a, (2 * h + s) * P:(2 * h + s + 1) * P],
                                             mix[:, t0 + h, s * P:(s + 1) * P], ident)
                    vt_mm.by(m)
                for ck in range(2):
                    for h in range(MH):
                        m = pe.transpose(ps[:, 2 + ck, h * P:(h + 1) * P], mix[:, T_V + h, ck * P:(ck + 1) * P], ident)
                    vt_mm.by(m)
                pe.wait_ge(glu_in, l * 16 + 16)
                s5_g.wait(pe, l, UT)
                rp_ev.wait(pe, l, 7)
                for n in range(4):
                    for k in range(4):
                        m = pe.matmul(ps[:, 4 + n // 2, (n % 2) * SEQ:(n % 2 + 1) * SEQ],
                                      glu_w[:, k * 512 + n * P:k * 512 + (n + 1) * P],
                                      mix[:, T_U + k, :], start=k == 0, stop=k == 3)
                    if n % 2:
                        glu_mm.by(m)

                pe.wait_ge(cst_in, 16)
                s5_y.wait(pe, l, UT)
                for t in range(TT):
                    m = pe.transpose(ps[:, 6, 32 * t:32 * t + 24], sg24[:, t * P:(t + 1) * P], K("ident", 0, 24, 24))
                vt_mm.by(m)
                ch_g.wait(pe, l, 2)
                w2o = A_OFF["cmp_w2"][0]
                pe.matmul(ps[:, 7, 128:158], aux[:, w2o:w2o + P], hid[:, 0, :], start=True, stop=True)
                for h in range(NKV):
                    m = pe.matmul(ps[0:NC, 7, 256 + h * P:384 + h * P], hid[:, 1, h * NC:(h + 1) * NC],
                                  aux[:, w2o + P:w2o + 2 * P], start=True, stop=True)
                cc_mm.by(m)

                def scores(n):
                    g, qt, kind = ITEMS[n]
                    if n >= 2:
                        ns_m.wait(pe, l, n - 1)
                    b = 2 * (n % 2)
                    for h in range(GQ):
                        q = mix[:, T_Q + GQ * g + h, qt * P:(qt + 1) * P]
                        if kind == 0:
                            m = pe.matmul(ps[:, b, h * 16:h * 16 + NC], q, kcT[:, g * NC:(g + 1) * NC],
                                          start=True, stop=True)
                        else:
                            kt = (T_KS if kind == 1 else T_KW) + g
                            nk = (qt + 1) * P
                            m = pe.matmul(ps[:, b + h // 2, (h % 2) * SEQ:(h % 2) * SEQ + nk], q, mix[:, kt, 0:nk],
                                          start=True, stop=True)
                    ns_s.by(m)

                rp_d.wait(pe, l, 7)
                cc_ev.wait(pe, l, 2)
                vt_ev.wait(pe, l, 5)
                scores(0)
                pe.wait_ge(cst_in, 16)
                mg_d.wait(pe, l, 1)
                for ck in range(2):
                    m = pe.transpose(ps[:, 7, 4 * ck:4 * ck + 4], rows[:, 3, ck * P:(ck + 1) * P], K("ident", 0, 4, 4))
                mb_mm.by(m)
                scores(1)
                for n, (g, qt, kind) in enumerate(ITEMS):
                    ns_p.wait(pe, l, n + 1)
                    if n >= 1:
                        ns_pt.wait(pe, l, n)
                    nst = 1 if kind == 0 else qt + 1
                    for s in range(nst):
                        for h in range(GQ):
                            if kind == 0:
                                m = pe.transpose(ps[0:NC, 4, h * P:(h + 1) * P], pr[:, n % 2, h, 0:NC], ident)
                            else:
                                m = pe.transpose(ps[:, 4 + s, h * P:(h + 1) * P], pr[:, n % 2, h, s * P:(s + 1) * P], ident)
                    ns_t.by(m)
                    if n + 2 < NI:
                        scores(n + 2)
                    ns_pt.wait(pe, l, n + 1)
                    if kind == 0 and n >= 3:
                        ns_y.wait(pe, l, n // 3)
                    if kind == 0:
                        m = pe.matmul(ps[:, 6, :], vct[:, g, :], pt[0:NC, 0, :], start=True, stop=False)
                    else:
                        for s in range(nst):
                            m = pe.matmul(ps[:, 6, :], vtok[:, kind - 1, g, s, :], pt[:, s, :], start=False,
                                          stop=kind == 2 and s == nst - 1)
                    ns_o.by(m)

                mc_a.wait(pe, l, 2)
                ns_y.wait(pe, l, 4)
                for ck in range(2):
                    m_row.wait(pe, l, ck + 1)
                    if ck == 1:
                        m_rs.wait(pe, l, 1)
                        mb_ev.wait(pe, l, 1)
                    for b, r in ((0, 6), (1, 0)) + (((5, 2),) if ck else ()):
                        for h in range(MH):
                            m = pe.matmul(ps[:, b, h * P:(h + 1) * P], K("sel", h * P, (h + 1) * P, 4),
                                          rows[:, r, ck * P:(ck + 1) * P], start=True, stop=True)
                    for h in range(MH):
                        m = pe.matmul(ps[:, 2, h * P:(h + 1) * P], mix[:, T_QK + 4 + h, ck * P:(ck + 1) * P],
                                      mix[:, T_QK + h, ck * P:(ck + 1) * P], start=True, stop=True)
                    if ck == 0:
                        for h in range(MH):
                            m = pe.transpose(ps[:, 5, h * P:(h + 1) * P], mix[:, T_QK + 4 + h, 0:P], ident)
                    m_kt.by(m) if ck == 0 else m_qi.by(m)
                    m_sw.wait(pe, l, ck + 1)
                    if ck == 1:
                        m_qib_ready.wait(pe, l, 1)
                        m_cev.wait(pe, l, 2)
                    for h in range(MH):
                        hs = slice(h * P, (h + 1) * P)
                        pe.matmul(ps[:, 3, hs], vm[:, ck, h, :], m_swb[ck][:, hs], start=True, stop=ck == 0)
                        if ck:
                            pe.matmul(ps[:, 3, hs], m_C[:, hs], m_qib[:, hs], start=False, stop=True)
                        m = pe.matmul(ps[:, 4, hs], ones, m_swb[ck][:, hs], start=True, stop=ck == 0)
                        if ck:
                            m = pe.matmul(ps[:, 4, hs], m_n[:, hs], m_qib[:, hs], start=False, stop=True)
                    m_num.by(m)
                    if ck == 0:
                        m_kw.wait(pe, l, 1)
                        for h in range(MH):
                            hs = slice(h * P, (h + 1) * P)
                            pe.matmul(ps[:, 6, hs], m_kwb[:, hs], vm[:, 0, h, :], start=True, stop=True)
                            m = pe.matmul(ps[:, 7, hs], m_kwb[:, hs], ones, start=True, stop=True)
                        m_c.by(m)
                    m_hsq.wait(pe, l, ck + 1)
                    m = pe.matmul(ps[:, 2, :], ones, m_tb, start=True, stop=True)
                    m_ss.by(m)

                for k in range(KT):
                    to_tokens(l * CHUNKS + (C_OUT + 2 * k), l * NXS + k, C_OUT + 2 * k, k, k == KT - 1)
                x_ready.wait(pe, l, 1)
                for a in range(2):
                    reduce_unit(l * UNITS + (8 + a), a, l * UNITS + 8, 0, a * UG)
                pe.wait_ge(mod_ready, l * UNITS + 10)
                norm_transposes(l, 1)

                def up(i, k):
                    for col in range(2):
                        c = C_UP + 4 * k + 2 * col
                        proj(l * CHUNKS + i * BODY + c, c, k, col * SEQ,
                             (ff_mul, l * (FREE + FT) + i * 5 + (k + 1)) if col == 0 else None,
                             (lambda half: h_lo.wait(pe, l, 12 + 4 * half)) if k == col == 0 else None)

                with pe.Fori(0, 6) as i:
                    for k in range(5):
                        up(i, k)
                    with pe.If(i + l * 4 < 4 * DEPTH - 2):
                        reduce_unit(l * UNITS + 10 + i, 0, l * UNITS + 10 + i)
                with pe.Fori(6, 8) as i:
                    for k in range(5):
                        up(i, k)
                for k in range(3):
                    up(8, k)
                pe.wait_ge(ff_mul, (l + 1) * (FREE + FT))
                gate_rows(l, 1)
                gt_ready.wait(pe, l, 2)
                def down(i, k, peeled=False, last=False):
                    c = C_DOWN + 2 * k
                    to_tokens(l * CHUNKS + i * BODY + c, l * NXS + i * 10 + (KT + k), c, k if peeled else k + 2, last)
                for k in range(10):
                    down(0, k, peeled=True)
                with pe.Fori(1, 4) as i:
                    for k in range(10):
                        down(i, k)
                for k in range(3):
                    down(4, k, last=k == 2)

        @block.scalar
        def _(s):
            s.wait_ge(c_in, 16)
            s.activation(cs[:, :], craw[:, :], ACT.Silu).then_inc(cs_ready, 1)
            for n, dst in enumerate((rope_s, rope_c)):
                s.wait_ge(rope_dve, ROPE_STEPS[n])
                s.activation(dst[:, :], mix[:, 2 + n, :], ACT.Sin).then_inc(rope_act, 1)
            s.wait_ge(x_in, 16)

            def apart(sem_, value):
                value = value if isinstance(value, int) else s.to_reg(value)
                s.wait_ge(c_in, 16)
                s.wait_ge(sem_, value)

            with s.Fori(0, DEPTH) as l:
                def w_head(c, i=0, used=True):
                    s.wait_ge(ring_full[c % RING], l * (CYCLES * 16) + i * (BODY // RING * 16) + (c // RING * 16 + 16))
                    if used:
                        s.wait_ge(w_used, l * CHUNKS + i * BODY + (c - SPLIT + 1))
                    s.activation(w_hi[:, c % SPLIT, :], ring[:, c % RING, :], ACT.Copy).then_inc(hi_ready, 1)

                def x_head(k, t, used=None):
                    src = mtile(t)
                    if used is not None:
                        apart(w_used, used)
                    s.activation(x_hi[:, k % 2, :], src, ACT.Copy).then_inc(xhi_ready, 1)

                def rms(n, src):
                    for t in range(TT):
                        if n == 2:
                            x_ready.wait(s, l, t + 1)
                        rms_act.by(s.activation(junk[:, t, :], src(t), ACT.Square, accum_out=stat[:, t:t + 1]))
                        rms_act.wait(s, l, 2 * n + t + 1)
                        rstd.by(s.activation(stat[:, 2 + t:3 + t], stat[:, t:t + 1], ACT.Sqrt, bias=K("eps"),
                                             scale=1.0 / D))

                def h_evac(n):
                    modA_ready.wait(s, l, n + 1)
                    for b in range(8):
                        h_tr.wait(s, l, 8 * n + b + 1)
                        for k in (2 * b, 2 * b + 1):
                            src = ps[:, b, k % 2 * SEQ:(k % 2 + 1) * SEQ]
                            if b in H_BY_ACT:
                                s.activation(h_t[:, k, :], src, ACT.Identity, bias=mod[:, 1, k:k + 1],
                                             scale=modA[:, k:k + 1])
                            h_hi.by(s.activation(hT_hi[:, k, :], src, ACT.Identity, bias=mod[:, 1, k:k + 1],
                                                 scale=modA[:, k:k + 1]))

                def gt_evac(n):
                    gt_mm.wait(s, l, n + 1)
                    gt_ready.by(s.activation(gt_row[:, :], psf[:, 0:D], ACT.Copy))

                rms(0, lambda t: xs[:, t, :])
                for c in range(AHEAD):
                    w_head(c, used=False)
                h_evac(0)
                s.sem_inc(in_ev, FREE)
                def in_tile(i, k, dst, head=True):
                    s.wait_ge(w_used, l * CHUNKS + i * (2 * BODY) + (2 * k + 2))
                    s.activation(dst, ps[:, k % 5, 0:SEQ], ACT.Copy).then_inc(in_ev, 1)
                    if head:
                        for c in (2 * k + AHEAD, 2 * k + AHEAD + 1):
                            w_head(c, i * 2)
                def phases(u):
                    ph, sn, co = s5_phase(u), s5_S[u % 2], s5_C[u % 2]
                    for j in range(SQ):
                        m = s.activation(ph[:, j, :], K("steps"), ACT.Copy, scale=s5p[:, 10, SQ * u + j:SQ * u + j + 1])
                    s5_ai.by(m)
                    s5_ai.wait(s, l, 2 * u + 1)
                    s5_ph.by(s.activation(sn, ph, ACT.Identity, bias=K("magic")))
                    s5_ai.by(s.activation(co, ph, ACT.Identity, bias=K("quarter")))
                    s5_ai.wait(s, l, 2 * u + 2)
                    s5_ph.by(s.activation(co, co, ACT.Identity, bias=K("magic")))

                for k in range(BODY):
                    in_tile(0, k, mix[:, k + T_U, :])
                    if k == 2:
                        s5_pa.by(s.activation(SP5(0), A("log_dt"), ACT.Exp))
                    if k == 5:
                        s5_pd.wait(s, l, 1)
                        s5_pa.by(s.activation(SP5(2), SP5(1), ACT.Exp))
                        s5_pd.wait(s, l, 3)
                        s5_pa.by(s.activation(SP5(7), SP5(5), ACT.Sin))
                        s5_pa.by(s.activation(SP5(8), SP5(6), ACT.Sin))
                for k in range(BODY):
                    in_tile(1, k, mix[:, (BODY + k + T_U) % NPROJ, :], head=k < BODY - 1)
                    if k == 2:
                        s5_pd.wait(s, l, 5)
                        phases(0)
                s.wait_ge(w_used, l * CHUNKS + C_CMP)
                gate_ev.by(s.activation(rows[:, 0, :], ps[G_I:G_I + MH, 5, 0:SEQ], ACT.Identity, bias=A("i_bias", p=4)))
                gate_ev.by(s.activation(rows[:, 1, :], ps[G_F:G_F + MH, 5, 0:SEQ], ACT.Identity, bias=A("f_bias", p=4)))
                gate_ev.by(s.activation(sg24[:, :], ps[G_N:G_N + 3 * NH, 5, 0:SEQ], ACT.Sigmoid))
                gt_evac(0)

                def tables(u):
                    s5_nf.wait(s, l, u + 1)
                    s.activation(s5_S[u % 2], s5_S[u % 2], ACT.Sin, scale=-TWO_PI_IN)
                    s5_tab.by(s.activation(s5_C[u % 2], s5_C[u % 2], ACT.Sin, scale=-TWO_PI_IN, bias=K("half_pi")))

                def rotated(n):
                    rp_mm.wait(s, l, n + 1)
                    if n >= 2:
                        rp_d.wait(s, l, n - 1)
                    rp_ev.by(s.activation(rp_buf(n), ps[:, 4 + n % 2, :].rearrange("p (a b) -> p a b", a=2), ACT.Copy))

                tables(0)
                rotated(0)
                phases(1)
                rotated(1)
                act.chain(s, l, s.activation(rows[:, 2, :], rows[:, 1, :], ACT.Abs))
                act.chain(s, l, s.activation(rows[:, 2, :], rows[:, 2, :], ACT.Exp, scale=-1.0))
                mg_a.by(s.activation(rows[:, 2, :], rows[:, 2, :], ACT.Ln, bias=1.0))
                for u in range(UT):
                    if u + 1 < UT:
                        tables(u + 1)
                    if u + 2 < UT:
                        s5_h.wait(s, l, 2 * u + 2)
                        phases(u + 2)
                    for n in ((2,), (3, 4), (5, 6), ())[u]:
                        rotated(n)
                    if u:
                        s5_y.wait(s, l, u)
                        s5_g.by(s.activation(mix[:, T_U + u - 1, :], mix[:, T_U + u - 1, :], ACT.Gelu_apprx_tanh))
                s5_y.wait(s, l, UT)
                s5_g.by(s.activation(mix[:, T_U + UT - 1, :], mix[:, T_U + UT - 1, :], ACT.Gelu_apprx_tanh))
                s.wait_ge(w_used, l * CHUNKS + C_OUT)
                for v in range(2):
                    ch_g.by(s.activation(hid[:, v, :], ps[:, 7, 64 * v:64 * v + 30], ACT.Gelu_apprx_tanh))
                for a in range(2):
                    vt_mm.wait(s, l, a + 1)
                    vt_ev.by(s.activation(vtok[:, a, :, :, :].rearrange("p h s e -> p (h s e)"), ps[:, a, :], ACT.Copy))
                for ck in range(2):
                    vt_mm.wait(s, l, 3 + ck)
                    vt_ev.by(s.activation(vm[:, ck, :, :].rearrange("p h e -> p (h e)"), ps[:, 2 + ck, :], ACT.Copy))
                for n in range(4):
                    if n % 2 == 0:
                        glu_mm.wait(s, l, n // 2 + 1)
                    o = A_OFF["s_b_glu"][0]
                    glu_z.by(s.activation(S5T[:, 4 + n, :], ps[:, 4 + n // 2, (n % 2) * SEQ:(n % 2 + 1) * SEQ], ACT.Sigmoid,
                                          bias=aux[:, o + n:o + n + 1]))
                vt_mm.wait(s, l, 5)
                vt_ev.by(s.activation(gates_t[:, :, :], ps[:, 6, 0:64].rearrange("p (t n) -> p t n", t=2)[:, :, 0:24],
                                      ACT.Copy))
                mg_d.wait(s, l, 2)
                m_row.by(s.activation(rows[:, 0, :], rows[:, 5, :], ACT.Exp, scale=-1.0))
                m_row.by(s.activation(rows[:, 2, P:SEQ], rows[:, 4, P:SEQ], ACT.Exp, scale=-1.0, bias=rcol[:, 0:1]))
                mc_p.wait(s, l, 19)
                mc_a.by(s.activation(mix[:, T_QK + 4:T_QK + 8, :], S5T[:, 8:12, :], ACT.Silu))
                mc_d.wait(s, l, 4)
                mc_a.by(s.activation(mix[:, T_QK:T_QK + 4, :].rearrange("p a b -> p (a b)"), scratch[:, 0:4 * SEQ],
                                     ACT.Silu))
                m_sig.by(s.activation(mix[:, T_O:T_O + 4, :], mix[:, T_O:T_O + 4, :], ACT.Sigmoid))
                cc_mm.wait(s, l, 1)
                cc_ev.by(s.activation(kcT, ps[:, 7, 128:158], ACT.Copy))
                cc_ev.by(s.activation(vct[:, :, :].rearrange("p h e -> p (h e)"), ps[0:NC, 7, 256:512], ACT.Copy))
                mb_mm.wait(s, l, 1)
                mb_ev.by(s.activation(bcol[:, :, :].rearrange("p c h -> p (c h)"), ps[:, 7, 0:8], ACT.Copy))
                def exps(n):
                    g, qt, kind = ITEMS[n]
                    nk = NC if kind == 0 else (qt + 1) * P
                    ns_m.wait(s, l, n + 1)
                    for h in range(GQ):
                        e = s.activation(pr[:, n % 2, h, 0:nk], pr[:, n % 2, h, 0:nk], ACT.Exp,
                                         bias=att_s[:, n % 2, h:h + 1], accum_out=att_s[:, n % 2, 4 + h:5 + h])
                    ns_e.by(e)

                exps(0)
                for n, (g, qt, kind) in enumerate(ITEMS):
                    if n + 1 < NI:
                        exps(n + 1)
                    ns_t.wait(s, l, n + 1)
                    if n:
                        ns_o.wait(s, l, n)
                    if kind == 0:
                        ns_pt.by(s.activation(pt[0:NC, 0, :], ps[0:NC, 4, :], ACT.Copy))
                    else:
                        ns_pt.by(s.activation(pt[:, 0:qt + 1, :], ps[:, 4:4 + qt + 1, :], ACT.Copy))
                    if kind == 2:
                        ns_o.wait(s, l, n + 1)
                        ns_y.by(s.activation(mix[:, T_Q + GQ * g:T_Q + GQ * (g + 1), qt * P:(qt + 1) * P],
                                             ps[:, 6, :].rearrange("p (h t) -> p h t", h=GQ), ACT.Copy))

                for c in range(AHEAD):
                    w_head(C_OUT + c)

                for ck in range(2):
                    m_dlog.wait(s, l, ck + 1)
                    m_exp.by(s.activation(m_dt[ck], m_dt[ck], ACT.Exp))
                    m_num.wait(s, l, ck + 1)
                    m_abs.by(s.activation(m_e1, ps[:, 4, :], ACT.Abs))
                    if ck == 0:
                        m_c.wait(s, l, 1)
                        m_cev.by(s.activation(m_C, ps[:, 6, :], ACT.Copy))
                        m_cev.by(s.activation(m_n, ps[:, 7, :], ACT.Copy))
                    m_h.wait(s, l, ck + 1)
                    m_hsq.by(s.activation(m_tb, m_hb, ACT.Square))
                    m_ss.wait(s, l, ck + 1)
                    m_rs.by(s.activation(m_e2, ps[:, 2, :], ACT.Sqrt, bias=K("eps"), scale=1.0 / HD))

                m_out.wait(s, l, 2)
                glu_y.wait(s, l, 1)
                for k in range(2):
                    x_head(k, k)
                for k in range(KT):
                    c = C_OUT + 2 * k + AHEAD
                    w_head(c)
                    w_head(c + 1)
                    if k + 2 < KT:
                        x_head(k + 2, k + 2, l * CHUNKS + C_OUT + 2 * k + 2)

                s.wait_ge(w_used, l * CHUNKS + C_UP)
                rms(1, lambda t: psf[:, t * D:(t + 1) * D])
                rms(2, lambda t: xs[:, t, :])
                h_evac(1)

                wo, bo = A_OFF["f_conv_w"][0], A_OFF["f_conv_b"][0]

                def gelu(i, k):
                    t = mtile(i * 5 + k)
                    apart(ff_conv, (l * FT + i * 5 + k) * 2 + 2)
                    s.activation(t, t, ACT.Gelu_apprx_tanh).then_inc(ff_gelu, 1)

                def tap(i, k):
                    t = i * 5 + k
                    w = aux[:, bass.ds(t * 3 + (wo + 2), 1)]
                    b = aux[:, bass.ds(t + bo, 1)]
                    apart(w_used, l * CHUNKS + i * BODY + (C_UP + 4 * k + 4))
                    s.activation(mtile(t), ps[:, k, 0:SEQ], ACT.Identity, scale=w, bias=b).then_inc(ff_tap, 1)

                def up(i, k, first=False):
                    c = C_UP + 4 * k + AHEAD
                    w_head(c, i)
                    if not first:
                        gelu(i, k - 1)
                    for j in (1, 2, 3):
                        w_head(c + j, i)
                    tap(i, k)

                for k in range(5):
                    up(0, k, k == 0)
                with s.Fori(1, 8) as i:
                    for k in range(5):
                        up(i, k)
                for k in range(3):
                    up(8, k)
                gelu(8, 2)
                s.wait_ge(ff_mul, (l + 1) * (FREE + FT))
                for k in range(2):
                    x_head(k, k)
                gt_evac(1)

                def down(i, k, head=True):
                    c = C_DOWN + 2 * k + AHEAD
                    if head:
                        w_head(c, i)
                        w_head(c + 1, i)
                        x_head(k, i * 10 + (k + 2), l * CHUNKS + i * BODY + (C_DOWN + 2 * k + 2))
                with s.Fori(0, 4) as i:
                    for k in range(10):
                        down(i, k)
                down(4, 0)
                s.wait_ge(w_used, (l + 1) * CHUNKS)
                rms(3, lambda t: psf[:, t * D:(t + 1) * D])
                x_ready.wait(s, l, 4)

        @block.vector
        def _(v):
            def tt(o, a, b, op):
                return v.tensor_tensor(o, a, b, op)

            def ts(o, a, s1, s2, op0, op1):
                return v.tensor_scalar(o, a, s1, s2, op0, op1)

            def stt(o, a, s, b, op0, op1):
                return v.scalar_tensor_tensor(o, a, s, b, op0, op1)

            def reduced_angle(step, src, k, r, shifted, scratch):
                step(ts(k, src, TURN, MAGIC, ALU.mult, ALU.add))
                step(ts(k, k, -MAGIC, None, ALU.add, ALU.bypass))
                step(stt(r, k, -PI_1, src, ALU.mult, ALU.add))
                step(stt(r, k, -PI_2, r, ALU.mult, ALU.add))
                step(stt(r, k, -PI_3, r, ALU.mult, ALU.add))
                step(ts(r, r, PI_IN, -PI_IN, ALU.min, ALU.max))
                step(ts(shifted, r, TWO_PI / 4, None, ALU.add, ALU.bypass))
                step(ts(scratch, shifted, PI_IN, -TWO_PI, ALU.is_gt, ALU.mult))
                step(tt(shifted, shifted, scratch, ALU.add))
                step(ts(shifted, shifted, PI_IN, -PI_IN, ALU.min, ALU.max))

            done = [0]

            def pro(ins):
                done[0] += 1
                ins.then_inc(rope_dve, 1)
                v.wait_ge(rope_dve, done[0])

            v.wait_ge(cst_in, 16)
            v.wait_ge(pos_in, 16)
            pro(v.tensor_copy(mix[:, 0, :], posi[:, :]))
            pro(ts(mix[:, 0, :], mix[:, 0, :], K("inv_freq"), None, ALU.mult, ALU.bypass))
            reduced_angle(pro, mix[:, 0, :], mix[:, 1, :], mix[:, 2, :], mix[:, 3, :], mix[:, 4, :])
            assert done[0] == ROPE_STEPS[1]
            v.wait_ge(cs_ready, 1)

            def ada_chunk(u, j, a=0):
                if j == 0:
                    v.wait_ge(acc_bias, u * 16 + 16)
                v.wait_ge(ada_full[j % ASLOT], u * (UCH // ASLOT * 16) + (16 * (j // ASLOT) + 16))
                if j:
                    v.wait_ge(ada_step, u * UCH + j)
                stt(ada_acc[:, a, :], ada_w[:, j % ASLOT, :], cs[:, j:j + 1], ada_acc[:, a, :], ALU.mult,
                    ALU.add).then_inc(ada_step, 1)

            def ada_finish(u, col):
                v.wait_ge(ada_red, u + 1)
                v.tensor_copy(col, ps[:, 7, 0:UG]).then_inc(mod_ready, 1)

            modf = mod[:, :, :].rearrange("p a b -> p (a b)")
            with v.Fori(0, 2) as i:
                for a in range(2):
                    for j in range(UCH):
                        ada_chunk(i * 2 + a, j, a)
                for a in range(2):
                    ada_finish(i * 2 + a, modf[:, bass.ds(i * (2 * UG) + (2 + a) * UG, UG)])
            v.wait_ge(x_in, 16)
            v.wait_ge(rope_act, 2)

            with v.Fori(0, DEPTH) as l:
                step = lambda ins: dve.chain(v, l, ins)

                def norm_in(n, gain):
                    v.wait_ge(mod_ready, l * UNITS + (4 if n == 0 else 10))
                    modA_ready.by(stt(modA[:, :], mod[:, 2, :], 1.0, A(gain), ALU.add, ALU.mult))
                    for t in range(TT):
                        rstd.wait(v, l, 4 * n + t + 1)
                        step(v.reciprocal(stat[:, 4 + t:5 + t], stat[:, 2 + t:3 + t]))
                        xn_ready.by(ts(xn[:, t, :], xs[:, t, :], stat[:, 4 + t:5 + t], None, ALU.mult, ALU.bypass))
                    modA_ready.wait(v, l, n + 1)
                    for b in range(8):
                        h_hi.wait(v, l, KT * n + 2 * b + 2)
                        if b not in H_BY_ACT:
                            for k in (2 * b, 2 * b + 1):
                                w = ts(h_t[:, k, :], ps[:, b, k % 2 * SEQ:(k % 2 + 1) * SEQ], modA[:, k:k + 1],
                                       mod[:, 1, k:k + 1], ALU.mult, ALU.add)
                            h_tmp.by(w)
                            h_tmp.wait(v, l, h_tmp.given)
                        h_lo.by(tt(hT_lo[:, 2 * b:2 * b + 2, :], h_t[:, 2 * b:2 * b + 2, :],
                                   hT_hi[:, 2 * b:2 * b + 2, :].bitcast(F32), ALU.subtract))

                def w_rest(c, i=0):
                    v.wait_ge(hi_ready, l * NSPLIT + i * BODY + (c + 1 - (N_CMP if c >= C_OUT else 0)))
                    tt(w_lo[:, c % SPLIT, :], ring[:, c % RING, :], w_hi[:, c % SPLIT, :].bitcast(F32),
                       ALU.subtract).then_inc(raw_free, 1)

                def x_rest(k, t, n):
                    v.wait_ge(xhi_ready, n + 1)
                    tt(x_lo[:, k % 2, :], mtile(t), x_hi[:, k % 2, :].bitcast(F32), ALU.subtract).then_inc(xlo_ready, 1)

                def residual(n):
                    gt_ready.wait(v, l, n + 1)
                    for t in range(TT):
                        rstd.wait(v, l, 4 * n + 2 + t + 1)
                        step(v.reciprocal(stat[:, 6 + t:7 + t], stat[:, 2 + t:3 + t]))
                        tmp = mix[:, 0:8, :].rearrange("p a b -> p (a b)")
                        step(stt(tmp, psf[:, t * D:(t + 1) * D], stat[:, 6 + t:7 + t], gt_row[:, :], ALU.mult, ALU.mult))
                        x_ready.by(tt(xs[:, t, :], xs[:, t, :], tmp, ALU.add))
                        x_ready.wait(v, l, 2 * n + t + 1)

                def gate_gain(n, gain):
                    gg_ready.by(tt(gg[:, :], mod[:, 0, :], A(gain), ALU.mult))

                v.wait_ge(aux_in, l * 16 + 16)
                norm_in(0, "g_pre_mix")
                for c in range(AHEAD):
                    w_rest(c)
                def s5_first():
                    s5_pa.wait(v, l, 1)
                    s5_pd.by(tt(SP5(1), A("lam_re"), SP5(0), ALU.mult))
                    step(tt(SP5(3), A("lam_im"), SP5(0), ALU.mult))
                    reduced_angle(step, SP5(3), SP5(4), SP5(5), SP5(6), SP5(9))
                    s5_pd.by(ts(SP5(10), SP5(5), TURN, None, ALU.mult, ALU.bypass))
                    s5_pd.by(tt(SP5(11), A("lam_re"), A("lam_re"), ALU.mult))
                    step(tt(SP5(12), A("lam_im"), A("lam_im"), ALU.mult))
                    step(tt(SP5(11), SP5(11), SP5(12), ALU.add))
                    dve.by(v.reciprocal(SP5(11), SP5(11)))

                def s5_second():
                    dve.wait(v, l, dve.given)
                    s5_pa.wait(v, l, 4)
                    step(tt(SP5(12), SP5(2), SP5(8), ALU.mult))
                    step(tt(SP5(13), SP5(2), SP5(7), ALU.mult))
                    step(ts(SP5(12), SP5(12), -1.0, None, ALU.add, ALU.bypass))
                    step(tt(SP5(14), SP5(12), A("lam_re"), ALU.mult))
                    step(tt(SP5(15), SP5(13), A("lam_im"), ALU.mult))
                    step(tt(SP5(14), SP5(14), SP5(15), ALU.add))
                    step(tt(SP5(14), SP5(14), SP5(11), ALU.mult))
                    step(tt(SP5(15), SP5(13), A("lam_re"), ALU.mult))
                    step(tt(SP5(16), SP5(12), A("lam_im"), ALU.mult))
                    step(tt(SP5(15), SP5(15), SP5(16), ALU.subtract))
                    step(tt(SP5(15), SP5(15), SP5(11), ALU.mult))
                    cr = A("s_c_re").rearrange("p (j c) -> p j c", j=ST)
                    ci = A("s_c_im").rearrange("p (j c) -> p j c", j=ST)
                    zr = s5p[:, 14, :].unsqueeze(2).to_broadcast([P, ST, SC])
                    zi = s5p[:, 15, :].unsqueeze(2).to_broadcast([P, ST, SC])
                    b5 = [S5T[:, 2 * i:2 * i + 2, :].rearrange("p a b -> p (a b)").rearrange("p (j c) -> p j c", j=ST)
                          for i in range(4)]
                    step(tt(b5[0], cr, zr, ALU.mult))
                    step(tt(b5[1], ci, zi, ALU.mult))
                    step(tt(b5[2], cr, zi, ALU.mult))
                    step(tt(b5[3], ci, zr, ALU.mult))
                    s5_pd.by(tt(cr, b5[0], b5[1], ALU.subtract))
                    s5_pd.by(stt(ci, b5[2], -1.0, b5[3], ALU.mult, ALU.subtract))

                with v.Fori(0, 2) as i:
                    for k in range(BODY):
                        if k < BODY - 1:
                            for c in (2 * k + AHEAD, 2 * k + AHEAD + 1):
                                w_rest(c, i * 2)
                        else:
                            with v.If(i < 1):
                                for c in (2 * k + AHEAD, 2 * k + AHEAD + 1):
                                    w_rest(c, i * 2)
                        for j in range(2 * UCH * k // ADA_STEPS, 2 * UCH * (k + 1) // ADA_STEPS):
                            if j < 2 * UCH:
                                ada_chunk(l * UNITS + i * 2 + (4 + j // UCH), j % UCH, j // UCH)
                        if k in (3, 8):
                            with v.If(i < 1):
                                s5_first() if k == 3 else s5_second()
                        if k - 1 in ADA_IN_PE:
                            a = ADA_IN_PE.index(k - 1)
                            ada_finish(l * UNITS + i * 2 + (4 + a), modf[:, bass.ds((i * 2 + a) * UG, UG)])
                v.wait_ge(mod_ready, l * UNITS + 8)
                gate_gain(0, "g_post_mix")

                pv = S5T[:, 0:8, :].rearrange("p a b -> p (a b)").rearrange("p (i n) -> p i n", i=4)
                fl = lambda a: a.rearrange("p a b -> p (a b)")
                two = lambda a: a.rearrange("p (a b) -> p a b", a=2)

                def s5_out(u):
                    s5_c.wait(v, l, 2 * u + 2)
                    o = A_OFF["s_d"][0] + u
                    s5_y.by(stt(mix[:, T_U + u, :], mix[:, T_U + u, :], aux[:, o:o + 1], ps[:, 6, 0:SEQ],
                                ALU.mult, ALU.add))

                for q in range(ST // 2):
                    u, hq = q // 2, q % 2
                    C3, S3 = (b[u % 2][:, 2 * hq:2 * hq + 2, :] for b in (s5_C, s5_S))
                    Cq, Sq = fl(C3), fl(S3)
                    t0, t1, t2, t3 = (pv[:, i, :] for i in range(4))
                    h_r, h_i = s5_hb(q, 0), s5_hb(q, 1)
                    wr, wi = ps[:, 0:2, 0:SEQ], ps[:, 2:4, 0:SEQ]
                    if hq == 0:
                        s5_tab.wait(v, l, u + 1)
                    s5_b.wait(v, l, q + 1)
                    tt(two(t0), wr, C3, ALU.mult)
                    tt(two(t1), wi, S3, ALU.mult)
                    step(tt(two(t3), wi, C3, ALU.mult))
                    s5_bv.by(tt(two(t2), wr, S3, ALU.mult))
                    step(tt(t0, t0, t1, ALU.add))
                    s5_bv.wait(v, l, q + 1)
                    step(tt(t1, t3, t2, ALU.subtract))
                    if hq == 0 and u:
                        s5_out(u - 1)
                    for half in range(2):
                        j = 2 * q + half
                        part = slice(half * SEQ, (half + 1) * SEQ)
                        a = s5p[:, 2, j:j + 1].to_broadcast([P, SEQ])
                        v.tensor_tensor_scan(t2[:, part], a, t0[:, part], 0.0, ALU.mult, ALU.add)
                        g = v.tensor_tensor_scan(t3[:, part], a, t1[:, part], 0.0, ALU.mult, ALU.add)
                    step(g)
                    if q >= 2:
                        s5_c.wait(v, l, q - 1)
                    tt(t0, t2, Cq, ALU.mult)
                    tt(t1, t3, Sq, ALU.mult)
                    step(tt(h_i, t2, Sq, ALU.mult))
                    step(tt(h_r, t0, t1, ALU.subtract))
                    step(tt(t0, t3, Cq, ALU.mult))
                    s5_h.by(tt(h_i, h_i, t0, ALU.add))
                    s5_h.wait(v, l, q + 1)
                    if q:
                        v.wait_ge(w_used, l * CHUNKS + C_CMP + q)
                        v.sem_inc(raw_free, 1)
                s5_out(UT - 1)
                v.wait_ge(w_used, l * CHUNKS + C_OUT)
                v.sem_inc(raw_free, 1)
                mg_a.wait(v, l, 1)
                step(ts(rows[:, 7, :], rows[:, 1, :], 0.0, None, ALU.min, ALU.bypass))
                step(tt(rows[:, 1, :], rows[:, 7, :], rows[:, 2, :], ALU.subtract))
                for ck in range(2):
                    cs_ = slice(ck * P, (ck + 1) * P)
                    g = v.tensor_tensor_scan(rows[:, 7, cs_], K("ones", p=4), rows[:, 1, cs_], 0.0, ALU.mult, ALU.add)
                step(g)
                mg_d.by(tt(rows[:, 3, :], rows[:, 0, :], rows[:, 7, :], ALU.subtract))
                mg_d.wait(v, l, 1)
                for ck in range(2):
                    cs_ = slice(ck * P, (ck + 1) * P)
                    step(v.tensor_tensor_scan(rows[:, 4, cs_], rows[:, 3, cs_], rows[:, 3, cs_],
                                              rcol[:, 0:1] if ck else 0.0, ALU.max, ALU.max))
                    step(tt(rows[:, 5, cs_], rows[:, 7, cs_], rows[:, 4, cs_], ALU.add))
                    if ck == 0:
                        step(v.tensor_copy(rcol[:, 0:1], rows[:, 5, P - 1:P]))
                mg_d.by(ts(rows[:, 6, :], rows[:, 4, :], -1.0, None, ALU.mult, ALU.bypass))
                cw, cb = A_OFF["m_conv_w"][0], A_OFF["m_conv_b"][0]
                for i in range(4):
                    src = mix[:, T_QK + i, :]
                    dst = m_cv(i)
                    wj = lambda j: aux[:, cw + 4 * i + j:cw + 4 * i + j + 1]
                    step(ts(dst, src, wj(3), aux[:, cb + i:cb + i + 1], ALU.mult, ALU.add))
                    for j in (1, 2, 3):
                        (step if j < 3 else mc_d.by)(
                            stt(dst[:, j:SEQ], src[:, 0:SEQ - j], wj(3 - j), dst[:, j:SEQ], ALU.mult, ALU.add))
                glu_z.wait(v, l, 4)
                glu_y.by(tt(mix[:, T_U:T_U + 4, :], mix[:, T_U:T_U + 4, :], S5T[:, 4:8, :], ALU.mult))

                mc_a.wait(v, l, 2)
                def masked(n):
                    g, qt, kind = ITEMS[n]
                    b = 2 * (n % 2)
                    nk = NC if kind == 0 else (qt + 1) * P
                    p3 = pr[:, n % 2, :, 0:nk]
                    ns_s.wait(v, l, n + 1)
                    if n >= 2:
                        ns_t.wait(v, l, n - 1)
                    if kind == 0:
                        s3 = ps[:, b, 0:64].rearrange("p (h s) -> p h s", h=GQ)[:, :, 0:NC]
                        m3 = K("cmp_mask", qt * NC, (qt + 1) * NC)
                    else:
                        s3 = ps[:, b:b + 2, :].rearrange("p a (c s) -> p (a c) s", c=2)[:, :, 0:nk]
                        m3 = K("mask", (1 - qt) * P, 2 * P)
                    step(stt(p3, s3, SCALE, m3.unsqueeze(1).to_broadcast([P, GQ, nk]), ALU.mult, ALU.add))
                    ns_m.by(v.tensor_reduce(att_s[:, n % 2, 0:4], p3, AX.X, ALU.max, negate=True))

                def weighted(n):
                    g, qt, kind = ITEMS[n]
                    nk = NC if kind == 0 else (qt + 1) * P
                    p3 = pr[:, n % 2, :, 0:nk]
                    st3 = att_s[:, n % 2, :]
                    ns_e.wait(v, l, n + 1)
                    step(v.reciprocal(st3[:, 8:12], st3[:, 4:8]))
                    step(tt(st3[:, 8:12], st3[:, 8:12],
                            gates_t[:, qt, :].rearrange("p (h c) -> p h c", c=3)[:, GQ * g:GQ * (g + 1), kind], ALU.mult))
                    w3 = st3[:, 8:12].unsqueeze(2).to_broadcast([P, GQ, nk])
                    if kind == 0:
                        step(tt(p3, p3, w3, ALU.mult))
                        ok = K("cmp_valid", qt * NC, (qt + 1) * NC).unsqueeze(1).to_broadcast([P, GQ, nk])
                        ns_p.by(tt(p3, p3, ok, ALU.mult))
                    else:
                        ns_p.by(tt(p3, p3, w3, ALU.mult))

                masked(0)
                for n in range(NI):
                    if n + 1 < NI:
                        masked(n + 1)
                    weighted(n)

                for c in range(AHEAD):
                    w_rest(C_OUT + c)

                for ck in range(2):
                    h4 = range(MH)
                    mb_ev.wait(v, l, 1)
                    (m_kt if ck == 0 else m_qi).wait(v, l, 1)
                    for h in h4:
                        hs = slice(h * P, (h + 1) * P)
                        d = stt(m_dt[ck][:, hs], ps[:, 0, hs], bcol[:, ck, h:h + 1], K("mask_t"), ALU.add, ALU.add)
                    m_dlog.by(d)
                    if ck == 1:
                        m_qib_ready.by(tt(m_qib.rearrange("p (h t) -> p h t", h=MH), mix[:, T_QK:T_QK + 4, P:SEQ],
                                          ps[:, 5, :].rearrange("p (h t) -> p h t", h=MH), ALU.mult))
                    m_exp.wait(v, l, ck + 1)
                    m_sw.by(stt(m_swb[ck], ps[:, 2, :], SCALE, m_dt[ck], ALU.mult, ALU.mult))
                    if ck == 0:
                        for h in h4:
                            hs = slice(h * P, (h + 1) * P)
                            d = ts(m_kwb[:, hs], ps[:, 5, hs], m_dt[0][:, h * P + P - 1:h * P + P], SCALE, ALU.mult, ALU.mult)
                        m_kw.by(d)
                    m_abs.wait(v, l, ck + 1)
                    step(tt(m_e1, m_e1, ps[:, 1, :], ALU.max))
                    step(v.reciprocal(m_e1, m_e1))
                    m_h.by(tt(m_hb, ps[:, 3, :], m_e1, ALU.mult))
                    m_rs.wait(v, l, ck + 1)
                    step(v.reciprocal(m_e2, m_e2))
                    step(tt(m_hb, m_hb, m_e2, ALU.mult))
                    m_sig.wait(v, l, 1)
                    for h in h4:
                        o = A_OFF["m_norm_g"][0] + h
                        yt = mix[:, T_O + h, ck * P:(ck + 1) * P]
                        d = stt(yt, m_hb[:, h * P:(h + 1) * P], aux[:, o:o + 1], yt, ALU.mult, ALU.mult)
                    m_out.by(d)

                ns_y.wait(v, l, 4)
                m_out.wait(v, l, 2)
                glu_y.wait(v, l, 1)
                for k in range(2):
                    x_rest(k, k, l * NXS + k)
                for k in range(KT):
                    c = C_OUT + 2 * k + AHEAD
                    w_rest(c)
                    w_rest(c + 1)
                    if k + 2 < KT:
                        x_rest(k + 2, k + 2, l * NXS + k + 2)
                    for j in (2 * k, 2 * k + 1):
                        ada_chunk(l * UNITS + (8 + j // UCH), j % UCH, j // UCH)
                residual(0)
                v.wait_ge(ada_red, l * UNITS + 10)
                v.tensor_copy(modf[:, 4 * UG:6 * UG], ps[:, 0, 0:2 * UG]).then_inc(mod_ready, 2)
                norm_in(1, "g_pre_ffn")

                v.sem_inc(ff_mul, FREE)
                wo = A_OFF["f_conv_w"][0]

                def conv(i, k):
                    t = i * 5 + k
                    g = mtile(t)
                    w = aux[:, wo + 3 * t:wo + 3 * t + 3] if isinstance(t, int) else aux[:, bass.ds(t * 3 + wo, 3)]
                    a = ps[:, k, 0:SEQ]
                    v.wait_ge(ff_tap, l * FT + i * 5 + (k + 1))
                    for j in (1, 2):
                        if j == 2:
                            v.wait_ge(ff_conv, (l * FT + i * 5 + k) * 2 + 1)
                        stt(g[:, j:SEQ], a[:, 0:SEQ - j], w[:, 2 - j:3 - j], g[:, j:SEQ], ALU.mult,
                            ALU.add).then_inc(ff_conv, 1)

                def gated(i, k):
                    g = mtile(i * 5 + k)
                    v.wait_ge(ff_gelu, l * FT + i * 5 + (k + 1))
                    tt(g, g, ps[:, k % 5, SEQ:2 * SEQ], ALU.mult).then_inc(ff_mul, 1)

                def up(i, k, first=False, ada=None):
                    c = C_UP + 4 * k + AHEAD
                    w_rest(c, i)
                    if not first:
                        gated(i, k - 1)
                    for j in (1, 2, 3):
                        w_rest(c + j, i)
                    conv(i, k)
                    if ada is not None:
                        u = l * UNITS + 10 + ada
                        with v.If(ada + l * 4 < 4 * DEPTH - 2):
                            if k < 4:
                                for j in range(4 * k, 4 * k + 4):
                                    ada_chunk(u, j)
                            else:
                                ada_finish(u, modf[:, bass.ds(ada * UG, UG)])

                for k in range(5):
                    up(0, k, k == 0, 0)
                with v.Fori(1, 6) as i:
                    for k in range(5):
                        up(i, k, False, i)
                with v.Fori(6, 8) as i:
                    for k in range(5):
                        up(i, k)
                for k in range(3):
                    up(8, k)
                gated(8, 2)
                gate_gain(1, "g_post_ffn")
                v.wait_ge(ff_mul, (l + 1) * (FREE + FT))
                for k in range(2):
                    x_rest(k, k, l * NXS + KT + k)

                def down(i, k):
                    c = C_DOWN + 2 * k + AHEAD
                    w_rest(c, i)
                    w_rest(c + 1, i)
                    x_rest(k, i * 10 + (k + 2), l * NXS + i * 10 + (KT + k + 2))
                with v.Fori(0, 4) as i:
                    for k in range(10):
                        down(i, k)
                down(4, 0)
                residual(1)

        wrong = [(str(sg.sem), sg.given, sg.per_layer) for sg in every if sg.given != sg.per_layer]
        assert not wrong, wrong


ROPE_TILES = [T_KC, T_KS, T_KW, T_Q, T_Q + 2, T_Q + 4, T_Q + 6]
ROPE_STEPS = (8, 12)
DVE_STEPS, ACT_STEPS = 165, 2
H_BY_ACT = (2, 5, 7)
ADA_STEPS, ADA_IN_PE = 18, (10, 18)



def _columns(a, n):
    return a.reshape(a.shape[0], n, P).transpose(0, 2, 1)


def _weights(i):
    out = np.empty((DEPTH, CHUNKS, P, CH), np.float32)

    def columns(w, c0, n):
        w = w[:, :, c0:c0 + n * P].reshape(DEPTH, 2, KH, P, n, P)
        return w.transpose(0, 4, 1, 3, 2, 5).reshape(DEPTH, 2 * n, P, CH)

    def rows(w, n):
        return w.reshape(DEPTH, n, P, 2, CH).transpose(0, 1, 3, 2, 4).reshape(DEPTH, 2 * n, P, CH)

    w_in = i["w_in"]
    at = 0
    for c0, n in ((2056, 4), (2568, 8), (3592, 12), (0, 8), (1024, 4), (1536, 4)):
        out[:, at:at + 2 * n] = columns(w_in, c0, n)
        at += 2 * n
    gates = np.zeros((DEPTH, D, P), np.float32)
    for row, c0, n in ((G_I, 2048, MH), (G_F, 2052, MH), (G_N, 5128, 3 * NH)):
        gates[:, :, row:row + n] = w_in[:, :, c0:c0 + n]
    out[:, C_GATES:C_CMP] = columns(gates, 0, 1)
    out[:, C_CMP:C_OUT] = i["n_cmp_w1"].reshape(DEPTH, 8, 8, P, P).transpose(0, 1, 3, 2, 4).reshape(DEPTH, 8, P, CH)
    out[:, C_OUT:C_UP] = rows(i["w_out"], KT)
    up = out[:, C_UP:C_DOWN].reshape(DEPTH, FT, 2, 2, P, CH)
    for branch in range(2):
        up[:, :, branch] = columns(i["f_w_up"], branch * DFF, FT).reshape(DEPTH, FT, 2, P, CH)
    out[:, C_DOWN:] = rows(i["f_w_down"], FT)
    return out.reshape(DEPTH * CHUNKS, P, CH)


def _params(i):
    out = np.zeros((DEPTH, P, A_W), np.float32)

    def put(name, a):
        o, w = A_OFF[name]
        out[:, :a.shape[1], o:o + w] = a.reshape(DEPTH, a.shape[1], w)

    for n in ("g_pre_mix", "g_post_mix", "g_pre_ffn", "g_post_ffn"):
        put(n, _columns(i[n], KT))
    put("m_conv_w", i["m_conv_w"].reshape(DEPTH, 4, 8, P).transpose(0, 3, 2, 1))
    put("m_conv_b", _columns(i["m_conv_b"], 8))
    put("m_norm_g", i["m_norm_g"].transpose(0, 2, 1))
    put("s_d", _columns(i["s_d"], 4))
    put("s_b_glu", _columns(i["s_b_glu"], 4))
    for n in ("lam_re", "lam_im"):
        put(n, i["s_" + n].reshape(DEPTH, ST, P).transpose(0, 2, 1))
    put("log_dt", np.repeat(i["s_log_dt"].reshape(DEPTH, ST, 2).transpose(0, 2, 1), S_STATE, axis=1))
    put("f_conv_w", i["f_conv_w"].reshape(DEPTH, 3, FT, P).transpose(0, 3, 2, 1))
    put("f_conv_b", _columns(i["f_conv_b"], FT))
    put("i_bias", i["m_i_bias"].reshape(DEPTH, 4, 1))
    put("f_bias", i["m_f_bias"].reshape(DEPTH, 4, 1))
    put("cmp_pos", i["n_cmp_pos"].transpose(0, 3, 1, 2))
    put("cmp_w2", i["n_cmp_w2"].transpose(0, 2, 1, 3))
    for part in ("re", "im"):
        ob, oc = A_OFF["s_b_" + part][0], A_OFF["s_c_" + part][0]
        for g in range(S_GROUPS):
            j, hb = g // 2, g % 2
            r, c = SC * (j % SQ) + S_GROUP * hb, ob + P * (j // SQ) + S_STATE * hb
            out[:, r:r + S_GROUP, c:c + S_STATE] = i["s_b_" + part][:, g].transpose(0, 2, 1)
            c = oc + SC * j + S_GROUP * hb
            out[:, S_STATE * hb:S_STATE * (hb + 1), c:c + S_GROUP] = i["s_c_" + part][:, g].transpose(0, 2, 1)
    return out


def _constants():
    out = np.zeros((P, K_W), np.float32)

    def put(name, a, rows=P):
        o, w = K_OFF[name]
        out[:rows, o:o + w] = np.asarray(a).reshape(rows, w)

    r = np.arange(P)
    put("ident", np.eye(P))
    put("ones", np.ones((P, P)))
    rot = np.zeros((P, P))
    rot[r[64:], r[:64]] = -1.0
    rot[r[:64], r[64:]] = 1.0
    put("rot", rot)
    put("mask", np.concatenate([np.zeros((P, P)), np.where(r[None] <= r[:, None], 0.0, NEG)], 1))
    put("mask_t", np.where(r[:, None] <= r[None], 0.0, NEG))
    t = r[:, None, None] + P * np.arange(TT)[None, :, None]
    ok = CS * np.arange(NC)[None, None] + CB - 1 <= t
    put("cmp_mask", np.where(ok, 0.0, NEG))
    put("cmp_valid", ok * 1.0)
    put("sel", (np.arange(MH)[:, None, None] == np.arange(MH)[None, :, None]) * np.ones((1, 1, P)), MH)
    put("steps", np.broadcast_to(np.arange(SEQ), (P, SEQ)))
    put("inv_freq", np.float32(10000.0) ** (-(r % 64).astype(np.float32) / np.float32(64)))
    put("half_pi", np.full(P, TWO_PI / 4))
    put("eps", np.full(P, EPS))
    put("magic", np.full(P, MAGIC))
    put("quarter", np.full(P, 0.25))
    return out


def kernel(**inputs):
    import concourse.bacc as bacc
    from concourse.bass_utils import run_bass_kernel_spmd

    i = {k: np.asarray(v) for k, v in inputs.items()}
    ada = i["w_ada"].reshape(DEPTH, UCH, P, UNITS, UC).transpose(0, 3, 1, 2, 4)
    arrays = {
        "x": i["x"],
        "c_cols": i["c"].reshape(KT, P).T,
        "pos": np.broadcast_to(i["positions"], (P, SEQ)),
        "consts": _constants(),
        "aux_d": _params(i),
        "ada_d": ada.reshape(DEPTH * UNITS * UCH, P, UC),
        "ada_b": i["b_ada"].reshape(DEPTH * UNITS, UC),
        "glu_d": i["s_w_glu"].reshape(DEPTH, 4, P, 512).transpose(0, 2, 1, 3).reshape(DEPTH, P, D),
        "stream": _weights(i),
    }
    arrays = {k: np.ascontiguousarray(a) for k, a in arrays.items()}
    nc = bacc.Bacc("TRN2", target_bir_lowering=False, num_devices=1)
    args = [nc.dram_tensor(k, a.shape, mybir.dt.from_np(a.dtype), kind="ExternalInput").ap() for k, a in arrays.items()]
    args.append(nc.dram_tensor("out", (1, SEQ, D), F32, kind="ExternalOutput").ap())
    trunk(nc, *args)
    r = run_bass_kernel_spmd(nc, [arrays], core_ids=[0])
    return r.results[0]["out"]
```
